# Optimizing a Trainium2 kernel written in Bass

```python
import jax, jax.numpy as jnp
from jax import lax
import numpy as np

D_MODEL = 2048
BATCH = 1
SEQ = 512
DEPTH = 1

GRID_W = 64
CTX_LEN = 256
EPS = 1e-6
N_MOD = 6

M_HEADS = 4
M_HEAD_DIM = 256
M_WIDTH = M_HEADS * M_HEAD_DIM
M_CHUNK = 64
M_GATES = 4 * M_HEADS
M_COLS = 4 * M_WIDTH + M_GATES

CV_WIDTH = D_MODEL - M_WIDTH
CV_KSIZE = 31
CV_COLS = 2 * CV_WIDTH

D_MIX = M_WIDTH + CV_WIDTH
N_COLS = M_COLS + CV_COLS

PEER_HEADS = 8
PEER_NKEYS = 128
PEER_EXPERTS = PEER_NKEYS * PEER_NKEYS
PEER_QDIM = 256
PEER_HALF = PEER_QDIM // 2
PEER_TOPK = 16
PEER_BLOCK = 128

kernel_name = 'hybrid_mlstm_conformer_peer_dit'

def rmsnorm(x, g):
    xf = x.astype(jnp.float32)
    y = xf * lax.rsqrt(jnp.mean(xf * xf, -1, keepdims=True) + EPS)
    return (y * g.astype(jnp.float32)).astype(x.dtype)

def layernorm(x, g, b):
    xf = x.astype(jnp.float32)
    mu = jnp.mean(xf, -1, keepdims=True)
    d = xf - mu
    y = d * lax.rsqrt(jnp.mean(d * d, -1, keepdims=True) + EPS)
    return (y * g.astype(jnp.float32) + b.astype(jnp.float32)).astype(x.dtype)

def modulate(h, shift, scale):
    return h * (1 + scale) + shift

def mlstm_scan(q, k, v, i_pre, f_pre):
    B, H, L, d = q.shape
    nc = L // M_CHUNK
    log_f = jax.nn.log_sigmoid(f_pre)

    def chunks(t):
        t = t.reshape(B, H, nc, M_CHUNK, *t.shape[3:])
        return jnp.moveaxis(t, 2, 0)

    xs = tuple(chunks(t) for t in (q, k, v, i_pre, log_f))
    causal = jnp.tril(jnp.ones((M_CHUNK, M_CHUNK), dtype=bool))

    def step(carry, inp):
        C, n, m = carry
        qb, kb, vb, ib, fb = inp
        b = jnp.cumsum(fb, -1)
        log_d = jnp.where(causal, b[..., :, None] - b[..., None, :] + ib[..., None, :], -jnp.inf)
        inter = b + m[..., None]
        m_row = jnp.maximum(inter, jnp.max(log_d, -1))
        w = jnp.exp(log_d - m_row[..., None])
        s_inter = jnp.exp(inter - m_row)
        qk = jnp.einsum('bhtd,bhsd->bhts', qb, kb) * w
        num = jnp.einsum('bhts,bhse->bhte', qk, vb) + s_inter[..., None] * jnp.einsum('bhtd,bhde->bhte', qb, C)
        den = jnp.sum(qk, -1) + s_inter * jnp.einsum('bhtd,bhd->bht', qb, n)
        h = num / jnp.maximum(jnp.abs(den), jnp.exp(-m_row))[..., None]
        b_last = b[..., -1]
        log_u = b_last[..., None] - b + ib
        m_new = jnp.maximum(b_last + m, jnp.max(log_u, -1))
        a = jnp.exp(b_last + m - m_new)
        u = jnp.exp(log_u - m_new[..., None])
        C_new = a[..., None, None] * C + jnp.einsum('bhs,bhsd,bhse->bhde', u, kb, vb)
        n_new = a[..., None] * n + jnp.einsum('bhs,bhsd->bhd', u, kb)
        return (C_new, n_new, m_new), h

    init = (jnp.zeros((B, H, d, d), jnp.float32), jnp.zeros((B, H, d), jnp.float32), jnp.zeros((B, H), jnp.float32))
    _, h = lax.scan(step, init, xs)
    return jnp.moveaxis(h, 0, 2).reshape(B, H, L, d)

def mlstm_bidir(pc, px, gate_bias, norm_w):
    p = jnp.concatenate([pc, px], 1).astype(jnp.float32)
    B, L, _ = p.shape
    q, k, v, o = [p[..., j * M_WIDTH:(j + 1) * M_WIDTH] for j in range(4)]
    gates = p[..., 4 * M_WIDTH:] + gate_bias.astype(jnp.float32)

    def heads(t):
        return t.reshape(B, L, M_HEADS, M_HEAD_DIM).transpose(0, 2, 1, 3)

    q = heads(q) * (M_HEAD_DIM ** -0.5)
    k = heads(k)
    v = heads(v)
    g = gates.reshape(B, L, 4, M_HEADS).transpose(2, 0, 3, 1)

    def rev(t):
        return jnp.concatenate([jnp.flip(t[:, :, :CTX_LEN], 2), jnp.flip(t[:, :, CTX_LEN:], 2)], 2)

    h_fwd = mlstm_scan(q, k, v, g[0], g[1])
    h_bwd = rev(mlstm_scan(rev(q), rev(k), rev(v), rev(g[2]), rev(g[3])))
    h = h_fwd + h_bwd
    h = h * lax.rsqrt(jnp.mean(h * h, -1, keepdims=True) + EPS)
    h = h.transpose(0, 2, 1, 3).reshape(B, L, M_WIDTH) * norm_w.astype(jnp.float32) * jax.nn.sigmoid(o)
    h = h.astype(pc.dtype)
    return h[:, :CTX_LEN], h[:, CTX_LEN:]

def conformer_conv(p, n_seq, seq_len, conv_w, conv_b, ln_g, ln_b):
    B, N, _ = p.shape
    u = p[..., :CV_WIDTH] * jax.nn.sigmoid(p[..., CV_WIDTH:])
    u = u.reshape(n_seq, seq_len, CV_WIDTH)
    y = lax.conv_general_dilated(u, conv_w[:, None, :], window_strides=(1,),
                                 padding=[(CV_KSIZE // 2, CV_KSIZE // 2)],
                                 dimension_numbers=('NWC', 'WIO', 'NWC'),
                                 feature_group_count=CV_WIDTH) + conv_b
    y = jax.nn.silu(layernorm(y, ln_g, ln_b))
    return y.reshape(B, N, CV_WIDTH)

def peer(h, w_query, sub_keys, u_emb, v_emb):
    B, N, D = h.shape
    t = h.reshape(B * N, D)
    T = t.shape[0]
    q = (t @ w_query).reshape(T, PEER_HEADS, 2, PEER_HALF)
    s = jnp.einsum('thpk,pnk->thpn', q, sub_keys).astype(jnp.float32)
    s_val, s_idx = lax.top_k(s, PEER_TOPK)
    cand = s_val[..., 0, :, None] + s_val[..., 1, None, :]
    cand_idx = s_idx[..., 0, :, None] * PEER_NKEYS + s_idx[..., 1, None, :]
    best, pos = lax.top_k(cand.reshape(T, PEER_HEADS, PEER_TOPK * PEER_TOPK), PEER_TOPK)
    expert = jnp.take_along_axis(cand_idx.reshape(T, PEER_HEADS, PEER_TOPK * PEER_TOPK), pos, -1)
    gate = jax.nn.softmax(best, -1).astype(t.dtype)
    nb = T // PEER_BLOCK

    def block(args):
        tb, eb, gb = args
        ub = jnp.take(u_emb, eb, axis=0)
        vb = jnp.take(v_emb, eb, axis=0)
        act = jax.nn.gelu(jnp.einsum('td,ted->te', tb, ub), approximate=False) * gb
        return jnp.einsum('te,ted->td', act, vb)

    out = lax.map(block, (t.reshape(nb, PEER_BLOCK, D),
                          expert.reshape(nb, PEER_BLOCK, PEER_HEADS * PEER_TOPK),
                          gate.reshape(nb, PEER_BLOCK, PEER_HEADS * PEER_TOPK)))
    return out.reshape(B, N, D)

def setup_inputs(seed: int = 0) -> dict:
    key = jax.random.key(seed)
    ks = jax.random.split(key, 24)
    D = D_MODEL

    def nrm(k, shape, s):
        return jax.random.normal(k, shape, jnp.float32) * s

    gate_base = jnp.concatenate([jnp.zeros((M_HEADS,), jnp.float32), jnp.linspace(3.0, 6.0, M_HEADS, dtype=jnp.float32),
                                 jnp.zeros((M_HEADS,), jnp.float32), jnp.linspace(3.0, 6.0, M_HEADS, dtype=jnp.float32)])
    return {
        'x': nrm(ks[0], (BATCH, SEQ, D), 1.0),
        'c': nrm(ks[1], (BATCH, D), 1.0),
        'ctx': nrm(ks[2], (BATCH, CTX_LEN, D), 1.0),
        'c_ctx': nrm(ks[3], (D,), 1.0),
        'w_mod': nrm(ks[4], (DEPTH, D, N_MOD * D), 0.5 * D ** -0.5),
        'b_mod': nrm(ks[5], (DEPTH, N_MOD * D), 0.02),
        'g_mix': 1.0 + nrm(ks[6], (DEPTH, D), 0.02),
        'g_ffn': 1.0 + nrm(ks[7], (DEPTH, D), 0.02),
        'w_in': nrm(ks[8], (DEPTH, D, N_COLS), D ** -0.5),
        'b_gate': gate_base + nrm(ks[9], (DEPTH, M_GATES), 0.1),
        'g_mhn': 1.0 + nrm(ks[10], (DEPTH, M_WIDTH), 0.02),
        'conv_w': nrm(ks[11], (DEPTH, CV_KSIZE, CV_WIDTH), CV_KSIZE ** -0.5),
        'conv_b': nrm(ks[12], (DEPTH, CV_WIDTH), 0.02),
        'cn_g': 1.0 + nrm(ks[13], (DEPTH, CV_WIDTH), 0.02),
        'cn_b': nrm(ks[14], (DEPTH, CV_WIDTH), 0.02),
        'w_out': nrm(ks[15], (DEPTH, D_MIX, D), D_MIX ** -0.5),
        'w_query': nrm(ks[16], (DEPTH, D, PEER_HEADS * PEER_QDIM), D ** -0.5),
        'sub_keys': nrm(ks[17], (DEPTH, 2, PEER_NKEYS, PEER_HALF), PEER_HALF ** -0.5),
        'u_emb': nrm(ks[18], (DEPTH, PEER_EXPERTS, D), D ** -0.5),
        'v_emb': nrm(ks[19], (DEPTH, PEER_EXPERTS, D), 1.0),
        'g_final': 1.0 + nrm(ks[20], (D,), 0.02),
    }

def reference(x, c, ctx, c_ctx, w_mod, b_mod, g_mix, g_ffn, w_in, b_gate, g_mhn, conv_w, conv_b,
              cn_g, cn_b, w_out, w_query, sub_keys, u_emb, v_emb, g_final):
    B, N, D = x.shape
    rows = N // GRID_W
    for l in range(DEPTH):
        need_ctx = l < DEPTH - 1
        mod_x = (jax.nn.silu(c) @ w_mod[l] + b_mod[l]).reshape(B, N_MOD, 1, D)
        mod_c = (jax.nn.silu(c_ctx)[None] @ w_mod[l] + b_mod[l]).reshape(1, N_MOD, 1, D)
        sh1, sc1, ga1, sh2, sc2, ga2 = [mod_x[:, j] for j in range(N_MOD)]
        csh1, csc1, cga1, csh2, csc2, cga2 = [mod_c[:, j] for j in range(N_MOD)]

        hx = modulate(rmsnorm(x, g_mix[l]), sh1, sc1)
        hc = modulate(rmsnorm(ctx, g_mix[l]), csh1, csc1)
        px = hx @ w_in[l]
        pc_m = hc @ w_in[l, :, :M_COLS]
        m_ctx, m_lat = mlstm_bidir(pc_m, px[..., :M_COLS], b_gate[l], g_mhn[l])
        cv_lat = conformer_conv(px[..., M_COLS:], B * rows, GRID_W, conv_w[l], conv_b[l], cn_g[l], cn_b[l])
        x = x + ga1 * (jnp.concatenate([m_lat, cv_lat], -1) @ w_out[l])

        x = x + ga2 * peer(modulate(rmsnorm(x, g_ffn[l]), sh2, sc2), w_query[l], sub_keys[l], u_emb[l], v_emb[l])

        if need_ctx:
            cv_ctx = conformer_conv(hc @ w_in[l, :, M_COLS:], B, CTX_LEN, conv_w[l], conv_b[l], cn_g[l], cn_b[l])
            ctx = ctx + cga1 * (jnp.concatenate([m_ctx, cv_ctx], -1) @ w_out[l])
            ctx = ctx + cga2 * peer(modulate(rmsnorm(ctx, g_ffn[l]), csh2, csc2), w_query[l], sub_keys[l], u_emb[l], v_emb[l])
    return rmsnorm(x, g_final)


_drawn_inputs = setup_inputs


def setup_inputs(seed=0):
    import zlib

    import numpy as np

    out = dict(_drawn_inputs(seed))
    spreads = {}
    factors = {'g_mix': 3.34,
     'g_mhn': 67.899,
     'conv_b': 4.159,
     'cn_g': 56.284,
     'cn_b': 60.404,
     'g_final': 23.435,
     'g_ffn': 11.752}
    for name, (base, spread) in spreads.items():
        noise = np.random.default_rng([zlib.crc32(name.encode()), seed]).standard_normal(out[name].shape)
        drawn = base * np.exp(spread * noise) if base else spread * noise
        out[name] = __import__('jax').numpy.asarray(drawn.astype(out[name].dtype))
    for name, factor in factors.items():
        out[name] = (out[name] * factor).astype(out[name].dtype)
    return out
```

```python
import concourse.bass as bass
from concourse import mybir
from contextlib import ExitStack

F32 = mybir.dt.float32
U32 = mybir.dt.uint32
ALU = mybir.AluOpType
ACT = mybir.ActivationFunctionType
AX = mybir.AxisListType

P = 128
D = 2048
KT = D // P
T = 512
C = 256
L = T + C
LT, CT = T // P, C // P
NB = 512
QT = KT // 4
GRID_W, ROWS = 64, T // 64
EPS = 1e-6
HEADS, HD = 4, 256
MW = HEADS * HD
GATES = 4 * HEADS
GATE0 = 4 * MW
CONV0 = GATE0 + GATES
CW = D - MW
CTILES = CW // P
TAPS = 31
PADW = GRID_W + TAPS - 1
PH, NK, TOPK = 8, 128, 16
SLOTS = PH * TOPK
BIG = 1e30
NEG = -3.0e38

MOD1, CONV, QO, KV, MOD2, WO, WQ = 0, 8, 12, 16, 20, 36, 40


def hybrid_layer(nc, x, c, ctx_in, c_ctx, w_mod, b_mod, g_mix, g_ffn, w_in, b_gate, g_mhn, conv_w, conv_b,
                 cn_g, cn_b, w_out, w_query, keys_t, u_t, v_emb, g_final, out):
    mod_dram = nc.dram_tensor("mod_rows", [1, 4 * D], F32)
    gate_dram = nc.dram_tensor("gate_table", [NK, NK, T], F32)

    with ExitStack() as ctx:
        def sem(name):
            return ctx.enter_context(nc.semaphore(name))

        names = {}

        def region(name, words):
            names[name] = ctx.enter_context(nc.sbuf_tensor(name, [P, words], F32))
            return names[name]

        big = region("ring_and_mix", 8192 + 8192)
        R0, R5 = big[:, 0:8192], big[:, 8192:16384]
        R1 = region("r1", 12288)[:, :]
        R23 = region("r23", 10240)[:, :]
        R2, R3 = R23[:, 0:4096], R23[:, 4096:10240]
        R4 = region("r4", 6168)[:, :]
        R6 = region("r6", 4096)[:, :]

        ident = region("ident", P)[:, :]
        mean_w = region("mean_w", P)[:, :]
        iota = region("iota", P)[:, :]
        mask = region("mask", 2 * P)[:, :].rearrange("p (d t) -> p d t", d=2)
        conv_col = region("conv_col", CTILES * TAPS)[:, :]
        chan_col = region("chan_col", 32)[:, :]
        c_sig = region("c_sig", 32)[:, :]
        c_silu = region("c_silu", 32)[:, :]
        stat = region("stat", 96)[:, :]
        gate_w = region("gate_w", KT * GATES)[:, :].rearrange("p (k n) -> p k n", n=GATES)
        gate_b = region("gate_b", 1)[:, :]
        eps_col = region("eps_col", 1)[:, :]
        one_col = region("one_col", 1)[:, :]
        keysT = region("keysT", 2 * NK)[:, :].rearrange("p (h n) -> p h n", h=2)
        m_rows = region("m_rows", T)[0:64, :]
        g_col = region("g_col", 6 * 64)[:, :].rearrange("p (s r) -> p s r", r=64)
        e_col = region("e_col", 4 * 64)[:, :].rearrange("p (s r) -> p s r", r=64)

        ring = R0.rearrange("p (q k n) -> p q k n", q=4, n=NB)
        hT = R1.rearrange("p (k t) -> p k t", t=L)
        x_tile = [R5[:, i * D:(i + 1) * D] for i in range(4)] + [R4[:, i * D:(i + 1) * D] for i in range(2)]
        mod_x, mod_c = R2, R3[:, 0:2 * D]
        g_mix_row = R4[:, 2 * D:3 * D]
        c_rep = R6.rearrange("p (v k m) -> p v k m", v=2, m=P)
        vec_rows = R1[0:32, 0:P]
        chan_rows = R1[0:32, P:2 * P]
        conv_rows = R1[0:TAPS, 1024:2048]
        gate_wp = R3[:, 4096:6144].rearrange("p (k m) -> p k m", m=P)
        u_pad = R4[:, 0:CTILES * ROWS * PADW].rearrange("p (c r w) -> p c r w", r=ROWS, w=PADW)
        mixT = R5.rearrange("p (f t) -> p f t", t=T)
        ln_sq = R6.rearrange("p (f t) -> p f t", t=T)
        qT = R2.rearrange("p (f t) -> p f t", t=T)
        kT = R3.rearrange("p (f t) -> p f t", t=L)
        v_aug = R4.rearrange("p (s h e) -> p s h e", s=6, h=HEADS)
        grow = [R4[0:64, i * L:(i + 1) * L] for i in range(6)]
        g_nat = R4[0:64, 6 * L:7 * L]
        e_nat = R4[0:64, 7 * L:7 * L + T]
        scoreT = R1[:, 0:3072].rearrange("p (s t) -> p s t", t=T)
        probT = R1[:, 3072:9216].rearrange("p (d s t) -> p d s t", d=2, t=T)
        diag_arg = R1[:, 9216:10240].rearrange("p (d s t) -> p d s t", d=2, t=P)
        pick = R1[0:64, 10240:11264].rearrange("p (r m) -> p r m", m=P)
        mod_row = R1[0:1, 11264:12288].rearrange("p (b n) -> p b n", b=2)
        h_sum = R6.rearrange("p (j h e) -> p j h e", j=LT, h=HEADS)
        x2 = R1[:, 0:8192].rearrange("p (j n) -> p j n", j=LT)
        ga1_row, sc2_row, sh2_row = (R4[:, i * D:(i + 1) * D] for i in range(3))
        g_ffn_row = R1[:, 8192:10240]
        out_part = R6[:, 0:2048].rearrange("p (j n) -> p j n", j=LT)
        h2_tile = [R6[:, 0:D], R6[:, D:2 * D]]
        h2T = R23[:, 0:8192].rearrange("p (k t) -> p k t", t=T)
        query = R1[:, 8192:12288].rearrange("p (b m t) -> p b m t", b=2, m=4)
        score = R5.rearrange("p (j s n) -> p j s n", j=LT, n=NK)
        top_val = R4[:, 0:1024].rearrange("p (j s k) -> p j s k", j=LT, k=TOPK)
        top_idx = R4[:, 1024:2048].bitcast(U32).rearrange("p (j s k) -> p j s k", j=LT, k=TOPK)
        best = R4[:, 2048:2560].rearrange("p (j h k) -> p j h k", j=LT, k=TOPK)
        pos = R4[:, 2560:3072].bitcast(U32).rearrange("p (j h k) -> p j h k", j=LT, k=TOPK)
        exp1 = R4[:, 3072:3584].rearrange("p (j h k) -> p j h k", j=LT, k=TOPK)
        exp2 = R4[:, 3584:4096].rearrange("p (j h k) -> p j h k", j=LT, k=TOPK)
        gate = R4[:, 4096:4608].rearrange("p (j h k) -> p j h k", j=LT, k=TOPK)
        pos_a = R4[:, 4608:5120].bitcast(U32).rearrange("p (j h k) -> p j h k", j=LT, k=TOPK)
        pos_b = R4[:, 5120:5632].bitcast(U32).rearrange("p (j h k) -> p j h k", j=LT, k=TOPK)
        slotT = R6[:, 0:1536].rearrange("p (w t) -> p w t", t=T)
        cand = R6[:, 1536:2560].rearrange("p (b h a c) -> p b h a c", b=2, h=2, c=TOPK)
        match = R6[:, 2560:3584].rearrange("p (b h a c) -> p b h a c", b=2, h=2, c=TOPK)
        onehot = R1[:, 8192:12288].rearrange("p (g s w n) -> p g s w n", g=4, s=4, w=2)
        stage = big[:, :].rearrange("p (i t) -> p i t", t=P)
        u_ring = [R0[:, i * D:(i + 1) * D].rearrange("p (k e) -> p k e", e=P) for i in range(2)]
        a_ring = [R0[:, 4096 + i * T:4096 + (i + 1) * T] for i in range(8)]
        v_ring = ([R5[:, i * D:(i + 1) * D] for i in range(4)] + [R6[:, i * D:(i + 1) * D] for i in range(2)]
                  + [R4[:, i * D:(i + 1) * D] for i in range(2)])
        acc = [R1[:, 8192:10240], R1[:, 10240:12288], R23[:, 8192:10240], R4[:, 4096:6144]]
        ga2_row, g_final_row = R0[:, 0:D], R0[:, D:2 * D]

        bank = ctx.enter_context(nc.psum_tensor("bank", [P, 8, 512], F32))

        ssq, rms, rstd = stat[:, 0:6], stat[:, 6:12], stat[:, 12:18]
        hssq, hrms, hrstd = stat[:, 18:34], stat[:, 34:50], stat[:, 50:66]
        ssq2, rms2, rstd2 = stat[:, 66:70], stat[:, 70:74], stat[:, 74:78]
        ssq3, rms3, rstd3 = stat[:, 78:82], stat[:, 82:86], stat[:, 86:90]
        den = region("den", 4)[:, :]
        soft = region("soft", 96)[:, :]

        consts_made = sem("consts_made")
        rows_loaded = sem("rows_loaded")
        gate_b_loaded = sem("gate_b_loaded")
        mod_bias_loaded = sem("mod_bias_loaded")
        x_loaded = [sem(f"x_loaded{i}") for i in range(6)]
        quarter_full = [sem(f"quarter_full{q}") for q in range(4)]
        quarter_used = sem("quarter_used")
        setup_cols = sem("setup_cols")
        csig_made = sem("csig_made")
        dve_a = sem("dve_a")
        crep_made = sem("crep_made")
        x_squared = sem("x_squared")
        x_rms = sem("x_rms")
        mod_bank_free = sem("mod_bank_free")
        h_made = sem("h_made")
        tr_full = sem("tr_full")
        tr_free = sem("tr_free")
        set_free = sem("set_free")
        upad_clear = sem("upad_clear")
        glu_done = sem("glu_done")
        conv_step = sem("conv_step")
        pass_full = sem("pass_full")
        ln_sub = sem("ln_sub")
        ln_std = sem("ln_std")
        ln_rstd = sem("ln_rstd")
        ln_scaled = sem("ln_scaled")
        conv_done = sem("conv_done")
        gate_wp_made = sem("gate_wp_made")
        gate_act = sem("gate_act")
        gate_dve = sem("gate_dve")
        v_ones = sem("v_ones")
        bproj_done = sem("bproj_done")
        pick_made = sem("pick_made")
        m_full = sem("m_full")
        s_full = sem("s_full")
        s_copied = sem("s_copied")
        diag_made = sem("diag_made")
        w_made = sem("w_made")
        p_made = sem("p_made")
        num_full = sem("num_full")
        num_step = sem("num_step")
        num_free = sem("num_free")
        mrow_loaded = [sem(f"mrow_loaded{b}") for b in range(2)]
        mrow_made = sem("mrow_made")
        mrow_stored = [sem(f"mrow_stored{b}") for b in range(2)]
        h_summed = sem("h_summed")
        h_rms = sem("h_rms")
        h_normed = sem("h_normed")
        ht_full = sem("ht_full")
        ht_mixed = sem("ht_mixed")
        x2_loaded = sem("x2_loaded")
        ga1_loaded = sem("ga1_loaded")
        ffn_rows_loaded = sem("ffn_rows_loaded")
        wo_step = sem("wo_step")
        wo_free = sem("wo_free")
        x2_squared = sem("x2_squared")
        x2_rms = sem("x2_rms")
        a2_made = sem("a2_made")
        h2_step = sem("h2_step")
        h2_made = sem("h2_made")
        tr2_full = sem("tr2_full")
        tr2_free = sem("tr2_free")
        q_copied = sem("q_copied")
        score_full = sem("score_full")
        score_copied = sem("score_copied")
        topk = sem("topk")
        soft_in = sem("soft_in")
        soft_exp = sem("soft_exp")
        slots_made = sem("slots_made")
        slotT_full = sem("slotT_full")
        slotT_made = sem("slotT_made")
        onehot_made = sem("onehot_made")
        onehot_used = sem("onehot_used")
        gbank_free = sem("gbank_free")
        table_stored = sem("table_stored")
        acc_clear = sem("acc_clear")
        u_full = [sem(f"u_full{i}") for i in range(2)]
        u_used = sem("u_used")
        g_full = [sem(f"g_full{i}") for i in range(8)]
        v_full = [sem(f"v_full{i}") for i in range(8)]
        gelu_made = sem("gelu_made")
        a_made = sem("a_made")
        o_full = sem("o_full")
        o_free = sem("o_free")
        last_rows = sem("last_rows")
        y_step = sem("y_step")
        y_squared = sem("y_squared")
        y_rms = sem("y_rms")
        y_made = sem("y_made")
        out_stored = sem("out_stored")

        def glu_of(j, half):
            at = (2 * (j % 2) + half) * 2 * T
            return R6[:, at:at + 2 * T].rearrange("p (c t) -> p c t", c=2)

        block = ctx.enter_context(nc.Block())

        @block.sync
        def _(sp):
            def quarter(blk, q, src):
                if not (isinstance(blk, int) and blk == 0):
                    sp.wait_ge(quarter_used, blk * 4 + (q - 3))
                sp.dma_start(ring[:, q, :, :], src).then_inc(quarter_full[q], 16)

            def rows(w, q):
                return w[0, q * QT * P:(q + 1) * QT * P, :]

            def cols(w, q, at):
                return rows(w, q)[:, bass.ds(at, NB)].rearrange("(k p) n -> p k n", p=P)

            for q in range(4):
                quarter(0, q, cols(w_mod, q, 0))
            with sp.Fori(1, 8) as b:
                for q in range(4):
                    quarter(b, q, cols(w_mod, q, b * NB))
            for j in range(4):
                for q in range(4):
                    at = CONV0 + j * 256
                    sp.wait_ge(quarter_used, (CONV + j) * 4 + q - 3)
                    for half in range(2):
                        src = rows(w_in, q)[:, at + half * CW:at + half * CW + 256]
                        sp.dma_start(ring[:, q, :, half * 256:half * 256 + 256],
                                     src.rearrange("(k p) n -> p k n", p=P)).then_inc(quarter_full[q], 8 * 2)
            for n, at in enumerate((0, NB, 3 * MW, 3 * MW + NB, MW, MW + NB, 2 * MW, 2 * MW + NB)):
                for q in range(4):
                    quarter(QO + n, q, cols(w_in, q, at))
            with sp.Fori(0, 16) as b:
                for q in range(4):
                    quarter(b + MOD2, q, cols(w_mod, q, b * NB + 2 * D))
            for w, first in ((w_out, WO), (w_query, WQ)):
                for b in range(4):
                    for q in range(4):
                        quarter(first + b, q, cols(w, q, b * NB))
            for j in range(LT):
                sp.wait_ge(gbank_free, 4 + 32 * (j + 1))
                sp.dma_start(gate_dram[:, :, j * P:(j + 1) * P].rearrange("i p t -> p i t"), stage)\
                  .then_inc(table_stored, 16)
            sp.wait_ge(table_stored, 16 * LT)

            def u_load(n, s, waits):
                if waits:
                    sp.wait_ge(u_used, n - 1)
                sp.dma_start(u_ring[s], u_t[bass.ds(n, 1), :, :].rearrange("a p n -> p (a n)")
                             if not isinstance(n, int) else u_t[n, :, :]).then_inc(u_full[s], 16)

            def g_load(n, s):
                src = gate_dram[bass.ds(n, 1), :, :].rearrange("a p t -> p (a t)") \
                    if not isinstance(n, int) else gate_dram[n, :, :]
                sp.dma_start(a_ring[s], src).then_inc(g_full[s], 16)

            def v_load(n, s):
                sp.dma_start(v_ring[s], v_emb[0, bass.ds(n * P, P), :]).then_inc(v_full[s], 16)

            def expert_group(first, half, waits):
                s0 = 4 * half
                u_load(first, 0, waits)
                u_load(first + 1, 1, waits)
                if waits:
                    sp.wait_ge(o_full, (first - 4) * 4)
                for e in range(4):
                    g_load(first + e, s0 + e)
                u_load(first + 2, 0, True)
                for e in range(2):
                    v_load(first + e, s0 + e)
                u_load(first + 3, 1, True)
                for e in range(2, 4):
                    v_load(first + e, s0 + e)

            expert_group(0, 0, False)
            u_load(4, 0, True)
            u_load(5, 1, True)
            for e in range(4):
                g_load(4 + e, 4 + e)
            u_load(6, 0, True)
            for e in range(2):
                v_load(4 + e, 4 + e)
            u_load(7, 1, True)
            for e in range(2, 4):
                v_load(4 + e, 4 + e)
            with sp.Fori(1, NK // 8) as i:
                expert_group(i * 8, 0, True)
                expert_group(i * 8 + 4, 1, True)
            sp.wait_ge(u_used, NK)
            sp.dma_start(ga2_row, mod_dram[0, 3 * D:4 * D].partition_broadcast(P)).then_inc(last_rows, 16)
            sp.dma_start(g_final_row, g_final[:].partition_broadcast(P)).then_inc(last_rows, 16)
            for j in range(LT):
                sp.wait_ge(y_made, j + 1)
                sp.dma_start(out[0, j * P:(j + 1) * P, :], x2[:, j, :]).then_inc(out_stored, 16)
            sp.wait_ge(out_stored, 16 * LT)

        @block.gpsimd
        def _(pool):
            nc.gpsimd.memset(ident, 0.0).then_inc(consts_made, 1)
            nc.gpsimd.memset(mask, 0.0).then_inc(consts_made, 1)
            nc.gpsimd.memset(gate_b, 0.0).then_inc(consts_made, 1)
            nc.gpsimd.memset(mean_w, 1.0 / CW)
            nc.gpsimd.memset(eps_col, EPS)
            nc.gpsimd.memset(one_col, 1.0)
            nc.gpsimd.iota(iota, pattern=[[1, P]], base=0, channel_multiplier=0,
                           allow_small_or_imprecise_dtypes=True).then_inc(consts_made, 1)
            pool.wait_ge(consts_made, 4)
            nc.gpsimd.affine_select(out=ident, in_=ident, compare_op=ALU.not_equal, fill=1.0, base=0,
                                    pattern=[[-1, P]], channel_multiplier=1).then_inc(consts_made, 1)
            nc.gpsimd.affine_select(out=mask[:, 0, :], in_=mask[:, 0, :], compare_op=ALU.is_ge, fill=BIG, base=0,
                                    pattern=[[1, P]], channel_multiplier=-1).then_inc(consts_made, 1)
            nc.gpsimd.affine_select(out=mask[:, 1, :], in_=mask[:, 1, :], compare_op=ALU.is_ge, fill=BIG, base=0,
                                    pattern=[[-1, P]], channel_multiplier=1).then_inc(consts_made, 1)
            for g, first in enumerate((0, 8, 4, 12)):
                pool.dma_start(gate_b[32 * g:32 * g + 4, :],
                               b_gate[0, first:first + 4].unsqueeze(1)).then_inc(gate_b_loaded, 16)

            pool.wait_ge(h_made, 6)
            pool.wait_ge(tr_full, 24)
            nc.gpsimd.memset(R4[:, 0:CTILES * ROWS * PADW], 0.0).then_inc(upad_clear, 1)
            pool.wait_ge(upad_clear, 1)
            for j in range(4):
                pool.wait_ge(set_free, 2 + j + 1)
                for cc in range(2):
                    last = nc.gpsimd.tensor_tensor(
                        out=u_pad[:, 2 * j + cc, :, TAPS // 2:TAPS // 2 + GRID_W],
                        in0=glu_of(j, 0)[:, cc, :].rearrange("p (r w) -> p r w", w=GRID_W),
                        in1=glu_of(j, 1)[:, cc, :].rearrange("p (r w) -> p r w", w=GRID_W), op=ALU.mult)
                last.then_inc(glu_done, 1)

            pool.wait_ge(bproj_done, 1)
            for b in range(16):
                if b >= 2:
                    pool.wait_ge(mrow_stored[b % 2], 16 * (b // 2))
                pool.dma_start(mod_row[:, b % 2, :], b_mod[0:1, 2 * D + b * NB:2 * D + (b + 1) * NB])\
                    .then_inc(mrow_loaded[b % 2], 16)
                if b >= 1:
                    pool.wait_ge(mrow_made, b)
                    pool.dma_start(mod_dram[:, (b - 1) * NB:b * NB], mod_row[:, (b - 1) % 2, :])\
                        .then_inc(mrow_stored[(b - 1) % 2], 16)
            pool.wait_ge(mrow_made, 16)
            pool.dma_start(mod_dram[:, 15 * NB:16 * NB], mod_row[:, 1, :]).then_inc(mrow_stored[1], 16)
            pool.wait_ge(mrow_stored[0], 16 * 8)
            pool.wait_ge(mrow_stored[1], 16 * 8)
            pool.wait_ge(num_full, 8 * LT)
            for k, row in enumerate((ga1_row, sh2_row, sc2_row)):
                pool.dma_start(row, mod_dram[0, k * D:(k + 1) * D].partition_broadcast(P))\
                    .then_inc(ga1_loaded if k == 0 else ffn_rows_loaded, 16)
            for j in range(LT):
                pool.dma_start(x2[:, j, :], x[0, j * P:(j + 1) * P, :]).then_inc(x2_loaded, 16)
            pool.wait_ge(h_summed, 16)
            pool.dma_start(g_ffn_row, g_ffn[0, :].partition_broadcast(P)).then_inc(ffn_rows_loaded, 16)
            pool.wait_ge(gbank_free, 4 + 128)
            for part in acc:
                last = nc.gpsimd.memset(part, 0.0)
            last.then_inc(acc_clear, 1)

        @block.scalar
        def _(act):
            act.dma_start(vec_rows[0:16, :], c[0, :].rearrange("(k p) -> k p", p=P)).then_inc(rows_loaded, 16)
            act.dma_start(vec_rows[16:32, :], c_ctx[:].rearrange("(k p) -> k p", p=P)).then_inc(rows_loaded, 16)
            for n, src in enumerate((cn_g, cn_b, conv_b, g_mhn)):
                act.dma_start(chan_rows[8 * n:8 * n + 8, :],
                              src[0, :].rearrange("(k p) -> k p", p=P)).then_inc(rows_loaded, 16)
            act.dma_start(conv_rows, conv_w[0, :, :]).then_inc(rows_loaded, 16)
            act.dma_start(gate_w, w_in[0, :, GATE0:CONV0].rearrange("(k p) n -> p k n", p=P))\
               .then_inc(rows_loaded, 16)
            act.dma_start(keysT, keys_t[:, :, :]).then_inc(rows_loaded, 16)
            act.dma_start(mod_x, b_mod[0, 0:2 * D].partition_broadcast(P)).then_inc(mod_bias_loaded, 16)
            act.dma_start(mod_c, b_mod[0, 0:2 * D].partition_broadcast(P)).then_inc(mod_bias_loaded, 16)
            act.dma_start(g_mix_row, g_mix[0, :].partition_broadcast(P)).then_inc(mod_bias_loaded, 16)
            for i in range(6):
                src = x[0, i * P:(i + 1) * P, :] if i < LT else ctx_in[0, (i - LT) * P:(i - LT + 1) * P, :]
                act.dma_start(x_tile[i], src).then_inc(x_loaded[i], 16)
            act.sem_inc(set_free, 2)

            act.wait_ge(setup_cols, 1)
            nc.scalar.activation(c_sig, bank[:, 0, 0:32], ACT.Sigmoid).then_inc(csig_made, 1)
            for i in range(6):
                act.wait_ge(x_loaded[i], 16)
                if i:
                    act.wait_ge(x_squared, i)
                nc.scalar.activation(bank[:, 4:8, :], x_tile[i].rearrange("p (b n) -> p b n", b=4), ACT.Square,
                                     accum_out=ssq[:, i:i + 1]).then_inc(x_squared, 1)
            act.wait_ge(x_squared, 6)
            act.wait_ge(consts_made, 7)
            nc.scalar.activation(rms, ssq, ACT.Sqrt, bias=eps_col, scale=1.0 / D).then_inc(x_rms, 1)
            for i in range(6):
                for g in range(4):
                    act.wait_ge(tr_full, 4 * i + g + 1)
                    nc.scalar.activation(hT[:, 4 * g:4 * g + 4, i * P:(i + 1) * P],
                                         bank[:, 4 + g, :].rearrange("p (k t) -> p k t", k=4), ACT.Copy)\
                        .then_inc(tr_free, 1)

            for j in range(4):
                s = 4 * (j % 2)
                act.wait_ge(quarter_used, 4 * (CONV + j + 1))
                if j >= 2:
                    act.wait_ge(glu_done, j - 1)
                nc.scalar.activation(glu_of(j, 0), bank[:, s:s + 2, :], ACT.Copy)
                nc.scalar.activation(glu_of(j, 1), bank[:, s + 2:s + 4, :], ACT.Sigmoid).then_inc(set_free, 1)
            for j in range(2):
                act.wait_ge(quarter_used, 4 * (QO + j + 1))
                s = 4 * (j % 2)
                nc.scalar.activation(qT[:, 4 * j:4 * j + 4, :], bank[:, s:s + 4, :], ACT.Copy,
                                     scale=HD ** -0.5).then_inc(set_free, 1)
            for j in range(2):
                act.wait_ge(quarter_used, 4 * (QO + 2 + j + 1))
                s = 4 * (j % 2)
                nc.scalar.activation(mixT[:, 4 * j:4 * j + 4, :], bank[:, s:s + 4, :], ACT.Sigmoid)\
                    .then_inc(set_free, 1)
            act.wait_ge(ln_sub, 8)
            nc.scalar.activation(ln_sq, mixT[:, 8:16, :], ACT.Square).then_inc(set_free, 1)
            act.wait_ge(pass_full, 2)
            act.wait_ge(gate_b_loaded, 64)
            for kind in range(2):
                for d in range(2):
                    src = 64 * kind + 32 * d
                    dst = grow[kind][32 * d:32 * d + 32, :]
                    dst_c, dst_x = dst[:, 0:C], dst[:, C:L]
                    if d:
                        dst_c, dst_x = dst_c[:, ::-1], dst_x[:, ::-1]
                    nc.scalar.activation(dst_x, bank[src:src + 32, 4, 0:T], ACT.Identity,
                                         bias=gate_b[src:src + 32, :])
                    last = nc.scalar.activation(dst_c, bank[src:src + 32, 5, 0:C], ACT.Identity,
                                                bias=gate_b[src:src + 32, :])
            last.then_inc(set_free, 1)
            act.wait_ge(set_free, 2 + 10)
            nc.scalar.activation(grow[2], grow[1], ACT.Abs).then_inc(gate_act, 1)
            act.wait_ge(gate_act, 1)
            nc.scalar.activation(grow[3], grow[2], ACT.Exp, scale=-1.0).then_inc(gate_act, 1)
            act.wait_ge(gate_act, 2)
            nc.scalar.activation(grow[4], grow[3], ACT.Ln, bias=one_col[0:64, :]).then_inc(gate_act, 1)
            act.wait_ge(pass_full, 3)
            nc.scalar.activation(kT[:, 0:4, 0:T], bank[:, 0:4, :], ACT.Copy).then_inc(set_free, 1)
            act.wait_ge(quarter_used, 4 * (KV + 1))
            nc.scalar.activation(kT[:, 0:4, T:L], bank[:, 4:8, 0:C], ACT.Copy).then_inc(set_free, 1)
            act.wait_ge(gate_dve, 5)
            nc.scalar.activation(grow[1], grow[2], ACT.Exp, scale=-1.0).then_inc(gate_act, 1)
            act.wait_ge(pass_full, 4)
            act.wait_ge(set_free, 2 + 12)
            nc.scalar.activation(glu_of(0, 0)[:, 0, :], bank[:, 0, :], ACT.Sqrt, bias=eps_col).then_inc(set_free, 1)
            act.wait_ge(pass_full, 5)
            nc.scalar.activation(kT[:, 4:8, 0:T], bank[:, 4:8, :], ACT.Copy).then_inc(set_free, 1)
            act.wait_ge(quarter_used, 4 * (KV + 2))
            nc.scalar.activation(kT[:, 4:8, T:L], bank[:, 0:4, 0:C], ACT.Copy).then_inc(set_free, 1)
            act.wait_ge(ln_scaled, 8)
            for f in range(CTILES):
                nc.scalar.activation(mixT[:, 8 + f, :], mixT[:, 8 + f, :], ACT.Silu,
                                     bias=chan_col[:, 8 + f:9 + f], scale=chan_col[:, f:f + 1])\
                    .then_inc(conv_done, 1)
            act.wait_ge(pass_full, 6)
            nc.scalar.activation(g_col, bank[:, 4, 0:384].rearrange("p (s r) -> p s r", r=64), ACT.Copy)
            nc.scalar.activation(e_col, bank[:, 5, 0:256].rearrange("p (s r) -> p s r", r=64), ACT.Copy)\
                .then_inc(set_free, 1)
            act.wait_ge(v_ones, 1)
            for half in range(2):
                act.wait_ge(pass_full, 7 + half)
                for j in range(LT):
                    last = nc.scalar.activation(v_aug[:, j, 2 * half:2 * half + 2, 0:HD],
                                                bank[:, j, :].rearrange("p (h e) -> p h e", h=2), ACT.Copy)
                last.then_inc(set_free, 1)
                act.wait_ge(quarter_used, 4 * (KV + 2 + half + 1))
                for j in range(CT):
                    last = nc.scalar.activation(v_aug[:, LT + j, 2 * half:2 * half + 2, 0:HD],
                                                bank[:, 4 + j, :].rearrange("p (h e) -> p h e", h=2), ACT.Copy)
                last.then_inc(set_free, 1)

            for h in range(HEADS):
                for s in range(6):
                    act.wait_ge(s_full, 6 * h + s + 1)
                    if h and s == 0:
                        act.wait_ge(p_made, 12 * h)
                    nc.scalar.activation(scoreT[:, s, :], bank[:, s % 2, :], ACT.Copy).then_inc(s_copied, 1)
                for d in range(2):
                    act.wait_ge(diag_made, 8 * h + 4 * (d + 1))
                    if h:
                        act.wait_ge(num_full, 8 * h)
                    r = 32 * d + h
                    for s in range(6):
                        g = g_col[:, s, r:r + 1]
                        if s >= LT:
                            last = nc.scalar.activation(probT[:, d, s, :], bank[:, 2 + d, :], ACT.Exp, bias=g,
                                                        scale=-1.0)
                        else:
                            lo, hi = ((s + 1) * P, T) if d == 0 else (0, s * P)
                            if hi > lo:
                                nc.scalar.activation(probT[:, d, s, lo:hi], bank[:, 2 + d, lo:hi], ACT.Exp, bias=g,
                                                     scale=-1.0)
                            last = nc.scalar.activation(probT[:, d, s, s * P:(s + 1) * P], diag_arg[:, d, s, :],
                                                        ACT.Exp, scale=-1.0)
                        last.then_inc(w_made, 1)
            act.wait_ge(h_summed, 16)
            nc.scalar.activation(hrms, hssq, ACT.Sqrt, bias=eps_col, scale=1.0 / HD).then_inc(h_rms, 1)

            for j in range(LT):
                act.wait_ge(wo_step, 4 * 8)
                if j:
                    act.wait_ge(x2_squared, j)
                nc.scalar.activation(bank[:, 0:4, :], x2[:, j, :].rearrange("p (b n) -> p b n", b=4), ACT.Square,
                                     accum_out=ssq2[:, j:j + 1]).then_inc(x2_squared, 1)
            act.wait_ge(x2_squared, LT)
            nc.scalar.activation(rms2, ssq2, ACT.Sqrt, bias=eps_col, scale=1.0 / D).then_inc(x2_rms, 1)
            for i in range(LT):
                for g in range(4):
                    act.wait_ge(tr2_full, 4 * i + g + 1)
                    nc.scalar.activation(h2T[:, 4 * g:4 * g + 4, i * P:(i + 1) * P],
                                         bank[:, 4 + g, :].rearrange("p (k t) -> p k t", k=4), ACT.Copy)\
                        .then_inc(tr2_free, 1)

            def copy_query(b):
                act.wait_ge(quarter_used, 4 * (WQ + b + 1))
                s = 4 * (b % 2)
                nc.scalar.activation(query[:, b % 2, :, :], bank[:, s:s + 4, :], ACT.Copy).then_inc(q_copied, 1)

            def copy_scores(b):
                act.wait_ge(score_full, b + 1)
                s = 4 * (b % 2)
                for m in range(4):
                    last = nc.scalar.activation(score[:, :, 4 * b + m, :],
                                                bank[:, s + m, :].rearrange("p (j n) -> p j n", j=LT), ACT.Copy)
                last.then_inc(score_copied, 1)

            copy_query(0)
            for b in range(1, 4):
                copy_query(b)
                copy_scores(b - 1)
            copy_scores(3)
            act.wait_ge(soft_in, 1)
            nc.scalar.activation(gate, gate, ACT.Exp).then_inc(soft_exp, 1)
            for w in range(3):
                act.wait_ge(slotT_full, w + 1)
                nc.scalar.activation(slotT[:, w, :], bank[:, w, :], ACT.Copy).then_inc(slotT_made, 1)
            act.sem_inc(gbank_free, 4)
            for j in range(LT):
                if j:
                    act.wait_ge(table_stored, 16 * j)
                with act.Fori(0, 8) as i:
                    for g in range(4):
                        act.wait_ge(onehot_used, i * 4 + (4 + 32 * j + g + 1))
                        nc.scalar.activation(
                            stage[:, :, bass.ds(i * 16 + 4 * g, 4)].rearrange("p i t -> p t i"),
                            bank[:, 4 + g, :].rearrange("p (t i) -> p t i", t=4), ACT.Copy)\
                            .then_inc(gbank_free, 1)
            with act.Fori(0, NK // 4) as i:
                for e in range(4):
                    act.wait_ge(u_used, i * 4 + (e + 1))
                    nc.scalar.activation(bank[:, e, :], bank[:, e, :], ACT.Gelu).then_inc(gelu_made, 1)
            for j in range(LT):
                act.wait_ge(y_step, 2 * (j + 1))
                if j:
                    act.wait_ge(y_squared, j)
                nc.scalar.activation(bank[:, 0:4, :], x2[:, j, :].rearrange("p (b n) -> p b n", b=4), ACT.Square,
                                     accum_out=ssq3[:, j:j + 1]).then_inc(y_squared, 1)
            act.wait_ge(y_squared, LT)
            nc.scalar.activation(rms3, ssq3, ACT.Sqrt, bias=eps_col, scale=1.0 / D).then_inc(y_rms, 1)

        @block.vector
        def _(dve):
            dve.sem_inc(mod_bank_free, 2)
            dve.wait_ge(setup_cols, 2)
            nc.vector.tensor_copy(chan_col, bank[:, 2, 0:32])
            nc.vector.tensor_copy(conv_col, bank[:, 1, 0:CTILES * TAPS]).then_inc(dve_a, 1)
            dve.wait_ge(csig_made, 1)
            nc.vector.tensor_tensor(c_silu, bank[:, 0, 0:32], c_sig, ALU.mult).then_inc(dve_a, 1)
            dve.wait_ge(dve_a, 2)
            for w in range(2):
                nc.vector.tensor_copy(c_rep[:, w, :, :], c_silu[:, KT * w:KT * w + KT].unsqueeze(2)
                                      .to_broadcast([P, KT, P])).then_inc(crep_made, 1)
            nc.vector.memset(gate_wp, 0.0).then_inc(dve_a, 1)
            dve.wait_ge(dve_a, 3)
            dve.wait_ge(rows_loaded, 16 * 9)
            for g, first in enumerate((0, 8, 4, 12)):
                last = nc.vector.tensor_copy(gate_wp[:, :, 32 * g:32 * g + 4], gate_w[:, :, first:first + 4])
            last.then_inc(gate_wp_made, 1)
            dve.wait_ge(mod_bias_loaded, 48)
            with dve.Fori(0, 4) as i:
                for par in range(2):
                    dve.wait_ge(quarter_used, i * 8 + 4 * (par + 1))
                    at = bass.ds(i * (2 * NB) + par * NB, NB)
                    nc.vector.tensor_tensor(mod_x[:, at], mod_x[:, at], bank[:, 2 * par, :], ALU.add)
                    nc.vector.tensor_tensor(mod_c[:, at], mod_c[:, at], bank[:, 2 * par + 1, :], ALU.add)\
                        .then_inc(mod_bank_free, 1)
            dve.wait_ge(mod_bank_free, 2 + 8)
            dve.wait_ge(x_rms, 1)
            nc.vector.reciprocal(rstd, rms).then_inc(dve_a, 1)
            for m in (mod_x, mod_c):
                nc.vector.scalar_tensor_tensor(m[:, D:2 * D], m[:, D:2 * D], 1.0, g_mix_row, ALU.add, ALU.mult)\
                    .then_inc(dve_a, 1)
            dve.wait_ge(dve_a, 6)
            for i in range(6):
                m = mod_x if i < LT else mod_c
                nc.vector.scalar_tensor_tensor(x_tile[i], x_tile[i], rstd[:, i:i + 1], m[:, D:2 * D], ALU.mult,
                                               ALU.mult).then_inc(dve_a, 1)
                dve.wait_ge(dve_a, 7 + i)
                nc.vector.tensor_tensor(x_tile[i], x_tile[i], m[:, 0:D], ALU.add).then_inc(h_made, 1)

            with dve.Fori(0, 4) as j:
                dve.wait_ge(glu_done, j + 1)
                for tap in range(TAPS):
                    for cc in range(2):
                        n = 2 * tap + cc
                        ct = j * 2 + cc
                        y = R5[:, bass.ds(j * (2 * T) + (8 + cc) * T, T)].rearrange("p (r w) -> p r w", w=GRID_W)
                        u = R4[:, bass.ds(j * (2 * ROWS * PADW) + cc * ROWS * PADW, ROWS * PADW)]\
                            .rearrange("p (r w) -> p r w", w=PADW)[:, :, tap:tap + GRID_W]
                        w = conv_col[:, bass.ds(j * (2 * TAPS) + cc * TAPS + tap, 1)]
                        if tap == 0:
                            nc.vector.tensor_scalar(y, u, w, chan_col[:, bass.ds(j * 2 + 16 + cc, 1)], ALU.mult,
                                                    ALU.add).then_inc(conv_step, 1)
                        else:
                            dve.wait_ge(conv_step, j * (2 * TAPS) + (n - 1))
                            nc.vector.scalar_tensor_tensor(y, u, w, y, ALU.mult, ALU.add).then_inc(conv_step, 1)
            dve.wait_ge(pass_full, 1)
            for f in range(CTILES):
                nc.vector.tensor_tensor(mixT[:, 8 + f, :], mixT[:, 8 + f, :], bank[:, 0, :], ALU.subtract)\
                    .then_inc(ln_sub, 1)
            dve.wait_ge(gate_act, 3)
            nc.vector.scalar_tensor_tensor(grow[5], grow[1], 0.0, grow[4], ALU.min, ALU.subtract)\
                .then_inc(gate_dve, 1)
            dve.wait_ge(gate_dve, 1)
            nc.vector.tensor_tensor_scan(grow[3], one_col[0:64, :].to_broadcast([64, L]), grow[5], 0.0, ALU.mult,
                                         ALU.add).then_inc(gate_dve, 1)
            dve.wait_ge(gate_dve, 2)
            nc.vector.tensor_tensor(grow[4], grow[0], grow[3], ALU.subtract).then_inc(gate_dve, 1)
            dve.wait_ge(gate_dve, 3)
            nc.vector.tensor_tensor_scan(grow[5], grow[4], grow[4], 0.0, ALU.max, ALU.max).then_inc(gate_dve, 1)
            dve.wait_ge(gate_dve, 4)
            nc.vector.tensor_tensor(grow[2], grow[3], grow[5], ALU.add).then_inc(gate_dve, 1)
            dve.wait_ge(gate_act, 4)
            for d in range(2):
                r = slice(32 * d, 32 * d + 32)
                g_c, g_x = g_nat[r, 0:C], g_nat[r, C:L]
                m_x, e_x = m_rows[r, :], e_nat[r, :]
                if d:
                    g_c, g_x, m_x, e_x = g_c[:, ::-1], g_x[:, ::-1], m_x[:, ::-1], e_x[:, ::-1]
                nc.vector.tensor_copy(g_c, grow[4][r, 0:C])
                nc.vector.tensor_copy(g_x, grow[4][r, C:L])
                nc.vector.tensor_copy(m_x, grow[5][r, C:L])
                nc.vector.tensor_copy(e_x, grow[1][r, C:L]).then_inc(gate_dve, 1)
            dve.wait_ge(set_free, 2 + 13)
            nc.vector.reciprocal(glu_of(0, 0)[:, 1, :], glu_of(0, 0)[:, 0, :]).then_inc(ln_rstd, 1)
            dve.wait_ge(ln_rstd, 1)
            for f in range(CTILES):
                nc.vector.tensor_tensor(mixT[:, 8 + f, :], mixT[:, 8 + f, :], glu_of(0, 0)[:, 1, :], ALU.mult)\
                    .then_inc(ln_scaled, 1)
            dve.wait_ge(set_free, 2 + 16)
            nc.vector.memset(v_aug[:, :, :, HD:HD + 1], 1.0).then_inc(v_ones, 1)

            dve.wait_ge(quarter_used, 4 * (KV + 4))
            dve.wait_ge(consts_made, 7)
            for r in range(8):
                col = 32 * (r // HEADS) + r % HEADS
                last = nc.vector.tensor_copy(pick[:, r, :], ident[0:64, col:col + 1].to_broadcast([64, P]))
            last.then_inc(pick_made, 1)
            steps = 0
            for h in range(HEADS):
                for d in range(2):
                    r = 32 * d + h
                    dve.wait_ge(m_full, 2 * h + d + 1)
                    if h:
                        dve.wait_ge(w_made, 12 * h)
                        dve.wait_ge(h_summed, 4 * h)
                    for s in range(LT):
                        nc.vector.scalar_tensor_tensor(diag_arg[:, d, s, :], bank[:, 2 + d, s * P:(s + 1) * P],
                                                       g_col[:, s, r:r + 1], mask[:, d, :], ALU.subtract, ALU.max)\
                            .then_inc(diag_made, 1)
                dve.wait_ge(s_copied, 6 * (h + 1))
                for d in range(2):
                    for s in range(6):
                        lo, hi = (0, T) if s >= LT else ((s * P, T) if d == 0 else (0, (s + 1) * P))
                        dve.wait_ge(w_made, 12 * h + 6 * d + s + 1)
                        nc.vector.tensor_tensor(probT[:, d, s, lo:hi], probT[:, d, s, lo:hi], scoreT[:, s, lo:hi],
                                                ALU.mult).then_inc(p_made, 1)
                for b in range(4 * h, 4 * h + 4):
                    dve.wait_ge(quarter_used, 4 * (MOD2 + b + 1))
                    dve.wait_ge(mrow_loaded[b % 2], 16 * (b // 2 + 1))
                    nc.vector.tensor_tensor(mod_row[:, b % 2, :], mod_row[:, b % 2, :], bank[0:1, 6 + b % 2, :],
                                            ALU.add).then_inc(mrow_made, 1)
                for j in range(LT):
                    for d in range(2):
                        nb = bank[:, 4 + d, :]
                        dve.wait_ge(num_full, 8 * h + 2 * j + d + 1)
                        nc.vector.tensor_scalar(den[:, d:d + 1], nb[:, HD:HD + 1], -1.0,
                                                e_col[:, j, 32 * d + h:32 * d + h + 1], ALU.mult, ALU.max)\
                            .then_inc(num_step, 1)
                        steps += 1
                        dve.wait_ge(num_step, steps)
                        nc.vector.tensor_tensor(den[:, d:d + 1], nb[:, HD:HD + 1], den[:, d:d + 1], ALU.max)\
                            .then_inc(num_step, 1)
                        steps += 1
                        dve.wait_ge(num_step, steps)
                        nc.vector.reciprocal(den[:, 2 + d:3 + d], den[:, d:d + 1]).then_inc(num_step, 1)
                        steps += 1
                        dve.wait_ge(num_step, steps)
                        hs = h_sum[:, j, h, :]
                        if d == 0:
                            nc.vector.tensor_scalar(hs, nb[:, 0:HD], den[:, 2:3], None, ALU.mult)\
                                .then_inc(num_free, 1)
                        else:
                            dve.wait_ge(num_free, 8 * h + 2 * j + 1)
                            nc.vector.scalar_tensor_tensor(hs, nb[:, 0:HD], den[:, 3:4], hs, ALU.mult, ALU.add)\
                                .then_inc(num_free, 1)
                for j in range(LT):
                    hs = h_sum[:, j, h, :]
                    dve.wait_ge(num_free, 8 * h + 2 * j + 2)
                    if j or h:
                        dve.wait_ge(h_summed, 4 * h + j)
                    nc.vector.tensor_tensor_reduce(out=diag_arg[:, 0, 0:2, :].rearrange("p a b -> p (a b)"), in0=hs,
                                                   in1=hs, scale=1.0, scalar=0.0, op0=ALU.mult, op1=ALU.add,
                                                   accum_out=hssq[:, 4 * j + h:4 * j + h + 1]).then_inc(h_summed, 1)
            dve.wait_ge(h_rms, 1)
            nc.vector.reciprocal(hrstd, hrms).then_inc(num_step, 1)
            steps += 1
            dve.wait_ge(num_step, steps)
            for h in range(HEADS):
                for j in range(LT):
                    hs = h_sum[:, j, h, :]
                    nc.vector.tensor_scalar(hs, hs, hrstd[:, 4 * j + h:4 * j + h + 1], None, ALU.mult)\
                        .then_inc(h_normed, 1)
            for f in range(8):
                dve.wait_ge(ht_full, f + 1)
                nc.vector.scalar_tensor_tensor(mixT[:, f, :], bank[:, f % 4, :], chan_col[:, 24 + f:25 + f],
                                               mixT[:, f, :], ALU.mult, ALU.mult).then_inc(ht_mixed, 1)

            dve.sem_inc(wo_free, 2)
            dve.wait_ge(ga1_loaded, 16)
            dve.wait_ge(x2_loaded, 64)
            with dve.Fori(0, 2) as i:
                for par in range(2):
                    at = bass.ds(i * (2 * NB) + par * NB, NB)
                    dve.wait_ge(quarter_used, i * 8 + 4 * (WO + par + 1))
                    for j in range(LT):
                        ins = nc.vector.tensor_tensor(out_part[:, j, :], bank[:, 4 * par + j, :], ga1_row[:, at],
                                                      ALU.mult)
                        ins.then_inc(wo_step, 1)
                    dve.wait_ge(wo_step, i * 16 + 8 * par + 4)
                    for j in range(LT):
                        nc.vector.tensor_tensor(x2[:, j, at], x2[:, j, at], out_part[:, j, :], ALU.add)\
                            .then_inc(wo_step, 1)
                    dve.wait_ge(wo_step, i * 16 + 8 * par + 8)
                    dve.sem_inc(wo_free, 1)
            dve.wait_ge(ffn_rows_loaded, 48)
            nc.vector.scalar_tensor_tensor(sc2_row, sc2_row, 1.0, g_ffn_row, ALU.add, ALU.mult).then_inc(a2_made, 1)
            dve.wait_ge(x2_rms, 1)
            nc.vector.reciprocal(rstd2, rms2).then_inc(a2_made, 1)
            dve.wait_ge(a2_made, 2)
            for i in range(LT):
                if i >= 2:
                    dve.wait_ge(tr2_full, 4 * (i - 1))
                nc.vector.scalar_tensor_tensor(h2_tile[i % 2], x2[:, i, :], rstd2[:, i:i + 1], sc2_row, ALU.mult,
                                               ALU.mult).then_inc(h2_step, 1)
                dve.wait_ge(h2_step, i + 1)
                nc.vector.tensor_tensor(h2_tile[i % 2], h2_tile[i % 2], sh2_row, ALU.add).then_inc(h2_made, 1)

            done = [0]

            def put(ins):
                ins.then_inc(topk, 1)
                done[0] += 1

            def top16(jobs):
                start = done[0]
                n = len(jobs)
                for k, (src, val, idx) in enumerate(jobs):
                    put(nc.vector.max(val[:, 0:8], src))
                for k, (src, val, idx) in enumerate(jobs):
                    dve.wait_ge(topk, start + k + 1)
                    put(nc.vector.max_index(idx[:, 0:8], val[:, 0:8], src))
                for k, (src, val, idx) in enumerate(jobs):
                    put(nc.vector.match_replace(src, val[:, 0:8], src, NEG))
                for k, (src, val, idx) in enumerate(jobs):
                    dve.wait_ge(topk, start + 2 * n + k + 1)
                    put(nc.vector.max(val[:, 8:16], src))
                for k, (src, val, idx) in enumerate(jobs):
                    dve.wait_ge(topk, start + 3 * n + k + 1)
                    put(nc.vector.max_index(idx[:, 8:16], val[:, 8:16], src))
                dve.wait_ge(topk, done[0])

            dve.wait_ge(tr2_full, 16)
            for b in range(4):
                dve.wait_ge(score_copied, b + 1)
                hh = slice(2 * b, 2 * b + 2)
                for j in range(LT):
                    top16([(score[:, j, 4 * b + m, :], top_val[:, j, 4 * b + m, :], top_idx[:, j, 4 * b + m, :])
                           for m in range(4)])
                for j0 in range(0, LT, 2):
                    for jj in range(2):
                        val = top_val[:, j0 + jj, 4 * b:4 * b + 4, :].rearrange("p (h s) k -> p h s k", s=2)
                        put(nc.vector.tensor_tensor(
                            cand[:, jj], val[:, :, 0, :].unsqueeze(3).to_broadcast([P, 2, TOPK, TOPK]),
                            val[:, :, 1, :].unsqueeze(2).to_broadcast([P, 2, TOPK, TOPK]), ALU.add))
                    dve.wait_ge(topk, done[0])
                    top16([(cand[:, jj, hl].rearrange("p a c -> p (a c)"), best[:, j0 + jj, 2 * b + hl, :],
                            pos[:, j0 + jj, 2 * b + hl, :]) for jj in range(2) for hl in range(2)])
                put(nc.vector.tensor_single_scalar(pos_a[:, :, hh, :], pos[:, :, hh, :], 4,
                                                   ALU.logical_shift_right))
                put(nc.vector.tensor_single_scalar(pos_b[:, :, hh, :], pos[:, :, hh, :], 15, ALU.bitwise_and))
                dve.wait_ge(topk, done[0])
                for j in range(LT):
                    idx = top_idx[:, j, 4 * b:4 * b + 4, :].rearrange("p (h s) k -> p h s k", s=2)
                    full = [P, 2, TOPK, TOPK]
                    for s, which in enumerate((pos_a, pos_b)):
                        put(nc.vector.tensor_tensor(
                            match[:, s], iota[:, 0:TOPK].unsqueeze(1).unsqueeze(1).to_broadcast(full),
                            which[:, j, hh, :].unsqueeze(3).to_broadcast(full), ALU.is_equal))
                    dve.wait_ge(topk, done[0])
                    for s in range(2):
                        put(nc.vector.tensor_tensor(match[:, s], match[:, s],
                                                    idx[:, :, s, :].unsqueeze(2).to_broadcast(full), ALU.mult))
                    dve.wait_ge(topk, done[0])
                    for s, dst in enumerate((exp1, exp2)):
                        put(nc.vector.tensor_reduce(dst[:, j, hh, :], match[:, s], AX.X, ALU.add))
                    dve.wait_ge(topk, done[0])
            dve.wait_ge(topk, done[0])
            best_g = best.rearrange("p j h k -> p (j h) k")
            gate_g = gate.rearrange("p j h k -> p (j h) k")
            nc.vector.tensor_tensor(gate_g, best_g, best_g[:, :, 0:1].to_broadcast([P, LT * PH, TOPK]),
                                    ALU.subtract).then_inc(soft_in, 1)
            dve.wait_ge(soft_exp, 1)
            put(nc.vector.tensor_reduce(soft[:, 0:32], gate_g, AX.X, ALU.add))
            dve.wait_ge(topk, done[0])
            put(nc.vector.reciprocal(soft[:, 32:64], soft[:, 0:32]))
            dve.wait_ge(topk, done[0])
            nc.vector.tensor_tensor(gate_g, gate_g, soft[:, 32:64].unsqueeze(2).to_broadcast([P, LT * PH, TOPK]),
                                    ALU.mult).then_inc(slots_made, 1)
            dve.wait_ge(slotT_made, 3)
            with dve.Fori(0, 32) as i:
                for g in range(4):
                    dve.wait_ge(onehot_used, i * 4 + (g + 1))
                    for s in range(4):
                        tok = bass.ds(i * 16 + 4 * g + s, 1)
                        nc.vector.tensor_scalar(onehot[:, g, s, 0, :], iota, slotT[:, 0, tok], None, ALU.is_equal)
                        last = nc.vector.tensor_scalar(onehot[:, g, s, 1, :], iota, slotT[:, 1, tok],
                                                       slotT[:, 2, tok], ALU.is_equal, ALU.mult)
                    last.then_inc(onehot_made, 1)

            def weigh_group(g, half, i_of):
                for e in range(4):
                    s = 4 * half + e
                    dve.wait_ge(gelu_made, g * 4 + (e + 1))
                    dve.wait_ge(g_full[s], i_of)
                    nc.vector.tensor_tensor(a_ring[s], bank[:, e, :], a_ring[s], ALU.mult).then_inc(a_made, 1)

            def add_group(g):
                for o in range(16):
                    j, n = o // 4, o % 4
                    dve.wait_ge(o_full, g * 16 + (o + 1))
                    part = acc[j][:, n * NB:(n + 1) * NB]
                    nc.vector.tensor_tensor(part, part, bank[:, 4 + o % 4, :], ALU.add).then_inc(o_free, 1)

            dve.sem_inc(o_free, 4)
            dve.wait_ge(acc_clear, 1)
            weigh_group(0, 0, 16)
            with dve.Fori(0, 15) as i:
                weigh_group(i * 2 + 1, 1, i * 16 + 16)
                add_group(i * 2)
                weigh_group(i * 2 + 2, 0, i * 16 + 32)
                add_group(i * 2 + 1)
            weigh_group(31, 1, 16 * 16)
            add_group(30)
            add_group(31)
            dve.wait_ge(last_rows, 32)
            dve.wait_ge(o_free, 4 + 16 * 32)
            for j in range(LT):
                nc.vector.tensor_tensor(acc[j], acc[j], ga2_row, ALU.mult).then_inc(y_step, 1)
                dve.wait_ge(y_step, 2 * j + 1)
                nc.vector.tensor_tensor(x2[:, j, :], x2[:, j, :], acc[j], ALU.add).then_inc(y_step, 1)
            dve.wait_ge(y_rms, 1)
            nc.vector.reciprocal(rstd3, rms3).then_inc(y_step, 1)
            dve.wait_ge(y_step, 9)
            for j in range(LT):
                nc.vector.scalar_tensor_tensor(x2[:, j, :], x2[:, j, :], rstd3[:, j:j + 1], g_final_row, ALU.mult,
                                               ALU.mult).then_inc(y_made, 1)

        @block.tensor
        def _(pe):
            mm = nc.tensor.matmul
            pe.wait_ge(consts_made, 5)
            pe.wait_ge(rows_loaded, 16 * 9)
            nc.tensor.transpose(bank[:, 0, 0:32], vec_rows, ident[0:32, 0:32]).then_inc(setup_cols, 1)
            nc.tensor.transpose(bank[:, 2, 0:32], chan_rows, ident[0:32, 0:32])
            for f in range(CTILES):
                last = nc.tensor.transpose(bank[:, 1, TAPS * f:TAPS * (f + 1)], conv_rows[:, f * P:(f + 1) * P],
                                           ident[0:TAPS, 0:TAPS])
            last.then_inc(setup_cols, 1)
            pe.wait_ge(crep_made, 2)

            def wait_quarter(blk, q):
                pe.wait_ge(quarter_full[q], (blk + 1) * 16)

            with pe.Fori(0, 4) as i:
                for par in range(2):
                    pe.wait_ge(mod_bank_free, i * 2 + (par + 1))
                    for q in range(4):
                        pe.wait_ge(quarter_full[q], i * 32 + 16 * (par + 1))
                        for kk in range(QT):
                            k = q * QT + kk
                            for w in range(2):
                                last = mm(bank[:, 2 * par + w, :], c_rep[:, w, k, :], ring[:, q, kk, :],
                                          start=k == 0, stop=k == KT - 1)
                        last.then_inc(quarter_used, 1)
            for i in range(6):
                pe.wait_ge(h_made, i + 1)
                for g in range(4):
                    if i:
                        pe.wait_ge(tr_free, 4 * (i - 1) + g + 1)
                    for k in range(4):
                        kk = 4 * g + k
                        last = nc.tensor.transpose(bank[:, 4 + g, k * P:(k + 1) * P],
                                                   x_tile[i][:, kk * P:(kk + 1) * P], ident)
                    last.then_inc(tr_full, 1)
            pe.wait_ge(tr_free, 24)

            def full(blk):
                return 16 * (blk + 1) + 16 * min(max(blk + 1 - CONV, 0), 4)

            def block_pass(blk, s, acts, n, weights, release, signal=None, tiles=4):
                for q in range(4):
                    pe.wait_ge(quarter_full[q], full(blk))
                    for kk in range(QT):
                        k = q * QT + kk
                        for m in range(tiles):
                            if weights:
                                last = mm(bank[:, s + m, 0:n], ring[:, q, kk, m * P:(m + 1) * P], acts(k, m),
                                          start=k == 0, stop=k == KT - 1)
                            else:
                                last = mm(bank[:, s + m, :], acts(k, m), ring[:, q, kk, :],
                                          start=k == 0, stop=k == KT - 1)
                    if release:
                        last.then_inc(quarter_used, 1)
                if signal is not None:
                    last.then_inc(signal, 1)

            with pe.Fori(0, 2) as i:
                for par in range(2):
                    pe.wait_ge(set_free, i * 2 + (par + 1))
                    for q in range(4):
                        pe.wait_ge(quarter_full[q], i * 64 + (16 * CONV + 32 * (par + 1)))
                        for kk in range(QT):
                            k = q * QT + kk
                            for m in range(4):
                                last = mm(bank[:, 4 * par + m, :], ring[:, q, kk, m * P:(m + 1) * P], hT[:, k, 0:T],
                                          start=k == 0, stop=k == KT - 1)
                        last.then_inc(quarter_used, 1)
            with pe.Fori(0, 2) as i:
                for par in range(2):
                    pe.wait_ge(set_free, i * 2 + (4 + par + 1))
                    for q in range(4):
                        pe.wait_ge(quarter_full[q], i * 32 + (full(QO - 1) + 16 * (par + 1)))
                        for kk in range(QT):
                            k = q * QT + kk
                            for m in range(4):
                                last = mm(bank[:, 4 * par + m, :], ring[:, q, kk, m * P:(m + 1) * P], hT[:, k, 0:T],
                                          start=k == 0, stop=k == KT - 1)
                        last.then_inc(quarter_used, 1)
            pe.wait_ge(set_free, 9)
            pe.wait_ge(conv_step, 4 * 2 * TAPS)
            for f in range(CTILES):
                last = mm(bank[:, 0, :], mean_w, mixT[:, 8 + f, :], start=f == 0, stop=f == CTILES - 1)
            last.then_inc(pass_full, 1)
            pe.wait_ge(set_free, 10)
            pe.wait_ge(gate_wp_made, 1)
            for k in range(KT):
                mm(bank[:, 4, :], gate_wp[:, k, :], hT[:, k, 0:T], start=k == 0, stop=k == KT - 1)
                last = mm(bank[:, 5, 0:C], gate_wp[:, k, :], hT[:, k, T:L], start=k == 0, stop=k == KT - 1)
            last.then_inc(pass_full, 1)
            pe.wait_ge(set_free, 11)
            block_pass(KV, 0, lambda k, m: hT[:, k, 0:T], T, True, False, pass_full)
            pe.wait_ge(set_free, 12)
            block_pass(KV, 4, lambda k, m: hT[:, k, T:L], C, True, True)
            pe.wait_ge(set_free, 13)
            for f in range(CTILES):
                last = mm(bank[:, 0, :], mean_w, ln_sq[:, f, :], start=f == 0, stop=f == CTILES - 1)
            last.then_inc(pass_full, 1)
            pe.wait_ge(set_free, 14)
            block_pass(KV + 1, 4, lambda k, m: hT[:, k, 0:T], T, True, False, pass_full)
            pe.wait_ge(set_free, 15)
            block_pass(KV + 1, 0, lambda k, m: hT[:, k, T:L], C, True, True)
            pe.wait_ge(set_free, 16)
            pe.wait_ge(gate_dve, 7)
            for s in range(6):
                at = C + s * P if s < LT else (s - LT) * P
                nc.tensor.transpose(bank[:, 4, 64 * s:64 * s + 64], g_nat[:, at:at + P], ident[0:64, 0:64])
            for s in range(LT):
                last = nc.tensor.transpose(bank[:, 5, 64 * s:64 * s + 64], e_nat[:, s * P:(s + 1) * P],
                                           ident[0:64, 0:64])
            last.then_inc(pass_full, 1)
            for half in range(2):
                pe.wait_ge(set_free, 17 + 2 * half)
                block_pass(KV + 2 + half, 0, lambda k, m: hT[:, k, m * P:(m + 1) * P], NB, False, False, pass_full)
                pe.wait_ge(set_free, 18 + 2 * half)
                block_pass(KV + 2 + half, 4, lambda k, m: hT[:, k, T + m * P:T + (m + 1) * P], NB, False, True,
                           tiles=CT)
            pe.wait_ge(quarter_used, 4 * (KV + 4))
            pe.sem_inc(bproj_done, 1)
            pe.wait_ge(set_free, 2 + 20)
            pe.wait_ge(pick_made, 1)

            for h in range(HEADS):
                for d in range(2):
                    if h:
                        pe.wait_ge(w_made, 12 * h)
                    mm(bank[:, 2 + d, :], pick[:, HEADS * d + h, :], m_rows, start=True, stop=True)\
                        .then_inc(m_full, 1)
                for s in range(6):
                    n = 6 * h + s
                    if n >= 2:
                        pe.wait_ge(s_copied, n - 1)
                    for k in range(2):
                        last = mm(bank[:, s % 2, :], kT[:, 2 * h + k, s * P:(s + 1) * P], qT[:, 2 * h + k, :],
                                  start=k == 0, stop=k == 1)
                    last.then_inc(s_full, 1)
                for b in range(4 * h, 4 * h + 4):
                    blk = MOD2 + b
                    if b >= 2:
                        pe.wait_ge(mrow_made, b - 1)
                    for q in range(4):
                        pe.wait_ge(quarter_full[q], full(blk))
                        for kk in range(QT):
                            k = q * QT + kk
                            last = mm(bank[0:1, 6 + b % 2, :], c_silu[:, k:k + 1], ring[:, q, kk, :],
                                      start=k == 0, stop=k == KT - 1)
                        last.then_inc(quarter_used, 1)
                for j in range(LT):
                    for d in range(2):
                        n = 8 * h + 2 * j + d
                        keys = [4, 5] + [s for s in range(LT) if (s <= j if d == 0 else s >= j)]
                        if n >= 2:
                            pe.wait_ge(num_free, n - 1)
                        pe.wait_ge(p_made, 12 * (h + 1))
                        for i, s in enumerate(keys):
                            last = mm(bank[:, 4 + d, 0:HD + 1], probT[:, d, s, j * P:(j + 1) * P],
                                      v_aug[:, s, h, :], start=i == 0, stop=i == len(keys) - 1)
                        last.then_inc(num_full, 1)
            for f in range(8):
                h, e = f // 2, f % 2
                pe.wait_ge(h_normed, 4 * (h + 1))
                if f >= 4:
                    pe.wait_ge(ht_mixed, f - 3)
                for j in range(LT):
                    last = nc.tensor.transpose(bank[:, f % 4, j * P:(j + 1) * P], h_sum[:, j, h, e * P:(e + 1) * P],
                                               ident)
                last.then_inc(ht_full, 1)

            pe.wait_ge(ht_mixed, 8)
            pe.wait_ge(conv_done, 8)
            pe.wait_ge(num_free, 32)
            with pe.Fori(0, 2) as i:
                for par in range(2):
                    pe.wait_ge(wo_free, i * 2 + (par + 1))
                    for q in range(4):
                        pe.wait_ge(quarter_full[q], i * 32 + (full(WO - 1) + 16 * (par + 1)))
                        for kk in range(QT):
                            k = q * QT + kk
                            for j in range(LT):
                                last = mm(bank[:, 4 * par + j, :], mixT[:, k, j * P:(j + 1) * P],
                                          ring[:, q, kk, :], start=k == 0, stop=k == KT - 1)
                        last.then_inc(quarter_used, 1)
            pe.wait_ge(wo_free, 6)
            for i in range(LT):
                pe.wait_ge(h2_made, i + 1)
                for g in range(4):
                    if i:
                        pe.wait_ge(tr2_free, 4 * (i - 1) + g + 1)
                    for k in range(4):
                        kk = 4 * g + k
                        last = nc.tensor.transpose(bank[:, 4 + g, k * P:(k + 1) * P],
                                                   h2_tile[i % 2][:, kk * P:(kk + 1) * P], ident)
                    last.then_inc(tr2_full, 1)
            pe.wait_ge(tr2_free, 16)

            def queries(b):
                if b >= 2:
                    pe.wait_ge(score_copied, b - 1)
                block_pass(WQ + b, 4 * (b % 2), lambda k, m: h2T[:, k, :], T, True, True)

            def scores(b):
                pe.wait_ge(q_copied, b + 1)
                for m in range(4):
                    for j in range(LT):
                        last = mm(bank[:, 4 * (b % 2) + m, j * P:(j + 1) * P],
                                  query[:, b % 2, m, j * P:(j + 1) * P], keysT[:, m % 2, :], start=True, stop=True)
                last.then_inc(score_full, 1)

            queries(0)
            for b in range(1, 4):
                queries(b)
                scores(b - 1)
            scores(3)
            pe.wait_ge(slots_made, 1)
            pe.wait_ge(score_copied, 4)
            for w, src in enumerate((exp1, exp2, gate)):
                for j in range(LT):
                    last = nc.tensor.transpose(bank[:, w, j * P:(j + 1) * P],
                                               src[:, j, :, :].rearrange("p h k -> p (h k)"), ident)
                last.then_inc(slotT_full, 1)
            pe.sem_inc(onehot_used, 4)
            with pe.Fori(0, 32) as i:
                for g in range(4):
                    pe.wait_ge(onehot_made, i * 4 + (g + 1))
                    pe.wait_ge(gbank_free, i * 4 + (g + 1))
                    for s in range(4):
                        last = mm(bank[:, 4 + g, s * NK:(s + 1) * NK], onehot[:, g, s, 1, :], onehot[:, g, s, 0, :],
                                  start=True, stop=True)
                    last.then_inc(onehot_used, 1)

            def neurons(g, u_count):
                for e in range(4):
                    pe.wait_ge(u_full[e % 2], u_count + 16 * (e // 2))
                    if not (isinstance(g, int) and g == 0):
                        pe.wait_ge(a_made, g * 4 + (e - 3))
                    for k in range(KT):
                        last = mm(bank[:, e, :], u_ring[e % 2][:, k, :], h2T[:, k, :], start=k == 0,
                                  stop=k == KT - 1)
                    last.then_inc(u_used, 1)

            def sums(g, half, v_count):
                pe.wait_ge(a_made, g * 4 + 4)
                for e in range(4):
                    pe.wait_ge(v_full[4 * half + e], v_count)
                for o in range(16):
                    j, n = o // 4, o % 4
                    pe.wait_ge(o_free, g * 16 + (o + 1))
                    for e in range(4):
                        s = 4 * half + e
                        last = mm(bank[:, 4 + o % 4, :], a_ring[s][:, j * P:(j + 1) * P],
                                  v_ring[s][:, n * NB:(n + 1) * NB], start=e == 0, stop=e == 3)
                    last.then_inc(o_full, 1)

            pe.wait_ge(gbank_free, 4 + 128)
            neurons(0, 16)
            with pe.Fori(0, 15) as i:
                neurons(i * 2 + 1, i * 64 + 48)
                sums(i * 2, 0, i * 16 + 16)
                neurons(i * 2 + 2, i * 64 + 80)
                sums(i * 2 + 1, 1, i * 16 + 16)
            neurons(31, 31 * 32 + 16)
            sums(30, 0, 16 * 16)
            sums(31, 1, 16 * 16)


_INS = ['x', 'c', 'ctx', 'c_ctx', 'w_mod', 'b_mod', 'g_mix', 'g_ffn', 'w_in', 'b_gate', 'g_mhn', 'conv_w', 'conv_b',
        'cn_g', 'cn_b', 'w_out', 'w_query', 'sub_keys', 'u_emb', 'v_emb', 'g_final']


def kernel(**inputs):
    import numpy as _np
    import concourse.bacc as _bacc
    from concourse import mybir as _mybir
    from concourse.bass_utils import run_bass_kernel_spmd as _run

    laid = {name: _np.asarray(inputs[name]) for name in _INS}
    laid['sub_keys'] = laid['sub_keys'][0].transpose(2, 0, 1)
    laid['u_emb'] = laid['u_emb'][0].reshape(NK, NK, KT, P).transpose(0, 3, 2, 1).reshape(NK, P, KT * NK)

    nc = _bacc.Bacc("TRN2", target_bir_lowering=False, num_devices=1)
    arrays, args = {}, []
    for name in _INS:
        a = _np.ascontiguousarray(laid[name])
        arrays[f"in_{name}"] = a
        args.append(nc.dram_tensor(f"in_{name}", a.shape, _mybir.dt.from_np(a.dtype), kind="ExternalInput").ap())
    args.append(nc.dram_tensor("out", (1, T, D), _mybir.dt.float32, kind="ExternalOutput").ap())
    hybrid_layer(nc, *args)
    r = _run(nc, [arrays], core_ids=[0])
    return r.results[0]["out"]
```

```python
import concourse.bass as bass
from concourse import mybir
from contextlib import ExitStack

F32 = mybir.dt.float32
F32R = mybir.dt.float32r
U32 = mybir.dt.uint32
ALU = mybir.AluOpType
ACT = mybir.ActivationFunctionType
AX = mybir.AxisListType

P = 128
D = 2048
KT = D // P
T = 512
C = 256
L = T + C
LT, CT = T // P, C // P
NB = 512
QT = KT // 4
GRID_W, ROWS = 64, T // 64
EPS = 1e-6
HEADS, HD = 4, 256
MW = HEADS * HD
GATES = 4 * HEADS
GATE0 = 4 * MW
CONV0 = GATE0 + GATES
CW = D - MW
CTILES = CW // P
TAPS = 31
PADW = GRID_W + TAPS - 1
PH, NK, TOPK = 8, 128, 16
SLOTS = PH * TOPK
BIG = 1e30
NEG = -3.0e38
U0 = 16
V0 = U0 + NK
PAIRS = NK // 2
HALF = D // 2
SWEEPS = 2
CHUNK = 64
CHUNKS = T // CHUNK

MOD1, CONV, QO, KV, MOD2, WO, WQ = 0, 8, 16, 24, 28, 36, 40


def mod2_block(b):
    return CONV + 2 * b + 1 if b < 8 else MOD2 + b - 8


def hybrid_layer(nc, x, c, ctx_in, c_ctx, w_mod, b_mod, g_mix, g_ffn, w_in, b_gate, g_mhn, conv_w, conv_b,
                 cn_g, cn_b, w_out, w_query, keys_t, u_t, v_emb, g_final, out):
    mod_dram = nc.dram_tensor("mod_rows", [1, 4 * D], F32)
    gate_dram = nc.dram_tensor("gate_table", [CHUNKS, NK, NK, CHUNK], F32)
    neuron_dram = nc.dram_tensor("neurons", [NK, NK, T], F32)
    x2_dram = nc.dram_tensor("x_after_mixer", [T, D], F32)

    with ExitStack() as ctx:
        def sem(name):
            return ctx.enter_context(nc.semaphore(name))

        def region(name, words, stack=ctx):
            return stack.enter_context(nc.sbuf_tensor(name, [P, words], F32))

        ident = region("ident", P)[:, :]
        mean_w = region("mean_w", P)[:, :]
        iota = region("iota", P)[:, :]
        mask = region("mask", 2 * P)[:, :].rearrange("p (d t) -> p d t", d=2)
        stat = region("stat", 96)[:, :]
        eps_col = region("eps_col", 1)[:, :]
        one_col = region("one_col", 1)[:, :]
        keysT = region("keysT", 2 * NK)[:, :].rearrange("p (h n) -> p h n", h=2)
        den = region("den", 4)[:, :]
        soft = region("soft", 96)[:, :]
        R0 = region("ring", 8192)[:, :]

        with ExitStack() as mixer:
            R5 = region("mix", 8192, mixer)[:, :]
            R1 = region("r1", 12288, mixer)[:, :]
            R23 = region("r23", 10240, mixer)[:, :]
            R4 = region("r4", 6168, mixer)[:, :]
            R6 = region("r6", 4096, mixer)[:, :]
            conv_col = region("conv_col", CTILES * TAPS, mixer)[:, :]
            chan_col = region("chan_col", 32, mixer)[:, :]
            c_sig = region("c_sig", 32, mixer)[:, :]
            c_silu = region("c_silu", 32, mixer)[:, :]
            gate_w = region("gate_w", KT * GATES, mixer)[:, :].rearrange("p (k n) -> p k n", n=GATES)
            gate_b = region("gate_b", 1, mixer)[:, :]
            c_rep = region("c_rep", KT * 32, mixer)[:, :].rearrange("p (k m) -> p k m", m=32)
            row_buf = region("row_buf", 2 * P, mixer)[:, :].rearrange("p (b n) -> p b n", b=2)
            bias_rows = region("bias_rows", P, mixer)[0:64, :]
            m_rows = region("m_rows", T, mixer)[0:64, :]
            g_col = region("g_col", 6 * 64, mixer)[:, :].rearrange("p (s r) -> p s r", r=64)
            e_col = region("e_col", 4 * 64, mixer)[:, :].rearrange("p (s r) -> p s r", r=64)
        R2, R3 = R23[:, 0:4096], R23[:, 4096:10240]
        with ExitStack() as search:
            h2_hi = region("h2_hi", 8192, search)[:, :].rearrange("p (k t) -> p k t", t=T)
            B1 = region("b1", 12288, search)[:, :]
            h2_lo = region("h2_lo", 8192, search)[:, :].rearrange("p (k t) -> p k t", t=T)
            split = region("split", 8192, search)[:, :].rearrange("p (s h w) -> p s h w", s=2, h=2)
            B4 = region("b4", 5632, search)[:, :]
            neuron_out = region("neuron_out", 2 * T, search)[:, :].rearrange("p (s t) -> p s t", s=2)
        with ExitStack() as sweep:
            x3 = region("x3", 8192, sweep)[:, :].rearrange("p (j n) -> p j n", j=LT)
            weigh = region("weigh", 8192, sweep)[:, :].rearrange("p (s w n) -> p s w n", s=4, w=2)
            a_split = region("a_split", 4096, sweep)[:, :].rearrange("p (s h w) -> p s h w", s=2, h=2)
            C3 = region("c3", 8192, sweep)[:, :]

        ring = R0.rearrange("p (q k n) -> p q k n", q=4, n=NB)
        hT = R1.rearrange("p (k t) -> p k t", t=L)
        x_tile = [R5[:, i * D:(i + 1) * D] for i in range(4)] + [R4[:, i * D:(i + 1) * D] for i in range(2)]
        mod_x, mod_c = R2, R3[:, 0:2 * D]
        g_mix_row = R4[:, 2 * D:3 * D]
        square_out = R1[:, 2048:4096]
        row_pick = R6[:, 0:8 * P].rearrange("p (r m) -> p r m", m=P)
        vec_rows = R1[0:32, 0:P]
        chan_rows = R1[0:32, P:2 * P]
        conv_rows = R1[0:TAPS, 1024:2048]
        gate_wp = R3[:, 4096:6144].rearrange("p (k m) -> p k m", m=P)
        u_pad = R4[:, 0:CTILES * ROWS * PADW].rearrange("p (c r w) -> p c r w", r=ROWS, w=PADW)
        mixT = R5.rearrange("p (f t) -> p f t", t=T)
        ln_sq = R6.rearrange("p (f t) -> p f t", t=T)
        qT = R2.rearrange("p (f t) -> p f t", t=T)
        kT = R3.rearrange("p (f t) -> p f t", t=L)
        v_aug = R4.rearrange("p (s h e) -> p s h e", s=6, h=HEADS)
        grow = [R4[0:64, i * L:(i + 1) * L] for i in range(6)]
        g_nat = R4[0:64, 6 * L:7 * L]
        e_nat = R4[0:64, 7 * L:7 * L + T]
        scoreT = R1[:, 0:3072].rearrange("p (s t) -> p s t", t=T)
        probT = R1[:, 3072:9216].rearrange("p (d s t) -> p d s t", d=2, t=T)
        diag_arg = R1[:, 9216:10240].rearrange("p (d s t) -> p d s t", d=2, t=P)
        pick = R1[0:64, 10240:11264].rearrange("p (r m) -> p r m", m=P)
        h_sum = R6.rearrange("p (j h e) -> p j h e", j=LT, h=HEADS)
        x2 = R1[:, 0:8192].rearrange("p (j n) -> p j n", j=LT)
        ga1_row, sc2_row, sh2_row = (R4[:, i * D:(i + 1) * D] for i in range(3))
        g_ffn_row = R1[:, 8192:10240]
        out_part = R6[:, 0:2048].rearrange("p (j n) -> p j n", j=LT)
        h2_tile = [R6[:, 0:D], R6[:, D:2 * D]]
        query = B1[:, 8192:12288].rearrange("p (b m t) -> p b m t", b=2, m=4)
        score = B1[:, 0:8192].rearrange("p (j s n) -> p j s n", j=LT, n=NK)
        top_val = B4[:, 0:1024].rearrange("p (j s k) -> p j s k", j=LT, k=TOPK)
        top_idx = B4[:, 1024:2048].bitcast(U32).rearrange("p (j s k) -> p j s k", j=LT, k=TOPK)
        best = B4[:, 2048:2560].rearrange("p (j h k) -> p j h k", j=LT, k=TOPK)
        pos = B4[:, 2560:3072].bitcast(U32).rearrange("p (j h k) -> p j h k", j=LT, k=TOPK)
        exp1 = B4[:, 3072:3584].rearrange("p (j h k) -> p j h k", j=LT, k=TOPK)
        exp2 = B4[:, 3584:4096].rearrange("p (j h k) -> p j h k", j=LT, k=TOPK)
        gate = B4[:, 4096:4608].rearrange("p (j h k) -> p j h k", j=LT, k=TOPK)
        pos_a = B4[:, 4608:5120].bitcast(U32).rearrange("p (j h k) -> p j h k", j=LT, k=TOPK)
        pos_b = B4[:, 5120:5632].bitcast(U32).rearrange("p (j h k) -> p j h k", j=LT, k=TOPK)
        slotT = B4[:, 0:1536].rearrange("p (w t) -> p w t", t=T)

        def pair_sums(j, b):
            return B1[:, j * D + b * 4 * NK:j * D + (b + 1) * 4 * NK].rearrange("p (h a c) -> p h a c", h=2, c=TOPK)

        onehot = B1[:, 8192:12288].rearrange("p (g s w n) -> p g s w n", g=4, s=4, w=2)
        stage = B1[:, 0:8192].rearrange("p (i t) -> p i t", t=CHUNK)
        ga2_row, g_final_row = C3[:, 0:D], C3[:, D:2 * D]
        gated = C3[:, 2 * D:4 * D].rearrange("p (b n) -> p b n", n=NB)

        bank = ctx.enter_context(nc.psum_tensor("bank", [P, 8, 512], F32))

        ssq, rms, rstd = stat[:, 0:6], stat[:, 6:12], stat[:, 12:18]
        hssq, hrms, hrstd = stat[:, 18:34], stat[:, 34:50], stat[:, 50:66]
        ssq2, rms2, rstd2 = stat[:, 66:70], stat[:, 70:74], stat[:, 74:78]
        ssq3, rms3, rstd3 = stat[:, 78:82], stat[:, 82:86], stat[:, 86:90]

        consts_made = sem("consts_made")
        rows_loaded = sem("rows_loaded")
        gate_b_loaded = sem("gate_b_loaded")
        mod_bias_loaded = sem("mod_bias_loaded")
        x_loaded = [sem(f"x_loaded{i}") for i in range(6)]
        quarter_full = [sem(f"quarter_full{q}") for q in range(4)]
        quarter_used = sem("quarter_used")
        setup_cols = sem("setup_cols")
        csig_made = sem("csig_made")
        dve_a = sem("dve_a")
        crep_made = sem("crep_made")
        x_squared = sem("x_squared")
        x_rms = sem("x_rms")
        mod_bank_free = sem("mod_bank_free")
        h_made = sem("h_made")
        tr_full = sem("tr_full")
        tr_free = sem("tr_free")
        set_free = sem("set_free")
        upad_clear = sem("upad_clear")
        glu_done = sem("glu_done")
        conv_step = sem("conv_step")
        pass_full = sem("pass_full")
        ln_sub = sem("ln_sub")
        ln_std = sem("ln_std")
        ln_rstd = sem("ln_rstd")
        ln_scaled = sem("ln_scaled")
        conv_done = sem("conv_done")
        gate_wp_made = sem("gate_wp_made")
        gate_act = sem("gate_act")
        gate_dve = sem("gate_dve")
        v_ones = sem("v_ones")
        bproj_done = sem("bproj_done")
        pick_made = sem("pick_made")
        m_full = sem("m_full")
        s_full = sem("s_full")
        s_copied = sem("s_copied")
        diag_made = sem("diag_made")
        w_made = sem("w_made")
        p_made = sem("p_made")
        num_full = sem("num_full")
        num_step = sem("num_step")
        num_free = sem("num_free")
        row_copied = sem("row_copied")
        mod_spread = sem("mod_spread")
        mrow_made = sem("mrow_made")
        mrow_stored = [sem(f"mrow_stored{b}") for b in range(2)]
        h_summed = sem("h_summed")
        h_rms = sem("h_rms")
        h_normed = sem("h_normed")
        ht_full = sem("ht_full")
        ht_mixed = sem("ht_mixed")
        x2_loaded = sem("x2_loaded")
        ga1_loaded = sem("ga1_loaded")
        ffn_rows_loaded = sem("ffn_rows_loaded")
        wo_step = sem("wo_step")
        wo_free = sem("wo_free")
        x2_squared = sem("x2_squared")
        x2_rms = sem("x2_rms")
        a2_made = sem("a2_made")
        h2_step = sem("h2_step")
        h2_made = sem("h2_made")
        tr2_full = sem("tr2_full")
        tr2_hi = sem("tr2_hi")
        tr2_free = sem("tr2_free")
        x2_stored = sem("x2_stored")
        hi_made = sem("hi_made")
        split_made = sem("split_made")
        split_used = sem("split_used")
        q_copied = sem("q_copied")
        score_full = sem("score_full")
        score_copied = sem("score_copied")
        topk = sem("topk")
        soft_in = sem("soft_in")
        soft_exp = sem("soft_exp")
        slots_made = sem("slots_made")
        slotT_full = sem("slotT_full")
        slotT_made = sem("slotT_made")
        onehot_made = sem("onehot_made")
        onehot_used = sem("onehot_used")
        gbank_free = sem("gbank_free")
        table_stored = sem("table_stored")
        gelu_made = sem("gelu_made")
        neuron_stored = [sem(f"neuron_stored{b}") for b in range(2)]
        weigh_full = [sem(f"weigh_full{b}") for b in range(4)]
        weighed = sem("weighed")
        a_hi_made = sem("a_hi_made")
        a_split_made = sem("a_split_made")
        sum_free = sem("sum_free")
        merge_step = sem("merge_step")
        last_rows = sem("last_rows")
        y_step = sem("y_step")
        y_squared = sem("y_squared")
        y_rms = sem("y_rms")
        y_made = sem("y_made")
        out_stored = sem("out_stored")

        def glu_of(j, half):
            at = (2 * (j % 2) + half) * 2 * T
            return R6[:, at:at + 2 * T].rearrange("p (c t) -> p c t", c=2)

        block = ctx.enter_context(nc.Block())

        @block.sync
        def _(sp):
            def quarter(blk, q, src):
                if not (isinstance(blk, int) and blk == 0):
                    sp.wait_ge(quarter_used, blk * 4 + (q - 3))
                sp.dma_start(ring[:, q, :, :], src).then_inc(quarter_full[q], 16)

            def rows(w, q):
                return w[0, q * QT * P:(q + 1) * QT * P, :]

            def cols(w, q, at):
                return rows(w, q)[:, bass.ds(at, NB)].rearrange("(k p) n -> p k n", p=P)

            for q in range(4):
                quarter(0, q, cols(w_mod, q, 0))
            with sp.Fori(1, 8) as b:
                for q in range(4):
                    quarter(b, q, cols(w_mod, q, b * NB))
            def mod2(b):
                for q in range(4):
                    quarter(mod2_block(b), q, cols(w_mod, q, 2 * D + b * NB))

            for j in range(4):
                for q in range(4):
                    at = CONV0 + j * 256
                    sp.wait_ge(quarter_used, (CONV + 2 * j) * 4 + q - 3)
                    for half in range(2):
                        src = rows(w_in, q)[:, at + half * CW:at + half * CW + 256]
                        sp.dma_start(ring[:, q, :, half * 256:half * 256 + 256],
                                     src.rearrange("(k p) n -> p k n", p=P)).then_inc(quarter_full[q], 8 * 2)
                mod2(j)
            for n, at in enumerate((0, NB, 3 * MW, 3 * MW + NB)):
                for q in range(4):
                    quarter(QO + 2 * n, q, cols(w_in, q, at))
                mod2(4 + n)
            for n, at in enumerate((MW, MW + NB, 2 * MW, 2 * MW + NB)):
                for q in range(4):
                    quarter(KV + n, q, cols(w_in, q, at))
            for b in range(8, 16):
                mod2(b)
            for b in range(4):
                for q in range(4):
                    quarter(WO + b, q, cols(w_out, q, b * NB))

            for r in range(U0):
                b, q = r // 4, r % 4
                if b == 0:
                    quarter(WQ, q, cols(w_query, q, 0))
                else:
                    sp.wait_ge(split_made, r - 3)
                    sp.dma_start(ring[:, q, :, :], cols(w_query, q, b * NB)).then_inc(quarter_full[q], 16)
            with sp.Fori(0, NK // 4) as i:
                for q in range(4):
                    sp.wait_ge(split_made, i * 4 + (U0 + q - 3))
                    sp.dma_start(ring[:, q, :, :].rearrange("p k n -> p (k n)"),
                                 u_t[bass.ds(i * 4 + q, 1), :, :].rearrange("a p n -> p (a n)"))\
                      .then_inc(quarter_full[q], 16)

            def v_load(count, pair, q, half):
                sp.wait_ge(split_made, count + (q - 3))
                src = v_emb[0, bass.ds(pair * (2 * P), 2 * P), half * HALF:(half + 1) * HALF]
                sp.dma_start(ring[:, q, :, :].rearrange("p k n -> p (k n)").rearrange("p (a n) -> p a n", a=2),
                             src.rearrange("(a p) n -> p a n", p=P)).then_inc(quarter_full[q], 16)

            def weigh_load(pair, q):
                sp.dma_start(weigh[:, q, 0, :].rearrange("p (a t) -> p a t", a=2),
                             neuron_dram[bass.ds(pair * 2, 2), :, :].rearrange("a p t -> p a t"))\
                  .then_inc(weigh_full[q], 16)
                sp.dma_start(weigh[:, q, 1, :].rearrange("p (c m) -> p c m", c=CHUNKS),
                             gate_dram[:, :, bass.ds(pair * 2, 2), :].rearrange("c p a t -> p c (a t)"))\
                  .then_inc(weigh_full[q], 16)

            sp.wait_ge(table_stored, 16 + 16 * CHUNKS)
            for b in range(2):
                sp.wait_ge(neuron_stored[b], 16 * (NK // 2 - 4))
            for q in range(4):
                v_load(V0, q, q, 0)
                weigh_load(q, q)
            for b in range(2):
                sp.wait_ge(neuron_stored[b], 16 * (NK // 2))
            with sp.Fori(1, PAIRS // 4) as i:
                for q in range(4):
                    v_load(i * 4 + V0, i * 4 + q, q, 0)
                    sp.wait_ge(a_split_made, i * 4 + (q - 3))
                    weigh_load(i * 4 + q, q)
            with sp.Fori(0, PAIRS // 4) as i:
                for q in range(4):
                    v_load(i * 4 + (V0 + PAIRS), i * 4 + q, q, 1)
                    sp.wait_ge(a_split_made, i * 4 + (PAIRS + q - 3))
                    weigh_load(i * 4 + q, q)
            for j in range(LT):
                sp.wait_ge(y_made, j + 1)
                sp.dma_start(out[0, j * P:(j + 1) * P, :], x3[:, j, :]).then_inc(out_stored, 16)
            sp.wait_ge(out_stored, 16 * LT)

        @block.gpsimd
        def _(pool):
            nc.gpsimd.memset(ident, 0.0).then_inc(consts_made, 1)
            nc.gpsimd.memset(mask, 0.0).then_inc(consts_made, 1)
            nc.gpsimd.memset(gate_b, 0.0).then_inc(consts_made, 1)
            nc.gpsimd.memset(mean_w, 1.0 / CW)
            nc.gpsimd.memset(eps_col, EPS)
            nc.gpsimd.memset(one_col, 1.0)
            nc.gpsimd.iota(iota, pattern=[[1, P]], base=0, channel_multiplier=0,
                           allow_small_or_imprecise_dtypes=True).then_inc(consts_made, 1)
            pool.wait_ge(consts_made, 4)
            nc.gpsimd.affine_select(out=ident, in_=ident, compare_op=ALU.not_equal, fill=1.0, base=0,
                                    pattern=[[-1, P]], channel_multiplier=1).then_inc(consts_made, 1)
            nc.gpsimd.affine_select(out=mask[:, 0, :], in_=mask[:, 0, :], compare_op=ALU.is_ge, fill=BIG, base=0,
                                    pattern=[[1, P]], channel_multiplier=-1).then_inc(consts_made, 1)
            nc.gpsimd.affine_select(out=mask[:, 1, :], in_=mask[:, 1, :], compare_op=ALU.is_ge, fill=BIG, base=0,
                                    pattern=[[-1, P]], channel_multiplier=1).then_inc(consts_made, 1)
            for g, first in enumerate((0, 8, 4, 12)):
                pool.dma_start(gate_b[32 * g:32 * g + 4, :],
                               b_gate[0, first:first + 4].unsqueeze(1)).then_inc(gate_b_loaded, 16)

            pool.wait_ge(h_made, 6)
            pool.wait_ge(tr_full, 24)
            nc.gpsimd.memset(R4[:, 0:CTILES * ROWS * PADW], 0.0).then_inc(upad_clear, 1)
            pool.wait_ge(upad_clear, 1)
            for j in range(4):
                pool.wait_ge(set_free, 2 + j + 1)
                for cc in range(2):
                    last = nc.gpsimd.tensor_tensor(
                        out=u_pad[:, 2 * j + cc, :, TAPS // 2:TAPS // 2 + GRID_W],
                        in0=glu_of(j, 0)[:, cc, :].rearrange("p (r w) -> p r w", w=GRID_W),
                        in1=glu_of(j, 1)[:, cc, :].rearrange("p (r w) -> p r w", w=GRID_W), op=ALU.mult)
                last.then_inc(glu_done, 1)

            pool.wait_ge(mrow_stored[0], 16 * 8)
            pool.wait_ge(mrow_stored[1], 16 * 8)
            pool.wait_ge(num_full, 8 * LT)
            for k, row in enumerate((ga1_row, sh2_row, sc2_row)):
                pool.dma_start(row, mod_dram[0, k * D:(k + 1) * D].partition_broadcast(P))\
                    .then_inc(ga1_loaded if k == 0 else ffn_rows_loaded, 16)
            for j in range(LT):
                pool.dma_start(x2[:, j, :], x[0, j * P:(j + 1) * P, :]).then_inc(x2_loaded, 16)
            pool.wait_ge(h_summed, 16)
            pool.dma_start(g_ffn_row, g_ffn[0, :].partition_broadcast(P)).then_inc(ffn_rows_loaded, 16)
            for j in range(LT):
                pool.wait_ge(wo_step, 4 * 8)
                pool.dma_start(x2_dram[j * P:(j + 1) * P, :], x2[:, j, :]).then_inc(x2_stored, 16)

            with pool.Fori(0, (V0 + SWEEPS * PAIRS) // 4) as i:
                for q in range(4):
                    pool.wait_ge(hi_made, i * 4 + (q + 1))
                    nc.gpsimd.tensor_tensor(split[:, q % 2, 1, :].bitcast(F32R),
                                            ring[:, q, :, :].rearrange("p k n -> p (k n)"), split[:, q % 2, 0, :],
                                            op=ALU.subtract).then_inc(split_made, 1)

        @block.scalar
        def _(act):
            act.dma_start(vec_rows[0:16, :], c[0, :].rearrange("(k p) -> k p", p=P)).then_inc(rows_loaded, 16)
            act.dma_start(vec_rows[16:32, :], c_ctx[:].rearrange("(k p) -> k p", p=P)).then_inc(rows_loaded, 16)
            for n, src in enumerate((cn_g, cn_b, conv_b, g_mhn)):
                act.dma_start(chan_rows[8 * n:8 * n + 8, :],
                              src[0, :].rearrange("(k p) -> k p", p=P)).then_inc(rows_loaded, 16)
            act.dma_start(conv_rows, conv_w[0, :, :]).then_inc(rows_loaded, 16)
            act.dma_start(gate_w, w_in[0, :, GATE0:CONV0].rearrange("(k p) n -> p k n", p=P))\
               .then_inc(rows_loaded, 16)
            act.dma_start(bias_rows, b_mod[0, 2 * D:].rearrange("(r n) -> r n", n=P)).then_inc(rows_loaded, 16)
            act.dma_start(keysT, keys_t[:, :, :]).then_inc(rows_loaded, 16)
            act.dma_start(mod_x, b_mod[0, 0:2 * D].partition_broadcast(P)).then_inc(mod_bias_loaded, 16)
            act.dma_start(mod_c, b_mod[0, 0:2 * D].partition_broadcast(P)).then_inc(mod_bias_loaded, 16)
            act.dma_start(g_mix_row, g_mix[0, :].partition_broadcast(P)).then_inc(mod_bias_loaded, 16)
            for i in range(6):
                src = x[0, i * P:(i + 1) * P, :] if i < LT else ctx_in[0, (i - LT) * P:(i - LT + 1) * P, :]
                act.dma_start(x_tile[i], src).then_inc(x_loaded[i], 16)
            act.sem_inc(set_free, 2)

            act.wait_ge(setup_cols, 1)
            nc.scalar.activation(c_sig, bank[:, 0, 0:32], ACT.Sigmoid).then_inc(csig_made, 1)
            for i in range(6):
                act.wait_ge(x_loaded[i], 16)
                if i:
                    act.wait_ge(x_squared, i)
                nc.scalar.activation(square_out, x_tile[i], ACT.Square,
                                     accum_out=ssq[:, i:i + 1]).then_inc(x_squared, 1)
            act.wait_ge(x_squared, 6)
            act.wait_ge(consts_made, 7)
            nc.scalar.activation(rms, ssq, ACT.Sqrt, bias=eps_col, scale=1.0 / D).then_inc(x_rms, 1)
            with act.Fori(0, 4) as i:
                for par in range(2):
                    act.wait_ge(quarter_used, i * 8 + 4 * (par + 1))
                    nc.scalar.activation(row_buf[:, par, :], bank[:, 4 + par, 0:P], ACT.Copy).then_inc(row_copied, 1)
            for i in range(6):
                for g in range(4):
                    act.wait_ge(tr_full, 4 * i + g + 1)
                    nc.scalar.activation(hT[:, 4 * g:4 * g + 4, i * P:(i + 1) * P],
                                         bank[:, 4 + g, :].rearrange("p (k t) -> p k t", k=4), ACT.Copy)\
                        .then_inc(tr_free, 1)

            def copy_row(b, n):
                act.wait_ge(quarter_used, 4 * (mod2_block(b) + 1))
                if b >= 2:
                    act.wait_ge(mrow_stored[b % 2], 16 * (b // 2))
                nc.scalar.activation(row_buf[:, b % 2, :], bank[:, n, 0:P], ACT.Copy).then_inc(mrow_made, 1)
                act.wait_ge(mrow_made, b + 1)
                act.dma_start(mod_dram[0, b * NB:(b + 1) * NB].rearrange("(j n) -> j n", n=P),
                              row_buf[0:P:32, b % 2, :]).then_inc(mrow_stored[b % 2], 16)

            for j in range(4):
                s = 4 * (j % 2)
                act.wait_ge(quarter_used, 4 * (CONV + 2 * j + 1))
                if j >= 2:
                    act.wait_ge(glu_done, j - 1)
                nc.scalar.activation(glu_of(j, 0), bank[:, s:s + 2, :], ACT.Copy)
                nc.scalar.activation(glu_of(j, 1), bank[:, s + 2:s + 4, :], ACT.Sigmoid).then_inc(set_free, 1)
                copy_row(j, 4 - s)
            for j in range(2):
                act.wait_ge(quarter_used, 4 * (QO + 2 * j + 1))
                s = 4 * (j % 2)
                nc.scalar.activation(qT[:, 4 * j:4 * j + 4, :], bank[:, s:s + 4, :], ACT.Copy,
                                     scale=HD ** -0.5).then_inc(set_free, 1)
                copy_row(4 + j, 4 - s)
            for j in range(2):
                act.wait_ge(quarter_used, 4 * (QO + 2 * (2 + j) + 1))
                s = 4 * (j % 2)
                nc.scalar.activation(mixT[:, 4 * j:4 * j + 4, :], bank[:, s:s + 4, :], ACT.Sigmoid)\
                    .then_inc(set_free, 1)
                copy_row(6 + j, 4 - s)
            act.wait_ge(ln_sub, 8)
            nc.scalar.activation(ln_sq, mixT[:, 8:16, :], ACT.Square).then_inc(set_free, 1)
            act.wait_ge(pass_full, 2)
            act.wait_ge(gate_b_loaded, 64)
            for kind in range(2):
                for d in range(2):
                    src = 64 * kind + 32 * d
                    dst = grow[kind][32 * d:32 * d + 32, :]
                    dst_c, dst_x = dst[:, 0:C], dst[:, C:L]
                    if d:
                        dst_c, dst_x = dst_c[:, ::-1], dst_x[:, ::-1]
                    nc.scalar.activation(dst_x, bank[src:src + 32, 4, 0:T], ACT.Identity,
                                         bias=gate_b[src:src + 32, :])
                    last = nc.scalar.activation(dst_c, bank[src:src + 32, 5, 0:C], ACT.Identity,
                                                bias=gate_b[src:src + 32, :])
            last.then_inc(set_free, 1)
            act.wait_ge(set_free, 2 + 10)
            nc.scalar.activation(grow[2], grow[1], ACT.Abs).then_inc(gate_act, 1)
            act.wait_ge(gate_act, 1)
            nc.scalar.activation(grow[3], grow[2], ACT.Exp, scale=-1.0).then_inc(gate_act, 1)
            act.wait_ge(gate_act, 2)
            nc.scalar.activation(grow[4], grow[3], ACT.Ln, bias=one_col[0:64, :]).then_inc(gate_act, 1)
            act.wait_ge(pass_full, 3)
            nc.scalar.activation(kT[:, 0:4, 0:T], bank[:, 0:4, :], ACT.Copy).then_inc(set_free, 1)
            act.wait_ge(quarter_used, 4 * (KV + 1))
            nc.scalar.activation(kT[:, 0:4, T:L], bank[:, 4:8, 0:C], ACT.Copy).then_inc(set_free, 1)
            act.wait_ge(gate_dve, 5)
            nc.scalar.activation(grow[1], grow[2], ACT.Exp, scale=-1.0).then_inc(gate_act, 1)
            act.wait_ge(pass_full, 4)
            act.wait_ge(set_free, 2 + 12)
            nc.scalar.activation(glu_of(0, 0)[:, 0, :], bank[:, 0, :], ACT.Sqrt, bias=eps_col).then_inc(set_free, 1)
            act.wait_ge(pass_full, 5)
            nc.scalar.activation(kT[:, 4:8, 0:T], bank[:, 4:8, :], ACT.Copy).then_inc(set_free, 1)
            act.wait_ge(quarter_used, 4 * (KV + 2))
            nc.scalar.activation(kT[:, 4:8, T:L], bank[:, 0:4, 0:C], ACT.Copy).then_inc(set_free, 1)
            act.wait_ge(ln_scaled, 8)
            for f in range(CTILES):
                nc.scalar.activation(mixT[:, 8 + f, :], mixT[:, 8 + f, :], ACT.Silu,
                                     bias=chan_col[:, 8 + f:9 + f], scale=chan_col[:, f:f + 1])\
                    .then_inc(conv_done, 1)
            act.wait_ge(pass_full, 6)
            nc.scalar.activation(g_col, bank[:, 4, 0:384].rearrange("p (s r) -> p s r", r=64), ACT.Copy)
            nc.scalar.activation(e_col, bank[:, 5, 0:256].rearrange("p (s r) -> p s r", r=64), ACT.Copy)\
                .then_inc(set_free, 1)
            act.wait_ge(v_ones, 1)
            for half in range(2):
                act.wait_ge(pass_full, 7 + half)
                for j in range(LT):
                    last = nc.scalar.activation(v_aug[:, j, 2 * half:2 * half + 2, 0:HD],
                                                bank[:, j, :].rearrange("p (h e) -> p h e", h=2), ACT.Copy)
                last.then_inc(set_free, 1)
                act.wait_ge(quarter_used, 4 * (KV + 2 + half + 1))
                for j in range(CT):
                    last = nc.scalar.activation(v_aug[:, LT + j, 2 * half:2 * half + 2, 0:HD],
                                                bank[:, 4 + j, :].rearrange("p (h e) -> p h e", h=2), ACT.Copy)
                last.then_inc(set_free, 1)

            for h in range(HEADS):
                for s in range(6):
                    act.wait_ge(s_full, 6 * h + s + 1)
                    if h and s == 0:
                        act.wait_ge(p_made, 12 * h)
                    nc.scalar.activation(scoreT[:, s, :], bank[:, s % 2, :], ACT.Copy).then_inc(s_copied, 1)
                for d in range(2):
                    act.wait_ge(diag_made, 8 * h + 4 * (d + 1))
                    if h:
                        act.wait_ge(num_full, 8 * h)
                    r = 32 * d + h
                    for s in range(6):
                        g = g_col[:, s, r:r + 1]
                        if s >= LT:
                            last = nc.scalar.activation(probT[:, d, s, :], bank[:, 2 + d, :], ACT.Exp, bias=g,
                                                        scale=-1.0)
                        else:
                            lo, hi = ((s + 1) * P, T) if d == 0 else (0, s * P)
                            if hi > lo:
                                nc.scalar.activation(probT[:, d, s, lo:hi], bank[:, 2 + d, lo:hi], ACT.Exp, bias=g,
                                                     scale=-1.0)
                            last = nc.scalar.activation(probT[:, d, s, s * P:(s + 1) * P], diag_arg[:, d, s, :],
                                                        ACT.Exp, scale=-1.0)
                        last.then_inc(w_made, 1)
                for b in (8 + 2 * h, 9 + 2 * h):
                    copy_row(b, 6 + b % 2)
            act.wait_ge(h_summed, 16)
            nc.scalar.activation(hrms, hssq, ACT.Sqrt, bias=eps_col, scale=1.0 / HD).then_inc(h_rms, 1)

            for j in range(LT):
                act.wait_ge(wo_step, 4 * 8)
                if j:
                    act.wait_ge(x2_squared, j)
                nc.scalar.activation(bank[:, 0:4, :], x2[:, j, :].rearrange("p (b n) -> p b n", b=4), ACT.Square,
                                     accum_out=ssq2[:, j:j + 1]).then_inc(x2_squared, 1)
            act.wait_ge(x2_squared, LT)
            nc.scalar.activation(rms2, ssq2, ACT.Sqrt, bias=eps_col, scale=1.0 / D).then_inc(x2_rms, 1)
            for i in range(LT):
                for g in range(4):
                    act.wait_ge(tr2_full, 4 * i + g + 1)
                    nc.scalar.activation(h2_hi[:, 4 * g:4 * g + 4, i * P:(i + 1) * P].bitcast(F32R),
                                         bank[:, 4 + g, :].rearrange("p (k t) -> p k t", k=4), ACT.Copy)\
                        .then_inc(tr2_hi, 1)

            def hi(count, q):
                act.wait_ge(quarter_full[q], count)
                nc.scalar.activation(split[:, q % 2, 0, :].bitcast(F32R),
                                     ring[:, q, :, :].rearrange("p k n -> p (k n)"), ACT.Copy).then_inc(hi_made, 1)

            landed = 16 * WQ + 64
            def copy_query(b):
                s = 4 * (b % 2)
                nc.scalar.activation(query[:, b % 2, :, :], bank[:, s:s + 4, :], ACT.Copy).then_inc(q_copied, 1)

            def copy_scores(b):
                act.wait_ge(score_full, b + 1)
                s = 4 * (b % 2)
                for m in range(4):
                    last = nc.scalar.activation(score[:, :, 4 * b + m, :],
                                                bank[:, s + m, :].rearrange("p (j n) -> p j n", j=LT), ACT.Copy)
                last.then_inc(score_copied, 1)

            act.wait_ge(h2_made, LT)
            hi(landed + 16, 0)
            hi(landed + 16, 1)
            for r in range(U0):
                act.wait_ge(split_used, r + 1)
                hi(landed + 16 * ((r + 2) // 4 + 1), (r + 2) % 4)
                if r % 4 == 3:
                    if r == 3:
                        act.wait_ge(x2_stored, 16 * LT)
                        act.wait_ge(tr2_free, 16)
                    copy_query(r // 4)
                if r % 4 == 1 and r > 4:
                    copy_scores(r // 4 - 1)

            def neurons(blk, q, store=True, wait=True):
                act.wait_ge(split_used, blk * 4 + (U0 + q + 1))
                hi(blk * 16 + (landed + 16 * (U0 // 4 + (q + 2) // 4 + 1)), (q + 2) % 4)
                if store:
                    store_neurons(blk * 4 + (q - 1), (q + 1) % 2)
                if wait:
                    act.wait_ge(neuron_stored[q % 2], blk * 32 + (16 * (q // 2)))
                nc.scalar.activation(neuron_out[:, q % 2, :], bank[:, q, :], ACT.Gelu).then_inc(gelu_made, 1)

            def store_neurons(n, s):
                act.wait_ge(gelu_made, n + 1)
                act.dma_start(neuron_dram[bass.ds(n, 1), :, :].rearrange("a p t -> p (a t)"), neuron_out[:, s, :])\
                   .then_inc(neuron_stored[s], 16)

            def stage_group(g, n, at):
                act.wait_ge(onehot_used, n)
                nc.scalar.activation(stage[:, :, at:at + 4].rearrange("p i t -> p t i"),
                                     bank[:, 4 + g, :].rearrange("p (t i) -> p t i", t=4), ACT.Copy)\
                    .then_inc(gbank_free, 1)

            for q in range(4):
                neurons(0, q, q > 0, q > 1)
                if q == 1:
                    copy_scores(3)
            with act.Fori(1, 5) as i:
                for q in range(4):
                    neurons(i, q)
            act.wait_ge(soft_in, 1)
            nc.scalar.activation(gate, gate, ACT.Exp).then_inc(soft_exp, 1)
            for q in range(4):
                neurons(5, q)
            for w in range(3):
                act.wait_ge(slotT_full, w + 1)
                nc.scalar.activation(slotT[:, w, :], bank[:, 4 + w, :], ACT.Copy).then_inc(slotT_made, 1)
            act.sem_inc(gbank_free, 4)
            act.sem_inc(table_stored, 16)
            with act.Fori(0, CHUNKS) as chunk:
                for q in range(4):
                    neurons(chunk * 3 + 6, q)
                act.wait_ge(table_stored, chunk * 16 + 16)
                for n in range(8):
                    neurons(chunk * 3 + (7 + n // 4), n % 4)
                    for g in range(2):
                        stage_group((2 * n + g) % 4, chunk * 16 + (4 + 2 * n + g + 1), 4 * (2 * n + g))
                act.wait_ge(gbank_free, chunk * 16 + (4 + 16))
                act.dma_start(gate_dram[bass.ds(chunk, 1), :, :, :].rearrange("a p i t -> p (a i t)"),
                              stage.rearrange("p i t -> p (i t)")).then_inc(table_stored, 16)
            with act.Fori(30, 32) as i:
                for q in range(4):
                    neurons(i, q)
            store_neurons(NK - 1, 1)

            def a_hi(q, n):
                act.wait_ge(weighed, n)
                nc.scalar.activation(a_split[:, q % 2, 0, :].bitcast(F32R), weigh[:, q, 0, :], ACT.Copy)\
                    .then_inc(a_hi_made, 1)

            def v_hi(blk, q):
                hi(blk * 16 + (landed + 16 * (V0 // 4 + (q + 2) // 4 + 1)), (q + 2) % 4)

            for q in range(2):
                a_hi(q, q + 1)
            for q in range(4):
                act.wait_ge(split_used, V0 + q + 1)
                v_hi(0, q)
                a_hi((q + 2) % 4, q + 3)
                if q == 0:
                    for j in range(LT):
                        act.dma_start(x3[:, j, :], x2_dram[j * P:(j + 1) * P, :]).then_inc(last_rows, 16)
                    act.dma_start(ga2_row, mod_dram[0, 3 * D:4 * D].partition_broadcast(P)).then_inc(last_rows, 16)
                    act.dma_start(g_final_row, g_final[:].partition_broadcast(P)).then_inc(last_rows, 16)
            with act.Fori(1, SWEEPS * PAIRS // 4 - 1) as i:
                for q in range(4):
                    act.wait_ge(split_used, i * 4 + (V0 + q + 1))
                    v_hi(i, q)
                    a_hi((q + 2) % 4, i * 4 + (q + 3))
            for q in range(2):
                n = SWEEPS * PAIRS - 4 + q
                act.wait_ge(split_used, V0 + n + 1)
                v_hi(SWEEPS * PAIRS // 4 - 1, q)
                a_hi(q + 2, n + 3)
            for j in range(LT):
                act.wait_ge(merge_step, 32)
                if j:
                    act.wait_ge(y_squared, j)
                nc.scalar.activation(bank[:, 0:4, :], x3[:, j, :].rearrange("p (b n) -> p b n", b=4), ACT.Square,
                                     accum_out=ssq3[:, j:j + 1]).then_inc(y_squared, 1)
            act.wait_ge(y_squared, LT)
            nc.scalar.activation(rms3, ssq3, ACT.Sqrt, bias=eps_col, scale=1.0 / D).then_inc(y_rms, 1)

        @block.vector
        def _(dve):
            dve.sem_inc(mod_bank_free, 2)
            dve.wait_ge(setup_cols, 2)
            nc.vector.tensor_copy(chan_col, bank[:, 2, 0:32])
            nc.vector.tensor_copy(conv_col, bank[:, 1, 0:CTILES * TAPS]).then_inc(dve_a, 1)
            dve.wait_ge(csig_made, 1)
            nc.vector.tensor_tensor(c_silu, bank[:, 0, 0:32], c_sig, ALU.mult).then_inc(dve_a, 1)
            dve.wait_ge(dve_a, 2)
            nc.vector.tensor_copy(c_rep.rearrange("p k (v r) -> p k v r", v=2),
                                  c_silu.rearrange("p (v k) -> p k v", v=2).unsqueeze(3)
                                  .to_broadcast([P, KT, 2, 16])).then_inc(crep_made, 1)
            nc.vector.tensor_copy(row_pick, ident[:, ::16].unsqueeze(2).to_broadcast([P, 8, P]))\
                .then_inc(crep_made, 1)
            nc.vector.memset(gate_wp, 0.0).then_inc(dve_a, 1)
            dve.wait_ge(dve_a, 3)
            dve.wait_ge(rows_loaded, 16 * 10)
            for g, first in enumerate((0, 8, 4, 12)):
                last = nc.vector.tensor_copy(gate_wp[:, :, 32 * g:32 * g + 4], gate_w[:, :, first:first + 4])
            last.then_inc(gate_wp_made, 1)
            dve.wait_ge(mod_bias_loaded, 48)
            with dve.Fori(0, 4) as i:
                for par in range(2):
                    dve.wait_ge(mod_spread, i * 2 + (par + 1))
                    at = bass.ds(i * (2 * NB) + par * NB, NB)
                    nc.vector.tensor_tensor(mod_x[:, at], mod_x[:, at], bank[:, 2 * par, :], ALU.add)
                    nc.vector.tensor_tensor(mod_c[:, at], mod_c[:, at], bank[:, 2 * par + 1, :], ALU.add)\
                        .then_inc(mod_bank_free, 1)
            dve.wait_ge(mod_bank_free, 2 + 8)
            dve.wait_ge(x_rms, 1)
            nc.vector.reciprocal(rstd, rms).then_inc(dve_a, 1)
            for m in (mod_x, mod_c):
                nc.vector.scalar_tensor_tensor(m[:, D:2 * D], m[:, D:2 * D], 1.0, g_mix_row, ALU.add, ALU.mult)\
                    .then_inc(dve_a, 1)
            dve.wait_ge(dve_a, 6)
            for i in range(6):
                m = mod_x if i < LT else mod_c
                nc.vector.scalar_tensor_tensor(x_tile[i], x_tile[i], rstd[:, i:i + 1], m[:, D:2 * D], ALU.mult,
                                               ALU.mult).then_inc(dve_a, 1)
                dve.wait_ge(dve_a, 7 + i)
                nc.vector.tensor_tensor(x_tile[i], x_tile[i], m[:, 0:D], ALU.add).then_inc(h_made, 1)

            with dve.Fori(0, 4) as j:
                dve.wait_ge(glu_done, j + 1)
                for tap in range(TAPS):
                    for cc in range(2):
                        n = 2 * tap + cc
                        ct = j * 2 + cc
                        y = R5[:, bass.ds(j * (2 * T) + (8 + cc) * T, T)].rearrange("p (r w) -> p r w", w=GRID_W)
                        u = R4[:, bass.ds(j * (2 * ROWS * PADW) + cc * ROWS * PADW, ROWS * PADW)]\
                            .rearrange("p (r w) -> p r w", w=PADW)[:, :, tap:tap + GRID_W]
                        w = conv_col[:, bass.ds(j * (2 * TAPS) + cc * TAPS + tap, 1)]
                        if tap == 0:
                            nc.vector.tensor_scalar(y, u, w, chan_col[:, bass.ds(j * 2 + 16 + cc, 1)], ALU.mult,
                                                    ALU.add).then_inc(conv_step, 1)
                        else:
                            dve.wait_ge(conv_step, j * (2 * TAPS) + (n - 1))
                            nc.vector.scalar_tensor_tensor(y, u, w, y, ALU.mult, ALU.add).then_inc(conv_step, 1)
            dve.wait_ge(pass_full, 1)
            for f in range(CTILES):
                nc.vector.tensor_tensor(mixT[:, 8 + f, :], mixT[:, 8 + f, :], bank[:, 0, :], ALU.subtract)\
                    .then_inc(ln_sub, 1)
            dve.wait_ge(gate_act, 3)
            nc.vector.scalar_tensor_tensor(grow[5], grow[1], 0.0, grow[4], ALU.min, ALU.subtract)\
                .then_inc(gate_dve, 1)
            dve.wait_ge(gate_dve, 1)
            nc.vector.tensor_tensor_scan(grow[3], one_col[0:64, :].to_broadcast([64, L]), grow[5], 0.0, ALU.mult,
                                         ALU.add).then_inc(gate_dve, 1)
            dve.wait_ge(gate_dve, 2)
            nc.vector.tensor_tensor(grow[4], grow[0], grow[3], ALU.subtract).then_inc(gate_dve, 1)
            dve.wait_ge(gate_dve, 3)
            nc.vector.tensor_tensor_scan(grow[5], grow[4], grow[4], 0.0, ALU.max, ALU.max).then_inc(gate_dve, 1)
            dve.wait_ge(gate_dve, 4)
            nc.vector.tensor_tensor(grow[2], grow[3], grow[5], ALU.add).then_inc(gate_dve, 1)
            dve.wait_ge(gate_act, 4)
            for d in range(2):
                r = slice(32 * d, 32 * d + 32)
                g_c, g_x = g_nat[r, 0:C], g_nat[r, C:L]
                m_x, e_x = m_rows[r, :], e_nat[r, :]
                if d:
                    g_c, g_x, m_x, e_x = g_c[:, ::-1], g_x[:, ::-1], m_x[:, ::-1], e_x[:, ::-1]
                nc.vector.tensor_copy(g_c, grow[4][r, 0:C])
                nc.vector.tensor_copy(g_x, grow[4][r, C:L])
                nc.vector.tensor_copy(m_x, grow[5][r, C:L])
                nc.vector.tensor_copy(e_x, grow[1][r, C:L]).then_inc(gate_dve, 1)
            dve.wait_ge(set_free, 2 + 13)
            nc.vector.reciprocal(glu_of(0, 0)[:, 1, :], glu_of(0, 0)[:, 0, :]).then_inc(ln_rstd, 1)
            dve.wait_ge(ln_rstd, 1)
            for f in range(CTILES):
                nc.vector.tensor_tensor(mixT[:, 8 + f, :], mixT[:, 8 + f, :], glu_of(0, 0)[:, 1, :], ALU.mult)\
                    .then_inc(ln_scaled, 1)
            dve.wait_ge(set_free, 2 + 16)
            nc.vector.memset(v_aug[:, :, :, HD:HD + 1], 1.0).then_inc(v_ones, 1)

            dve.wait_ge(quarter_used, 4 * (KV + 4))
            dve.wait_ge(consts_made, 7)
            for r in range(8):
                col = 32 * (r // HEADS) + r % HEADS
                last = nc.vector.tensor_copy(pick[:, r, :], ident[0:64, col:col + 1].to_broadcast([64, P]))
            last.then_inc(pick_made, 1)
            steps = 0
            for h in range(HEADS):
                for d in range(2):
                    r = 32 * d + h
                    dve.wait_ge(m_full, 2 * h + d + 1)
                    if h:
                        dve.wait_ge(w_made, 12 * h)
                        dve.wait_ge(h_summed, 4 * h)
                    for s in range(LT):
                        nc.vector.scalar_tensor_tensor(diag_arg[:, d, s, :], bank[:, 2 + d, s * P:(s + 1) * P],
                                                       g_col[:, s, r:r + 1], mask[:, d, :], ALU.subtract, ALU.max)\
                            .then_inc(diag_made, 1)
                dve.wait_ge(s_copied, 6 * (h + 1))
                for d in range(2):
                    for s in range(6):
                        lo, hi = (0, T) if s >= LT else ((s * P, T) if d == 0 else (0, (s + 1) * P))
                        dve.wait_ge(w_made, 12 * h + 6 * d + s + 1)
                        nc.vector.tensor_tensor(probT[:, d, s, lo:hi], probT[:, d, s, lo:hi], scoreT[:, s, lo:hi],
                                                ALU.mult).then_inc(p_made, 1)
                for j in range(LT):
                    for d in range(2):
                        nb = bank[:, 4 + d, :]
                        dve.wait_ge(num_full, 8 * h + 2 * j + d + 1)
                        nc.vector.tensor_scalar(den[:, d:d + 1], nb[:, HD:HD + 1], -1.0,
                                                e_col[:, j, 32 * d + h:32 * d + h + 1], ALU.mult, ALU.max)\
                            .then_inc(num_step, 1)
                        steps += 1
                        dve.wait_ge(num_step, steps)
                        nc.vector.tensor_tensor(den[:, d:d + 1], nb[:, HD:HD + 1], den[:, d:d + 1], ALU.max)\
                            .then_inc(num_step, 1)
                        steps += 1
                        dve.wait_ge(num_step, steps)
                        nc.vector.reciprocal(den[:, 2 + d:3 + d], den[:, d:d + 1]).then_inc(num_step, 1)
                        steps += 1
                        dve.wait_ge(num_step, steps)
                        hs = h_sum[:, j, h, :]
                        if d == 0:
                            nc.vector.tensor_scalar(hs, nb[:, 0:HD], den[:, 2:3], None, ALU.mult)\
                                .then_inc(num_free, 1)
                        else:
                            dve.wait_ge(num_free, 8 * h + 2 * j + 1)
                            nc.vector.scalar_tensor_tensor(hs, nb[:, 0:HD], den[:, 3:4], hs, ALU.mult, ALU.add)\
                                .then_inc(num_free, 1)
                for j in range(LT):
                    hs = h_sum[:, j, h, :]
                    dve.wait_ge(num_free, 8 * h + 2 * j + 2)
                    if j or h:
                        dve.wait_ge(h_summed, 4 * h + j)
                    nc.vector.tensor_tensor_reduce(out=diag_arg[:, 0, 0:2, :].rearrange("p a b -> p (a b)"), in0=hs,
                                                   in1=hs, scale=1.0, scalar=0.0, op0=ALU.mult, op1=ALU.add,
                                                   accum_out=hssq[:, 4 * j + h:4 * j + h + 1]).then_inc(h_summed, 1)
            dve.wait_ge(h_rms, 1)
            nc.vector.reciprocal(hrstd, hrms).then_inc(num_step, 1)
            steps += 1
            dve.wait_ge(num_step, steps)
            for h in range(HEADS):
                for j in range(LT):
                    hs = h_sum[:, j, h, :]
                    nc.vector.tensor_scalar(hs, hs, hrstd[:, 4 * j + h:4 * j + h + 1], None, ALU.mult)\
                        .then_inc(h_normed, 1)
            for f in range(8):
                dve.wait_ge(ht_full, f + 1)
                nc.vector.scalar_tensor_tensor(mixT[:, f, :], bank[:, f % 4, :], chan_col[:, 24 + f:25 + f],
                                               mixT[:, f, :], ALU.mult, ALU.mult).then_inc(ht_mixed, 1)

            dve.sem_inc(wo_free, 2)
            dve.wait_ge(ga1_loaded, 16)
            dve.wait_ge(x2_loaded, 64)
            with dve.Fori(0, 2) as i:
                for par in range(2):
                    at = bass.ds(i * (2 * NB) + par * NB, NB)
                    dve.wait_ge(quarter_used, i * 8 + 4 * (WO + par + 1))
                    for j in range(LT):
                        ins = nc.vector.tensor_tensor(out_part[:, j, :], bank[:, 4 * par + j, :], ga1_row[:, at],
                                                      ALU.mult)
                        ins.then_inc(wo_step, 1)
                    dve.wait_ge(wo_step, i * 16 + 8 * par + 4)
                    for j in range(LT):
                        nc.vector.tensor_tensor(x2[:, j, at], x2[:, j, at], out_part[:, j, :], ALU.add)\
                            .then_inc(wo_step, 1)
                    dve.wait_ge(wo_step, i * 16 + 8 * par + 8)
                    dve.sem_inc(wo_free, 1)
            dve.wait_ge(ffn_rows_loaded, 48)
            nc.vector.scalar_tensor_tensor(sc2_row, sc2_row, 1.0, g_ffn_row, ALU.add, ALU.mult).then_inc(a2_made, 1)
            dve.wait_ge(x2_rms, 1)
            nc.vector.reciprocal(rstd2, rms2).then_inc(a2_made, 1)
            dve.wait_ge(a2_made, 2)
            def modulated(i):
                if i >= 2:
                    dve.wait_ge(tr2_full, 4 * (i - 1))
                nc.vector.scalar_tensor_tensor(h2_tile[i % 2], x2[:, i, :], rstd2[:, i:i + 1], sc2_row, ALU.mult,
                                               ALU.mult).then_inc(h2_step, 1)
                dve.wait_ge(h2_step, i + 1)
                nc.vector.tensor_tensor(h2_tile[i % 2], h2_tile[i % 2], sh2_row, ALU.add).then_inc(h2_made, 1)

            def rest(i):
                for g in range(4):
                    dve.wait_ge(tr2_hi, 4 * i + g + 1)
                    at = (slice(None), slice(4 * g, 4 * g + 4), slice(i * P, (i + 1) * P))
                    nc.vector.tensor_tensor(h2_lo[at].bitcast(F32R), bank[:, 4 + g, :].rearrange(
                        "p (k t) -> p k t", k=4), h2_hi[at], ALU.subtract).then_inc(tr2_free, 1)

            modulated(0)
            for i in range(1, LT):
                modulated(i)
                rest(i - 1)
            rest(LT - 1)

            done = [0]

            def put(ins):
                ins.then_inc(topk, 1)
                done[0] += 1

            def top16(jobs):
                start = done[0]
                n = len(jobs)
                for k, (src, val, idx) in enumerate(jobs):
                    put(nc.vector.max(val[:, 0:8], src))
                for k, (src, val, idx) in enumerate(jobs):
                    dve.wait_ge(topk, start + k + 1)
                    put(nc.vector.max_index(idx[:, 0:8], val[:, 0:8], src))
                for k, (src, val, idx) in enumerate(jobs):
                    put(nc.vector.match_replace(src, val[:, 0:8], src, NEG))
                for k, (src, val, idx) in enumerate(jobs):
                    dve.wait_ge(topk, start + 2 * n + k + 1)
                    put(nc.vector.max(val[:, 8:16], src))
                for k, (src, val, idx) in enumerate(jobs):
                    dve.wait_ge(topk, start + 3 * n + k + 1)
                    put(nc.vector.max_index(idx[:, 8:16], val[:, 8:16], src))
                dve.wait_ge(topk, done[0])

            dve.wait_ge(tr2_full, 16)
            for b in range(4):
                dve.wait_ge(score_copied, b + 1)
                hh = slice(2 * b, 2 * b + 2)
                for j in range(LT):
                    top16([(score[:, j, 4 * b + m, :], top_val[:, j, 4 * b + m, :], top_idx[:, j, 4 * b + m, :])
                           for m in range(4)])
                for j0 in range(0, LT, 2):
                    for jj in range(2):
                        cand = pair_sums(j0 + jj, b)
                        val = top_val[:, j0 + jj, 4 * b:4 * b + 4, :].rearrange("p (h s) k -> p h s k", s=2)
                        put(nc.vector.tensor_tensor(
                            cand, val[:, :, 0, :].unsqueeze(3).to_broadcast([P, 2, TOPK, TOPK]),
                            val[:, :, 1, :].unsqueeze(2).to_broadcast([P, 2, TOPK, TOPK]), ALU.add))
                    dve.wait_ge(topk, done[0])
                    top16([(pair_sums(j0 + jj, b)[:, hl].rearrange("p a c -> p (a c)"), best[:, j0 + jj, 2 * b + hl, :],
                            pos[:, j0 + jj, 2 * b + hl, :]) for jj in range(2) for hl in range(2)])
                put(nc.vector.tensor_single_scalar(pos_a[:, :, hh, :], pos[:, :, hh, :], 4,
                                                   ALU.logical_shift_right))
                put(nc.vector.tensor_single_scalar(pos_b[:, :, hh, :], pos[:, :, hh, :], 15, ALU.bitwise_and))
                dve.wait_ge(topk, done[0])
                for j in range(LT):
                    idx = top_idx[:, j, 4 * b:4 * b + 4, :].rearrange("p (h s) k -> p h s k", s=2)
                    full = [P, 2, TOPK, TOPK]
                    match = [pair_sums(2 * (j % 2) + s, b) for s in range(2)]
                    for s, which in enumerate((pos_a, pos_b)):
                        put(nc.vector.tensor_tensor(
                            match[s], iota[:, 0:TOPK].unsqueeze(1).unsqueeze(1).to_broadcast(full),
                            which[:, j, hh, :].unsqueeze(3).to_broadcast(full), ALU.is_equal))
                    dve.wait_ge(topk, done[0])
                    for s in range(2):
                        put(nc.vector.tensor_tensor(match[s], match[s],
                                                    idx[:, :, s, :].unsqueeze(2).to_broadcast(full), ALU.mult))
                    dve.wait_ge(topk, done[0])
                    for s, dst in enumerate((exp1, exp2)):
                        put(nc.vector.tensor_reduce(dst[:, j, hh, :], match[s], AX.X, ALU.add))
                    dve.wait_ge(topk, done[0])
            dve.wait_ge(topk, done[0])
            best_g = best.rearrange("p j h k -> p (j h) k")
            gate_g = gate.rearrange("p j h k -> p (j h) k")
            nc.vector.tensor_tensor(gate_g, best_g, best_g[:, :, 0:1].to_broadcast([P, LT * PH, TOPK]),
                                    ALU.subtract).then_inc(soft_in, 1)
            dve.wait_ge(soft_exp, 1)
            put(nc.vector.tensor_reduce(soft[:, 0:32], gate_g, AX.X, ALU.add))
            dve.wait_ge(topk, done[0])
            put(nc.vector.reciprocal(soft[:, 32:64], soft[:, 0:32]))
            dve.wait_ge(topk, done[0])
            nc.vector.tensor_tensor(gate_g, gate_g, soft[:, 32:64].unsqueeze(2).to_broadcast([P, LT * PH, TOPK]),
                                    ALU.mult).then_inc(slots_made, 1)
            dve.wait_ge(slotT_made, 3)
            dve.wait_ge(score_full, 4)
            with dve.Fori(0, 32) as i:
                for g in range(4):
                    dve.wait_ge(onehot_used, i * 4 + (g + 1))
                    for s in range(4):
                        tok = bass.ds(i * 16 + 4 * g + s, 1)
                        nc.vector.tensor_scalar(onehot[:, g, s, 0, :], iota, slotT[:, 0, tok], None, ALU.is_equal)
                        last = nc.vector.tensor_scalar(onehot[:, g, s, 1, :], iota, slotT[:, 1, tok],
                                                       slotT[:, 2, tok], ALU.is_equal, ALU.mult)
                    last.then_inc(onehot_made, 1)

            def weigh_unit(q, count):
                dve.wait_ge(weigh_full[q], count)
                neurons = weigh[:, q, 0, :].rearrange("p (a c t) -> p a c t", a=2, t=CHUNK)
                gates = weigh[:, q, 1, :].rearrange("p (c a t) -> p a c t", a=2, t=CHUNK)
                nc.vector.tensor_tensor(neurons, neurons, gates, ALU.mult).then_inc(weighed, 1)

            def rest_unit(q, n):
                dve.wait_ge(a_hi_made, n)
                nc.vector.tensor_tensor(a_split[:, q % 2, 1, :].bitcast(F32R), weigh[:, q, 0, :],
                                        a_split[:, q % 2, 0, :], ALU.subtract).then_inc(a_split_made, 1)

            def merge(s):
                dve.wait_ge(split_used, V0 + (s + 1) * PAIRS)
                for k in range(8):
                    b = (k + 4) % 8
                    if s:
                        dve.wait_ge(merge_step, 16)
                    nc.vector.tensor_tensor(gated[:, b, :], bank[:, b, :],
                                            ga2_row[:, s * HALF + (b % 2) * NB:s * HALF + (b % 2 + 1) * NB],
                                            ALU.mult).then_inc(sum_free, 1)
                for k in range(8):
                    b = (k + 4) % 8
                    part = x3[:, b // 2, s * HALF + (b % 2) * NB:s * HALF + (b % 2 + 1) * NB]
                    dve.wait_ge(sum_free, 8 * s + k + 1)
                    nc.vector.tensor_tensor(part, part, gated[:, b, :], ALU.add).then_inc(merge_step, 2)

            for q in range(3):
                weigh_unit(q, 32)
            with dve.Fori(0, PAIRS // 4) as i:
                for q in range(4):
                    rest_unit(q, i * 4 + (q + 1))
                    weigh_unit((q + 3) % 4, i * 32 + (32 if q == 0 else 64))
            for q in range(2):
                rest_unit(q, PAIRS + q + 1)
                weigh_unit((q + 3) % 4, PAIRS * 8 + (32 if q == 0 else 64))
            dve.wait_ge(last_rows, 16 * (LT + 2))
            merge(0)
            for q in range(2, 4):
                rest_unit(q, PAIRS + q + 1)
                weigh_unit((q + 3) % 4, PAIRS * 8 + 64)
            with dve.Fori(PAIRS // 4 + 1, SWEEPS * PAIRS // 4 - 1) as i:
                for q in range(4):
                    rest_unit(q, i * 4 + (q + 1))
                    weigh_unit((q + 3) % 4, i * 32 + (32 if q == 0 else 64))
            for q in range(4):
                rest_unit(q, SWEEPS * PAIRS - 4 + q + 1)
                if q == 0:
                    weigh_unit(3, SWEEPS * PAIRS * 8)
            merge(1)
            dve.wait_ge(y_rms, 1)
            nc.vector.reciprocal(rstd3, rms3).then_inc(y_step, 1)
            dve.wait_ge(y_step, 1)
            for j in range(LT):
                nc.vector.scalar_tensor_tensor(x3[:, j, :], x3[:, j, :], rstd3[:, j:j + 1], g_final_row, ALU.mult,
                                               ALU.mult).then_inc(y_made, 1)

        @block.tensor
        def _(pe):
            mm = nc.tensor.matmul
            pe.wait_ge(consts_made, 5)
            pe.wait_ge(rows_loaded, 16 * 10)
            nc.tensor.transpose(bank[:, 0, 0:32], vec_rows, ident[0:32, 0:32]).then_inc(setup_cols, 1)
            nc.tensor.transpose(bank[:, 2, 0:32], chan_rows, ident[0:32, 0:32])
            for f in range(CTILES):
                last = nc.tensor.transpose(bank[:, 1, TAPS * f:TAPS * (f + 1)], conv_rows[:, f * P:(f + 1) * P],
                                           ident[0:TAPS, 0:TAPS])
            last.then_inc(setup_cols, 1)
            pe.wait_ge(crep_made, 2)

            def wait_quarter(blk, q):
                pe.wait_ge(quarter_full[q], (blk + 1) * 16)

            def row_quarter(n, q, first=True):
                for kk in range(QT):
                    k = q * QT + kk
                    for j in range(4):
                        last = mm(bank[32 * j:32 * j + 32, n, 0:P], c_rep[:, k, :], ring[:, q, kk, j * P:(j + 1) * P],
                                  start=first and k == 0, stop=k == KT - 1, tile_position=(0, 32 * j))
                last.then_inc(quarter_used, 1)

            with pe.Fori(0, 4) as i:
                for par in range(2):
                    for q in range(4):
                        pe.wait_ge(quarter_full[q], i * 32 + 16 * (par + 1))
                        row_quarter(4 + par, q)
                    pe.wait_ge(row_copied, i * 2 + (par + 1))
                    pe.wait_ge(mod_bank_free, i * 2 + (par + 1))
                    for w in range(2):
                        for j in range(4):
                            last = mm(bank[:, 2 * par + w, j * P:(j + 1) * P], row_pick[:, 2 * j + w, :],
                                      row_buf[:, par, :], start=True, stop=True)
                    last.then_inc(mod_spread, 1)
            for i in range(6):
                pe.wait_ge(h_made, i + 1)
                for g in range(4):
                    if i:
                        pe.wait_ge(tr_free, 4 * (i - 1) + g + 1)
                    for k in range(4):
                        kk = 4 * g + k
                        last = nc.tensor.transpose(bank[:, 4 + g, k * P:(k + 1) * P],
                                                   x_tile[i][:, kk * P:(kk + 1) * P], ident)
                    last.then_inc(tr_full, 1)
            pe.wait_ge(tr_free, 24)

            def full(blk):
                return 16 * (blk + 1) + 16 * min(max((blk - CONV) // 2 + 1, 0), 4)

            def mod2(b, n):
                for j in range(4):
                    mm(bank[32 * j:32 * j + 32, n, 0:P], ident[0:64, 4 * b + j:4 * b + j + 1].to_broadcast([64, 32]),
                       bias_rows, start=True, stop=False, tile_position=(0, 32 * j))
                for q in range(4):
                    pe.wait_ge(quarter_full[q], full(mod2_block(b)))
                    row_quarter(n, q, False)

            def block_pass(blk, s, acts, n, weights, release, signal=None, tiles=4):
                for q in range(4):
                    pe.wait_ge(quarter_full[q], full(blk))
                    for kk in range(QT):
                        k = q * QT + kk
                        for m in range(tiles):
                            if weights:
                                last = mm(bank[:, s + m, 0:n], ring[:, q, kk, m * P:(m + 1) * P], acts(k, m),
                                          start=k == 0, stop=k == KT - 1)
                            else:
                                last = mm(bank[:, s + m, :], acts(k, m), ring[:, q, kk, :],
                                          start=k == 0, stop=k == KT - 1)
                    if release:
                        last.then_inc(quarter_used, 1)
                if signal is not None:
                    last.then_inc(signal, 1)

            for j in range(8):
                par = j % 2
                pe.wait_ge(set_free, j + 1)
                if j:
                    pe.wait_ge(mrow_made, j)
                block_pass(CONV + 2 * j, 4 * par, lambda k, m: hT[:, k, 0:T], T, True, True)
                pe.wait_ge(set_free, j + 2)
                mod2(j, 4 - 4 * par)
            pe.wait_ge(mrow_made, 8)
            pe.wait_ge(set_free, 9)
            pe.wait_ge(conv_step, 4 * 2 * TAPS)
            for f in range(CTILES):
                last = mm(bank[:, 0, :], mean_w, mixT[:, 8 + f, :], start=f == 0, stop=f == CTILES - 1)
            last.then_inc(pass_full, 1)
            pe.wait_ge(set_free, 10)
            pe.wait_ge(gate_wp_made, 1)
            for k in range(KT):
                mm(bank[:, 4, :], gate_wp[:, k, :], hT[:, k, 0:T], start=k == 0, stop=k == KT - 1)
                last = mm(bank[:, 5, 0:C], gate_wp[:, k, :], hT[:, k, T:L], start=k == 0, stop=k == KT - 1)
            last.then_inc(pass_full, 1)
            pe.wait_ge(set_free, 11)
            block_pass(KV, 0, lambda k, m: hT[:, k, 0:T], T, True, False, pass_full)
            pe.wait_ge(set_free, 12)
            block_pass(KV, 4, lambda k, m: hT[:, k, T:L], C, True, True)
            pe.wait_ge(set_free, 13)
            for f in range(CTILES):
                last = mm(bank[:, 0, :], mean_w, ln_sq[:, f, :], start=f == 0, stop=f == CTILES - 1)
            last.then_inc(pass_full, 1)
            pe.wait_ge(set_free, 14)
            block_pass(KV + 1, 4, lambda k, m: hT[:, k, 0:T], T, True, False, pass_full)
            pe.wait_ge(set_free, 15)
            block_pass(KV + 1, 0, lambda k, m: hT[:, k, T:L], C, True, True)
            pe.wait_ge(set_free, 16)
            pe.wait_ge(gate_dve, 7)
            for s in range(6):
                at = C + s * P if s < LT else (s - LT) * P
                nc.tensor.transpose(bank[:, 4, 64 * s:64 * s + 64], g_nat[:, at:at + P], ident[0:64, 0:64])
            for s in range(LT):
                last = nc.tensor.transpose(bank[:, 5, 64 * s:64 * s + 64], e_nat[:, s * P:(s + 1) * P],
                                           ident[0:64, 0:64])
            last.then_inc(pass_full, 1)
            for half in range(2):
                pe.wait_ge(set_free, 17 + 2 * half)
                block_pass(KV + 2 + half, 0, lambda k, m: hT[:, k, m * P:(m + 1) * P], NB, False, False, pass_full)
                pe.wait_ge(set_free, 18 + 2 * half)
                block_pass(KV + 2 + half, 4, lambda k, m: hT[:, k, T + m * P:T + (m + 1) * P], NB, False, True,
                           tiles=CT)
            pe.wait_ge(quarter_used, 4 * (KV + 4))
            pe.sem_inc(bproj_done, 1)
            pe.wait_ge(set_free, 2 + 20)
            pe.wait_ge(pick_made, 1)

            for h in range(HEADS):
                for d in range(2):
                    if h:
                        pe.wait_ge(w_made, 12 * h)
                    mm(bank[:, 2 + d, :], pick[:, HEADS * d + h, :], m_rows, start=True, stop=True)\
                        .then_inc(m_full, 1)
                for s in range(6):
                    n = 6 * h + s
                    if n >= 2:
                        pe.wait_ge(s_copied, n - 1)
                    for k in range(2):
                        last = mm(bank[:, s % 2, :], kT[:, 2 * h + k, s * P:(s + 1) * P], qT[:, 2 * h + k, :],
                                  start=k == 0, stop=k == 1)
                    last.then_inc(s_full, 1)
                for b in (8 + 2 * h, 9 + 2 * h):
                    pe.wait_ge(mrow_made, b - 1)
                    mod2(b, 6 + b % 2)
                for j in range(LT):
                    for d in range(2):
                        n = 8 * h + 2 * j + d
                        keys = [4, 5] + [s for s in range(LT) if (s <= j if d == 0 else s >= j)]
                        if n >= 2:
                            pe.wait_ge(num_free, n - 1)
                        pe.wait_ge(p_made, 12 * (h + 1))
                        for i, s in enumerate(keys):
                            last = mm(bank[:, 4 + d, 0:HD + 1], probT[:, d, s, j * P:(j + 1) * P],
                                      v_aug[:, s, h, :], start=i == 0, stop=i == len(keys) - 1)
                        last.then_inc(num_full, 1)
            for f in range(8):
                h, e = f // 2, f % 2
                pe.wait_ge(h_normed, 4 * (h + 1))
                if f >= 4:
                    pe.wait_ge(ht_mixed, f - 3)
                for j in range(LT):
                    last = nc.tensor.transpose(bank[:, f % 4, j * P:(j + 1) * P], h_sum[:, j, h, e * P:(e + 1) * P],
                                               ident)
                last.then_inc(ht_full, 1)

            pe.wait_ge(ht_mixed, 8)
            pe.wait_ge(conv_done, 8)
            pe.wait_ge(num_free, 32)
            with pe.Fori(0, 2) as i:
                for par in range(2):
                    pe.wait_ge(wo_free, i * 2 + (par + 1))
                    for q in range(4):
                        pe.wait_ge(quarter_full[q], i * 32 + (full(WO - 1) + 16 * (par + 1)))
                        for kk in range(QT):
                            k = q * QT + kk
                            for j in range(LT):
                                last = mm(bank[:, 4 * par + j, :], mixT[:, k, j * P:(j + 1) * P],
                                          ring[:, q, kk, :], start=k == 0, stop=k == KT - 1)
                        last.then_inc(quarter_used, 1)
            pe.wait_ge(wo_free, 6)
            for i in range(LT):
                pe.wait_ge(h2_made, i + 1)
                for g in range(4):
                    if i:
                        pe.wait_ge(tr2_free, 4 * (i - 1) + g + 1)
                    for k in range(4):
                        kk = 4 * g + k
                        last = nc.tensor.transpose(bank[:, 4 + g, k * P:(k + 1) * P],
                                                   h2_tile[i % 2][:, kk * P:(kk + 1) * P], ident)
                    last.then_inc(tr2_full, 1)
            pe.wait_ge(tr2_free, 16)

            def mm3(out_, left, right, start, stop):
                for n, (a, b) in enumerate(((0, 0), (0, 1), (1, 0))):
                    last = mm(out_, left[a].bitcast(F32R), right[b].bitcast(F32R), start=start and n == 0,
                              stop=stop and n == 2)
                return last

            def query_unit(r):
                b, q = r // 4, r % 4
                pe.wait_ge(split_made, r + 1)
                for kk in range(QT):
                    k = q * QT + kk
                    for m in range(4):
                        at = slice(kk * NB + m * P, kk * NB + (m + 1) * P)
                        last = mm3(bank[:, 4 * (b % 2) + m, :], [split[:, r % 2, h, at] for h in range(2)],
                                   [h2_hi[:, k, :], h2_lo[:, k, :]], k == 0, k == KT - 1)
                last.then_inc(split_used, 1)

            def scores(b):
                pe.wait_ge(q_copied, b + 1)
                for m in range(4):
                    for j in range(LT):
                        last = mm(bank[:, 4 * (b % 2) + m, j * P:(j + 1) * P],
                                  query[:, b % 2, m, j * P:(j + 1) * P], keysT[:, m % 2, :], start=True, stop=True)
                last.then_inc(score_full, 1)

            for r in range(U0):
                if r % 4 == 0 and r >= 8:
                    pe.wait_ge(score_copied, r // 4 - 1)
                query_unit(r)
                if r % 4 == 1 and r >= 4:
                    scores(r // 4 - 1)

            def neurons(blk, q, wait=True):
                pe.wait_ge(split_made, blk * 4 + (U0 + q + 1))
                if wait:
                    pe.wait_ge(gelu_made, blk * 4 + (q - 3))
                for k in range(KT):
                    last = mm3(bank[:, q, :], [split[:, q % 2, h, k * P:(k + 1) * P] for h in range(2)],
                               [h2_hi[:, k, :], h2_lo[:, k, :]], k == 0, k == KT - 1)
                last.then_inc(split_used, 1)

            pe.wait_ge(score_copied, 3)
            for q in range(4):
                neurons(0, q, False)
                if q == 0:
                    scores(3)
            with pe.Fori(1, 6) as i:
                for q in range(4):
                    neurons(i, q)
            pe.wait_ge(slots_made, 1)
            pe.wait_ge(score_copied, 4)
            for w, src in enumerate((exp1, exp2, gate)):
                for j in range(LT):
                    last = nc.tensor.transpose(bank[:, 4 + w, j * P:(j + 1) * P],
                                               src[:, j, :, :].rearrange("p h k -> p (h k)"), ident)
                last.then_inc(slotT_full, 1)
            pe.sem_inc(onehot_used, 4)
            with pe.Fori(0, CHUNKS) as chunk:
                for q in range(4):
                    neurons(chunk * 3 + 6, q)
                for n in range(8):
                    neurons(chunk * 3 + (7 + n // 4), n % 4)
                    for g in range(2 * n, 2 * n + 2):
                        pe.wait_ge(onehot_made, chunk * 16 + (g + 1))
                        pe.wait_ge(gbank_free, chunk * 16 + (g + 1))
                        for s in range(4):
                            last = mm(bank[:, 4 + g % 4, s * NK:(s + 1) * NK], onehot[:, g % 4, s, 1, :],
                                      onehot[:, g % 4, s, 0, :], start=True, stop=True)
                        last.then_inc(onehot_used, 1)
            with pe.Fori(30, 32) as i:
                for q in range(4):
                    neurons(i, q)

            def sums(count, q, first=None, stop=False):
                pe.wait_ge(split_made, count + (V0 + q + 1))
                pe.wait_ge(a_split_made, count + (q + 1))
                for a in range(2):
                    for k in range(8):
                        b = (k + 4) % 8
                        if first == 0 and a == 0:
                            if b == 4:
                                pe.wait_ge(gbank_free, 4 + 128)
                            if b < 4:
                                pe.wait_ge(gelu_made, NK - 3 + b)
                        if first == 1 and a == 0:
                            pe.wait_ge(sum_free, k + 1)
                        j, n = b // 2, b % 2
                        last = mm3(bank[:, b, :],
                                   [a_split[:, q % 2, h, a * T + j * P:a * T + (j + 1) * P] for h in range(2)],
                                   [split[:, q % 2, h, a * HALF + n * NB:a * HALF + (n + 1) * NB] for h in range(2)],
                                   first is not None and a == 0, stop and a == 1)
                last.then_inc(split_used, 1)

            for s in range(SWEEPS):
                for q in range(4):
                    sums(s * PAIRS, q, s if q == 0 else None)
                with pe.Fori(1, PAIRS // 4 - 1) as i:
                    for q in range(4):
                        sums(i * 4 + s * PAIRS, q)
                for q in range(4):
                    sums((s + 1) * PAIRS - 4, q, None, q == 3)


_INS = ['x', 'c', 'ctx', 'c_ctx', 'w_mod', 'b_mod', 'g_mix', 'g_ffn', 'w_in', 'b_gate', 'g_mhn', 'conv_w', 'conv_b',
        'cn_g', 'cn_b', 'w_out', 'w_query', 'sub_keys', 'u_emb', 'v_emb', 'g_final']


def kernel(**inputs):
    import numpy as _np
    import concourse.bacc as _bacc
    from concourse import mybir as _mybir
    from concourse.bass_utils import run_bass_kernel_spmd as _run

    laid = {name: _np.asarray(inputs[name]) for name in _INS}
    laid['sub_keys'] = laid['sub_keys'][0].transpose(2, 0, 1)
    laid['u_emb'] = laid['u_emb'][0].reshape(NK, NK, KT, P).transpose(0, 3, 2, 1).reshape(NK, P, KT * NK)

    nc = _bacc.Bacc("TRN2", target_bir_lowering=False, num_devices=1)
    arrays, args = {}, []
    for name in _INS:
        a = _np.ascontiguousarray(laid[name])
        arrays[f"in_{name}"] = a
        args.append(nc.dram_tensor(f"in_{name}", a.shape, _mybir.dt.from_np(a.dtype), kind="ExternalInput").ap())
    args.append(nc.dram_tensor("out", (1, T, D), _mybir.dt.float32, kind="ExternalOutput").ap())
    hybrid_layer(nc, *args)
    r = _run(nc, [arrays], core_ids=[0])
    return r.results[0]["out"]
```

```python
import concourse.bass as bass
from concourse import mybir
from contextlib import ExitStack

F32 = mybir.dt.float32
F32R = mybir.dt.float32r
BF16 = mybir.dt.bfloat16
U32 = mybir.dt.uint32
ALU = mybir.AluOpType
ACT = mybir.ActivationFunctionType
AX = mybir.AxisListType

P = 128
D = 2048
KT = D // P
T = 512
C = 256
L = T + C
LT, CT = T // P, C // P
NB = 512
QT = KT // 4
GRID_W, ROWS = 64, T // 64
EPS = 1e-6
HEADS, HD = 4, 256
MW = HEADS * HD
GATES = 4 * HEADS
GATE0 = 4 * MW
CONV0 = GATE0 + GATES
CW = D - MW
CTILES = CW // P
TAPS = 31
PADW = GRID_W + TAPS - 1
PH, NK, TOPK = 8, 128, 16
SLOTS = PH * TOPK
BIG = 1e30
NEG = -3.0e38
U0 = 16
V0 = U0 + NK
PAIRS = NK // 2
HALF = D // 2
SWEEPS = 2
CHUNK = 64
CHUNKS = T // CHUNK

MOD1, CONV, QO, KV, MOD2, WO, WQ = 0, 8, 16, 24, 28, 36, 40
PAIRED = (QO - CONV) // 2 + (KV - QO) // 2
PAIR_W, PAIR_M = (0, 2, 4, 7), (1, 3, 5, 6)


def weight_seq(r):
    if r < 4 * PAIRED:
        return 4 * CONV + 8 * (r // 4) + PAIR_W[r % 4]
    if r < 4 * PAIRED + 16:
        return 4 * KV + r - 4 * PAIRED
    return 4 * WO + r - 4 * PAIRED - 16


def row_seq(b, q):
    return 4 * CONV + 8 * b + PAIR_M[q] if b < PAIRED else 4 * (MOD2 + b - PAIRED) + q


KV_R, WO_R = 4 * PAIRED, 4 * PAIRED + 16
BANK_ORDER = (0, 4, 1, 2, 5, 3)


def hybrid_layer(nc, x, c, ctx_in, c_ctx, w_mod, b_mod, g_mix, g_ffn, w_in, b_gate, g_mhn, conv_w, conv_b,
                 cn_g, cn_b, w_out, w_query, keys_t, u_t, v_emb, g_final, out):
    mod_dram = nc.dram_tensor("mod_rows", [4 * D], F32)
    part_dram = nc.dram_tensor("mod_row_parts", [4, 4 * D], F32)
    q_dram = nc.dram_tensor("q", [P, 8, T], F32)
    o_dram = nc.dram_tensor("sigmoid_o", [P, 8, T], F32)
    k_dram = nc.dram_tensor("k", [P, 8, L], F32)
    v_dram = nc.dram_tensor("v", [P, 6, HEADS, HD], F32)
    gate_dram = nc.dram_tensor("gate_table", [CHUNKS, NK, NK, CHUNK], F32)
    neuron_dram = nc.dram_tensor("neurons", [NK, NK, T], F32)
    x2_dram = nc.dram_tensor("x_after_mixer", [T, D], F32)

    with ExitStack() as ctx:
        def sem(name):
            return ctx.enter_context(nc.semaphore(name))

        def region(name, words, stack=ctx):
            return stack.enter_context(nc.sbuf_tensor(name, [P, words], F32))

        ident = region("ident", P)[:, :]
        mean_w = region("mean_w", P)[:, :]
        iota = region("iota", P)[:, :]
        mask = region("mask", 2 * P)[:, :].rearrange("p (d t) -> p d t", d=2)
        stat = region("stat", 96)[:, :]
        eps_col = region("eps_col", 1)[:, :]
        one_col = region("one_col", 1)[:, :]
        keysT = region("keysT", 2 * NK)[:, :].rearrange("p (h n) -> p h n", h=2)
        den = region("den", 4)[:, :]
        soft = region("soft", 96)[:, :]
        with ExitStack() as parts:
            ring_lo = region("ring_lo", 8192, parts)[:, :].rearrange("p (q w) -> p q w", q=4)
        R0 = region("ring", 8192)[:, :]

        with ExitStack() as mixer:
            low = region("low", 28696, mixer)
            top = region("top", 12312, mixer)
            conv_col = region("conv_col", CTILES * TAPS, mixer)[:, :]
            chan_col = region("chan_col", 32, mixer)[:, :]
            c_silu = region("c_silu", 32, mixer)[:, :]
            gate_w = region("gate_w", KT * GATES, mixer)[:, :]
            gate_split = region("gate_split", 2 * KT * GATES, mixer)[:, :].rearrange("p (h w) -> p h w", h=2)
            gate_b = region("gate_b", 1, mixer)[0:GATES, :]
            c_rep = region("c_rep", KT * 32, mixer)[:, :].rearrange("p (k m) -> p k m", m=32)
            bias_rows = region("bias_rows", P, mixer)[0:64, :]
            m_rows = region("m_rows", T, mixer)[0:64, :]
            g_col = region("g_col", 6 * 64, mixer)[:, :].rearrange("p (s r) -> p s r", r=64)
            e_col = region("e_col", 4 * 64, mixer)[:, :].rearrange("p (s r) -> p s r", r=64)
        with ExitStack() as project:
            hT_hi = region("hT_hi", KT * L, project)[:, :].rearrange("p (k t) -> p k t", t=L)
            hT_lo = region("hT_lo", KT * L, project)[:, :].rearrange("p (k t) -> p k t", t=L)
            w_hi = region("w_hi", 4096, project)[:, :].rearrange("p (s w) -> p s w", s=2)
        with ExitStack() as output:
            mix_hi = region("mix_hi", 8192, output)[:, :].rearrange("p (f t) -> p f t", t=T)
            region("x2_place", 8192, output)
            wo_hi = region("wo_hi", 4096, output)[:, :].rearrange("p (s w) -> p s w", s=2)
            mix_lo = region("mix_lo", 8192, output)[:, :].rearrange("p (f t) -> p f t", t=T)
        with ExitStack() as search:
            h2_hi = region("h2_hi", 8192, search)[:, :].rearrange("p (k t) -> p k t", t=T)
            B1 = region("b1", 12288, search)[:, :]
            h2_lo = region("h2_lo", 8192, search)[:, :].rearrange("p (k t) -> p k t", t=T)
            split = region("split", 8192, search)[:, :].rearrange("p (s h w) -> p s h w", s=2, h=2)
            B4 = region("b4", 5632, search)[:, :]
            neuron_out = region("neuron_out", 2 * T, search)[:, :].rearrange("p (s t) -> p s t", s=2)
        with ExitStack() as sweep:
            x3 = region("x3", 8192, sweep)[:, :].rearrange("p (j n) -> p j n", j=LT)
            weigh = region("weigh", 8192, sweep)[:, :].rearrange("p (s w n) -> p s w n", s=4, w=2)
            a_split = region("a_split", 4096, sweep)[:, :].rearrange("p (s h w) -> p s h w", s=2, h=2)
            C3 = region("c3", 8192, sweep)[:, :]

        ring = R0.rearrange("p (q k n) -> p q k n", q=4, n=NB)
        x_slot = [top[:, i * D:(i + 1) * D] for i in range(6)]
        vec_rows = low[0:32, 0:P]
        chan_rows = low[0:32, P:2 * P]
        mix_rows = low[0:48, 2 * P:3 * P]
        conv_rows = low[0:TAPS, 1024:2048]
        square_out = low[:, 2048:4096]
        pick_col = low[:, 8448:8450]
        c_sig = low[:, 8456:8488]
        mix_col = low[:, 8488:8536]
        row_buf_a = low[:, 9216:10240].rearrange("p (b n) -> p b n", b=2)
        mod_col = soft[:, 0:64].rearrange("p (k v) -> p k v", v=2)
        xT = low[:, 12288:24576].rearrange("p (k t) -> p k t", t=L)
        UPW = ROWS * PADW
        u_pad = top[:, 0:4 * UPW].rearrange("p (c r w) -> p c r w", r=ROWS, w=PADW)
        row_buf_b = top[:, 3072:4096].rearrange("p (b n) -> p b n", b=2)
        spill = top[:, 0:3072]
        spill_o = spill[:, 0:2048].rearrange("p (m t) -> p m t", t=T)
        spill_q = top[:, 8216:10264].rearrange("p (m t) -> p m t", t=T)
        spill_k = spill.rearrange("p (m t) -> p m t", t=L)
        spill_v = spill.rearrange("p (s n) -> p s n", n=NB)
        ln_std, ln_inv = top[:, 3072:3584], top[:, 3584:4096]
        convT = top[:, 4120:8216].rearrange("p (f t) -> p f t", t=T)
        glu = top[:, 8216:12312].rearrange("p (h c t) -> p h c t", h=2, t=T)
        ln_sq = top[:, 8216:12312].rearrange("p (f t) -> p f t", t=T)
        grow = [top[0:64, 8216 + i * L:8216 + (i + 1) * L] for i in range(5)] + [top[0:64, 3072:3840]]
        gates_in = grow[4][0:GATES, :]
        g_nat, e_nat = grow[3], grow[0][:, 0:T]
        scoreT = low[:, 0:3072].rearrange("p (s t) -> p s t", t=T)
        diag_arg = low[:, 3072:4096].rearrange("p (d s t) -> p d s t", d=2, t=P)
        qT = low[:, 4096:8192].rearrange("p (f t) -> p f t", t=T)
        v_aug = low[:, 8192:14360].rearrange("p (s h e) -> p s h e", s=6, h=HEADS)
        probT = low[:, 14360:20504].rearrange("p (d s t) -> p d s t", d=2, t=T)
        pick = low[0:64, 20504:21528].rearrange("p (r m) -> p r m", m=P)
        row_buf_c = low[:, 21528:22552].rearrange("p (b n) -> p b n", b=2)
        kT = low[:, 22552:28696].rearrange("p (f t) -> p f t", t=L)
        oT = top[:, 0:4096].rearrange("p (f t) -> p f t", t=T)
        h_sum = top[:, 8216:12312].rearrange("p (j h e) -> p j h e", j=LT, h=HEADS)
        row_parts = m_rows.rearrange("p (j n) -> p j n", j=4)
        x2 = low[:, 8192:16384].rearrange("p (j n) -> p j n", j=LT)
        ga1_row, sc2_row, sh2_row = (top[:, 2048 + i * D:2048 + (i + 1) * D] for i in range(3))
        g_ffn_row = top[:, 0:2048]
        out_part = top[:, 8216:10264].rearrange("p (j n) -> p j n", j=LT)
        square2_out = top[:, 10264:10264 + T]
        h2_tile = [top[:, 8216:10264], top[:, 10264:12312]]
        query = B1[:, 8192:12288].rearrange("p (b m t) -> p b m t", b=2, m=4)
        score = B1[:, 0:8192].rearrange("p (j s n) -> p j s n", j=LT, n=NK)
        top_val = B4[:, 0:1024].rearrange("p (j s k) -> p j s k", j=LT, k=TOPK)
        top_idx = B4[:, 1024:2048].bitcast(U32).rearrange("p (j s k) -> p j s k", j=LT, k=TOPK)
        best = B4[:, 2048:2560].rearrange("p (j h k) -> p j h k", j=LT, k=TOPK)
        pos = B4[:, 2560:3072].bitcast(U32).rearrange("p (j h k) -> p j h k", j=LT, k=TOPK)
        exp1 = B4[:, 3072:3584].rearrange("p (j h k) -> p j h k", j=LT, k=TOPK)
        exp2 = B4[:, 3584:4096].rearrange("p (j h k) -> p j h k", j=LT, k=TOPK)
        gate = B4[:, 4096:4608].rearrange("p (j h k) -> p j h k", j=LT, k=TOPK)
        pos_a = B4[:, 4608:5120].bitcast(U32).rearrange("p (j h k) -> p j h k", j=LT, k=TOPK)
        pos_b = B4[:, 5120:5632].bitcast(U32).rearrange("p (j h k) -> p j h k", j=LT, k=TOPK)
        slotT = B4[:, 0:2560].rearrange("p (w t) -> p w t", t=T)

        def pair_sums(j, b):
            return B1[:, j * D + b * 4 * NK:j * D + (b + 1) * 4 * NK].rearrange("p (h a c) -> p h a c", h=2, c=TOPK)

        gate_rest, gate_round = B4[:, 2560:3072], B4[:, 4608:5120].bitcast(BF16)[:, 0:T]
        onehot = B1[:, 8192:12288].bitcast(BF16).rearrange("p (g s w n) -> p g s w n", g=4, s=4, w=4)
        stage = B1[:, 0:8192].rearrange("p (i t) -> p i t", t=CHUNK)
        square3_out = neuron_out.rearrange("p s t -> p (s t)")
        ga2_row, g_final_row = C3[:, 0:D], C3[:, D:2 * D]
        gated = C3[:, 2 * D:4 * D].rearrange("p (b n) -> p b n", n=NB)

        bank = ctx.enter_context(nc.psum_tensor("bank", [P, 8, 512], F32))

        ssq, rms, rstd = stat[:, 0:6], stat[:, 6:12], stat[:, 12:18]
        hssq, hrms, hrstd = stat[:, 18:34], stat[:, 34:50], stat[:, 50:66]
        ssq2, rms2, rstd2 = stat[:, 66:70], stat[:, 70:74], stat[:, 74:78]
        ssq3, rms3, rstd3 = stat[:, 78:82], stat[:, 82:86], stat[:, 86:90]

        consts_made = sem("consts_made")
        rows_loaded = sem("rows_loaded")
        gate_b_loaded = sem("gate_b_loaded")
        x_loaded = [sem(f"x_loaded{i}") for i in range(6)]
        quarter_full = [sem(f"quarter_full{q}") for q in range(4)]
        quarter_used = sem("quarter_used")
        setup_cols = sem("setup_cols")
        csig_made = sem("csig_made")
        dve_a = sem("dve_a")
        crep_made = sem("crep_made")
        x_squared = sem("x_squared")
        modulated1 = sem("modulated1")
        h_hi = sem("h_hi")
        h_split = sem("h_split")
        whi_made = sem("whi_made")
        first_hi = sem("first_hi")
        first_split = sem("first_split")
        wsplit_made = sem("wsplit_made")
        gate_split_made = sem("gate_split_made")
        kv_free = sem("kv_free")
        spill_stored = sem("spill_stored")
        ln_squared = sem("ln_squared")
        ln_std_made = sem("ln_std_made")
        gate_nat = sem("gate_nat")
        gate_clear = sem("gate_clear")
        gate_spread = sem("gate_spread")
        gate_turned = sem("gate_turned")
        q_loaded = [sem(f"q_loaded{h}") for h in range(HEADS)]
        k_loaded = [sem(f"k_loaded{h}") for h in range(HEADS)]
        v_loaded = [sem(f"v_loaded{h}") for h in range(HEADS)]
        o_loaded = sem("o_loaded")
        conv_hi = sem("conv_hi")
        conv_lo = sem("conv_lo")
        ht_hi = sem("ht_hi")
        ht_lo = sem("ht_lo")
        parts_loaded = sem("parts_loaded")
        rows_summed = sem("rows_summed")
        rows_stored = sem("rows_stored")
        x_rms = sem("x_rms")
        mod_bank_free = sem("mod_bank_free")
        h_made = sem("h_made")
        tr_full = sem("tr_full")
        tr_free = sem("tr_free")
        set_free = sem("set_free")
        upad_clear = sem("upad_clear")
        glu_done = sem("glu_done")
        conv_step = sem("conv_step")
        pass_full = sem("pass_full")
        ln_sub = sem("ln_sub")
        ln_rstd = sem("ln_rstd")
        ln_scaled = sem("ln_scaled")
        conv_done = sem("conv_done")
        gate_act = sem("gate_act")
        gate_dve = sem("gate_dve")
        v_ones = sem("v_ones")
        pick_made = sem("pick_made")
        m_full = sem("m_full")
        s_full = sem("s_full")
        s_copied = sem("s_copied")
        diag_made = sem("diag_made")
        w_made = sem("w_made")
        p_made = sem("p_made")
        p_back_made = sem("p_back_made")
        num_full = sem("num_full")
        num_step = sem("num_step")
        num_free = sem("num_free")
        row_copied = sem("row_copied")
        mod_summed = sem("mod_summed")
        mrow_made = sem("mrow_made")
        mrow_stored = [sem(f"mrow_stored{b}") for b in range(2)]
        h_summed = sem("h_summed")
        h_rms = sem("h_rms")
        h_normed = sem("h_normed")
        ht_full = sem("ht_full")
        ht_mixed = sem("ht_mixed")
        x2_loaded = sem("x2_loaded")
        ga1_loaded = sem("ga1_loaded")
        ffn_rows_loaded = sem("ffn_rows_loaded")
        wo_step = sem("wo_step")
        wo_free = sem("wo_free")
        x2_squared = sem("x2_squared")
        x2_rms = sem("x2_rms")
        a2_made = sem("a2_made")
        h2_step = sem("h2_step")
        h2_made = sem("h2_made")
        tr2_full = sem("tr2_full")
        tr2_hi = sem("tr2_hi")
        tr2_free = sem("tr2_free")
        x2_stored = sem("x2_stored")
        hi_made = sem("hi_made")
        split_made = sem("split_made")
        split_used = sem("split_used")
        q_copied = sem("q_copied")
        score_full = sem("score_full")
        score_copied = sem("score_copied")
        topk = sem("topk")
        soft_in = sem("soft_in")
        soft_exp = sem("soft_exp")
        slots_made = sem("slots_made")
        slotT_full = sem("slotT_full")
        slotT_made = sem("slotT_made")
        gate_parts = sem("gate_parts")
        onehot_made = sem("onehot_made")
        onehot_used = sem("onehot_used")
        gbank_free = sem("gbank_free")
        table_stored = sem("table_stored")
        gelu_made = sem("gelu_made")
        neuron_stored = [sem(f"neuron_stored{b}") for b in range(2)]
        weigh_full = [sem(f"weigh_full{b}") for b in range(4)]
        weighed = sem("weighed")
        a_hi_made = sem("a_hi_made")
        a_split_made = sem("a_split_made")
        sum_free = sem("sum_free")
        sum_full = sem("sum_full")
        merge_step = sem("merge_step")
        last_rows = sem("last_rows")
        y_step = sem("y_step")
        y_squared = sem("y_squared")
        y_rms = sem("y_rms")
        y_made = sem("y_made")
        out_stored = sem("out_stored")

        def weight_slot(r):
            return (w_hi if r < WO_R else wo_hi)[:, r % 2, :]

        def split_hi(act, r):
            seq = weight_seq(r)
            act.wait_ge(quarter_full[seq % 4], 16 * (seq // 4 + 1))
            if r >= 2:
                act.wait_ge(quarter_used, weight_seq(r - 2) + 1)
            nc.scalar.activation(weight_slot(r).bitcast(F32R), ring[:, seq % 4, :, :].rearrange("p k n -> p (k n)"),
                                 ACT.Copy).then_inc(whi_made, 1)

        def split_lo(pool, r):
            at = weight_seq(r) % 4
            pool.wait_ge(whi_made, r + 1)
            nc.gpsimd.tensor_tensor(ring_lo[:, at, :].bitcast(F32R), ring[:, at, :, :].rearrange("p k n -> p (k n)"),
                                    weight_slot(r), op=ALU.subtract).then_inc(wsplit_made, 1)

        block = ctx.enter_context(nc.Block())

        @block.sync
        def _(sp):
            def rows(w, q):
                return w[0, q * QT * P:(q + 1) * QT * P, :]

            def cols(w, q, at):
                return rows(w, q)[:, bass.ds(at, NB)].rearrange("(k p) n -> p k n", p=P)

            def load(seq, src):
                if seq >= 4:
                    sp.wait_ge(quarter_used, seq - 3)
                sp.dma_start(ring[:, seq % 4, :, :], src).then_inc(quarter_full[seq % 4], 16)

            for q in range(4):
                load(q, cols(w_mod, q, 0))
            with sp.Fori(1, 8) as b:
                for q in range(4):
                    sp.wait_ge(quarter_used, b * 4 + (q - 3))
                    sp.dma_start(ring[:, q, :, :], cols(w_mod, q, b * NB)).then_inc(quarter_full[q], 16)

            def row_load(b, q):
                load(row_seq(b, q), cols(w_mod, q, 2 * D + b * NB))

            for j, at in enumerate((CONV0, CONV0 + CW, CONV0 + NB, CONV0 + CW + NB, 0, NB, 3 * MW, 3 * MW + NB)):
                for place in range(8):
                    if place in PAIR_W:
                        q = PAIR_W.index(place)
                        load(weight_seq(4 * j + q), cols(w_in, q, at))
                    else:
                        row_load(j, PAIR_M.index(place))
            for n, at in enumerate((MW, MW + NB, 2 * MW, 2 * MW + NB)):
                for q in range(4):
                    load(weight_seq(KV_R + 4 * n + q), cols(w_in, q, at))
            for q in range(4):
                row_load(8, q)
            sp.wait_ge(quarter_used, 4 * (KV + 4))
            sp.wait_ge(spill_stored, 16 * 8)
            def qk_load(h):
                sp.dma_start(qT[:, 2 * h:2 * h + 2, :], q_dram[:, 2 * h:2 * h + 2, :]).then_inc(q_loaded[h], 16)
                sp.dma_start(kT[:, 2 * h:2 * h + 2, :], k_dram[:, 2 * h:2 * h + 2, :]).then_inc(k_loaded[h], 16)

            def v_load_head(h):
                sp.dma_start(v_aug[:, :, h, 0:HD], v_dram[:, :, h, :]).then_inc(v_loaded[h], 16)

            qk_load(0)
            for b in range(9, 16):
                for q in range(4):
                    row_load(b, q)
                if b in (9, 10, 12):
                    qk_load((9, 10, 12).index(b) + 1)
                if b in (9, 10, 12, 14):
                    v_load_head((9, 10, 12, 14).index(b))
            sp.wait_ge(gate_dve, 7)
            sp.dma_start(oT, o_dram[:, :, :]).then_inc(o_loaded, 16)
            for b in range(4):
                for q in range(4):
                    load(weight_seq(WO_R + 4 * b + q), cols(w_out, (q + 2) % 4, b * NB))
            for r in range(U0):
                b, q = r // 4, r % 4
                if b == 0:
                    load(4 * WQ + q, cols(w_query, q, 0))
                else:
                    sp.wait_ge(split_made, r - 3)
                    sp.dma_start(ring[:, q, :, :], cols(w_query, q, b * NB)).then_inc(quarter_full[q], 16)
            with sp.Fori(0, NK // 4) as i:
                for q in range(4):
                    sp.wait_ge(split_made, i * 4 + (U0 + q - 3))
                    sp.dma_start(ring[:, q, :, :].rearrange("p k n -> p (k n)"),
                                 u_t[bass.ds(i * 4 + q, 1), :, :].rearrange("a p n -> p (a n)"))\
                      .then_inc(quarter_full[q], 16)

            def v_load(count, pair, q, half):
                sp.wait_ge(split_made, count + (q - 3))
                src = v_emb[0, bass.ds(pair * (2 * P), 2 * P), half * HALF:(half + 1) * HALF]
                sp.dma_start(ring[:, q, :, :].rearrange("p k n -> p (k n)").rearrange("p (a n) -> p a n", a=2),
                             src.rearrange("(a p) n -> p a n", p=P)).then_inc(quarter_full[q], 16)

            def weigh_load(pair, q):
                sp.dma_start(weigh[:, q, 0, :].rearrange("p (a t) -> p a t", a=2),
                             neuron_dram[bass.ds(pair * 2, 2), :, :].rearrange("a p t -> p a t"))\
                  .then_inc(weigh_full[q], 16)
                sp.dma_start(weigh[:, q, 1, :].rearrange("p (c m) -> p c m", c=CHUNKS),
                             gate_dram[:, :, bass.ds(pair * 2, 2), :].rearrange("c p a t -> p c (a t)"))\
                  .then_inc(weigh_full[q], 16)

            sp.wait_ge(table_stored, 16 + 16 * CHUNKS)
            for b in range(2):
                sp.wait_ge(neuron_stored[b], 16 * (NK // 2 - 4))
            for q in range(4):
                v_load(V0, q, q, 0)
                weigh_load(q, q)
            for b in range(2):
                sp.wait_ge(neuron_stored[b], 16 * (NK // 2))
            with sp.Fori(1, PAIRS // 4) as i:
                for q in range(4):
                    v_load(i * 4 + V0, i * 4 + q, q, 0)
                    sp.wait_ge(a_split_made, i * 4 + (q - 3))
                    weigh_load(i * 4 + q, q)
            with sp.Fori(0, PAIRS // 4) as i:
                for q in range(4):
                    v_load(i * 4 + (V0 + PAIRS), i * 4 + q, q, 1)
                    sp.wait_ge(a_split_made, i * 4 + (PAIRS + q - 3))
                    weigh_load(i * 4 + q, q)
            for j in range(LT):
                sp.wait_ge(y_made, j + 1)
                sp.dma_start(out[0, j * P:(j + 1) * P, :], x3[:, j, :]).then_inc(out_stored, 16)
            sp.wait_ge(out_stored, 16 * LT)

        @block.gpsimd
        def _(pool):
            nc.gpsimd.memset(ident, 0.0).then_inc(consts_made, 1)
            nc.gpsimd.memset(mask, 0.0).then_inc(consts_made, 1)
            nc.gpsimd.memset(mean_w, 1.0 / CW).then_inc(consts_made, 1)
            nc.gpsimd.memset(eps_col, EPS)
            nc.gpsimd.memset(one_col, 1.0)
            nc.gpsimd.iota(iota, pattern=[[1, P]], base=0, channel_multiplier=0,
                           allow_small_or_imprecise_dtypes=True).then_inc(consts_made, 1)
            pool.wait_ge(consts_made, 4)
            nc.gpsimd.affine_select(out=ident, in_=ident, compare_op=ALU.not_equal, fill=1.0, base=0,
                                    pattern=[[-1, P]], channel_multiplier=1).then_inc(consts_made, 1)
            nc.gpsimd.affine_select(out=mask[:, 0, :], in_=mask[:, 0, :], compare_op=ALU.is_ge, fill=BIG, base=0,
                                    pattern=[[1, P]], channel_multiplier=-1).then_inc(consts_made, 1)
            nc.gpsimd.affine_select(out=mask[:, 1, :], in_=mask[:, 1, :], compare_op=ALU.is_ge, fill=BIG, base=0,
                                    pattern=[[-1, P]], channel_multiplier=1).then_inc(consts_made, 1)
            pool.dma_start(gate_b, b_gate[0, :].unsqueeze(1)).then_inc(gate_b_loaded, 16)

            pool.wait_ge(tr_full, 24)
            nc.gpsimd.memset(top[:, 0:4 * UPW], 0.0).then_inc(upad_clear, 1)
            for kk in range(QT):
                at = slice(kk * NB, (kk + 1) * NB)
                if kk < QT - 1:
                    pool.wait_ge(first_hi, kk + 1)
                else:
                    pool.wait_ge(whi_made, 1)
                nc.gpsimd.tensor_tensor(ring_lo[:, 0, at].bitcast(F32R), ring[:, 0, kk, :], weight_slot(0)[:, at],
                                        op=ALU.subtract).then_inc(first_split if kk < QT - 1 else wsplit_made, 1)
            for r in range(1, WO_R):
                split_lo(pool, r)
                if r in (4 * 2 + 1, 4 * 4 + 1):
                    half = (r - 9) // 8
                    pool.wait_ge(set_free, 2 + 2 * half + 2)
                    pool.wait_ge(upad_clear, 1)
                    if half:
                        pool.wait_ge(conv_step, 4 * TAPS)
                    for cc in range(4):
                        last = nc.gpsimd.tensor_tensor(
                            out=u_pad[:, cc, :, TAPS // 2:TAPS // 2 + GRID_W],
                            in0=glu[:, 0, cc, :].rearrange("p (r w) -> p r w", w=GRID_W),
                            in1=glu[:, 1, cc, :].rearrange("p (r w) -> p r w", w=GRID_W), op=ALU.mult)
                        if cc % 2:
                            last.then_inc(glu_done, 1)
            for h in range(HEADS):
                pool.wait_ge(s_copied, 6 * (h + 1))
                for s in range(6):
                    hi = T if s >= LT else (s + 1) * P
                    pool.wait_ge(w_made, 12 * h + 6 + s + 1)
                    nc.gpsimd.tensor_tensor(probT[:, 1, s, 0:hi], probT[:, 1, s, 0:hi], scoreT[:, s, 0:hi],
                                            op=ALU.mult).then_inc(p_back_made, 1)
            for f in range(8):
                pool.wait_ge(conv_hi, f + 1)
                nc.gpsimd.tensor_tensor(mix_lo[:, 8 + f, :].bitcast(F32R), convT[:, f, :], mix_hi[:, 8 + f, :],
                                        op=ALU.subtract).then_inc(conv_lo, 1)
            for j in range(LT):
                pool.wait_ge(num_full, 8 * LT)
                pool.dma_start(x2[:, j, :], x[0, j * P:(j + 1) * P, :]).then_inc(x2_loaded, 16)
            split_lo(pool, WO_R)
            split_lo(pool, WO_R + 1)
            pool.wait_ge(mrow_stored[0], 16 * 8)
            pool.wait_ge(mrow_stored[1], 16 * 8)
            pool.wait_ge(m_full, 2 * HEADS)
            pool.dma_start(row_parts, part_dram[:, :].rearrange("j (r n) -> r j n", n=P)).then_inc(parts_loaded, 16)
            split_lo(pool, WO_R + 2)
            pool.wait_ge(rows_summed, 4)
            pool.dma_start(mod_dram[:].rearrange("(r n) -> r n", n=P), bias_rows).then_inc(rows_stored, 16)
            pool.wait_ge(rows_stored, 16)
            pool.wait_ge(ht_lo, 8)
            pool.wait_ge(conv_lo, 8)
            for k, row in enumerate((ga1_row, sh2_row, sc2_row)):
                pool.dma_start(row, mod_dram[k * D:(k + 1) * D].partition_broadcast(P))\
                    .then_inc(ga1_loaded if k == 0 else ffn_rows_loaded, 16)
            pool.dma_start(g_ffn_row, g_ffn[0, :].partition_broadcast(P)).then_inc(ffn_rows_loaded, 16)
            for r in range(WO_R + 3, WO_R + 16):
                split_lo(pool, r)
            for j in range(LT):
                pool.wait_ge(wo_step, 4 * 8)
                pool.dma_start(x2_dram[j * P:(j + 1) * P, :], x2[:, j, :]).then_inc(x2_stored, 16)

            for i in range(LT):
                pool.wait_ge(h2_step, i + 1)
                nc.gpsimd.tensor_tensor(h2_tile[i % 2], h2_tile[i % 2], sh2_row, op=ALU.add).then_inc(h2_made, 1)

            with pool.Fori(0, (V0 + SWEEPS * PAIRS) // 4) as i:
                for q in range(4):
                    pool.wait_ge(hi_made, i * 4 + (q + 1))
                    nc.gpsimd.tensor_tensor(split[:, q % 2, 1, :].bitcast(F32R),
                                            ring[:, q, :, :].rearrange("p k n -> p (k n)"), split[:, q % 2, 0, :],
                                            op=ALU.subtract).then_inc(split_made, 1)

        @block.scalar
        def _(act):
            act.dma_start(vec_rows[0:16, :], c[0, :].rearrange("(k p) -> k p", p=P)).then_inc(rows_loaded, 16)
            act.dma_start(vec_rows[16:32, :], c_ctx[:].rearrange("(k p) -> k p", p=P)).then_inc(rows_loaded, 16)
            for n, src in enumerate((cn_g, cn_b, conv_b, g_mhn)):
                act.dma_start(chan_rows[8 * n:8 * n + 8, :],
                              src[0, :].rearrange("(k p) -> k p", p=P)).then_inc(rows_loaded, 16)
            act.dma_start(conv_rows, conv_w[0, :, :]).then_inc(rows_loaded, 16)
            act.dma_start(gate_w, w_in[0, :, GATE0:CONV0].rearrange("(k p) n -> p k n", p=P))\
               .then_inc(rows_loaded, 16)
            act.dma_start(bias_rows, b_mod[0, 2 * D:].rearrange("(r n) -> r n", n=P)).then_inc(rows_loaded, 16)
            act.dma_start(keysT, keys_t[:, :, :]).then_inc(rows_loaded, 16)
            act.dma_start(mix_rows[0:32, :], b_mod[0, 0:2 * D].rearrange("(r n) -> r n", n=P)).then_inc(rows_loaded, 16)
            act.dma_start(mix_rows[32:48, :], g_mix[0, :].rearrange("(r n) -> r n", n=P)).then_inc(rows_loaded, 16)

            def load_x(i):
                src = x[0, i * P:(i + 1) * P, :] if i < LT else ctx_in[0, (i - LT) * P:(i - LT + 1) * P, :]
                act.dma_start(x_slot[i], src).then_inc(x_loaded[i], 16)

            for i in range(6):
                load_x(i)
            act.sem_inc(set_free, 2)

            act.wait_ge(setup_cols, 1)
            nc.scalar.activation(c_sig, bank[:, 0, 0:32], ACT.Sigmoid).then_inc(csig_made, 1)
            act.wait_ge(consts_made, 7)

            def mean_square(i):
                act.wait_ge(x_loaded[i], 16)
                if i:
                    act.wait_ge(x_squared, i)
                nc.scalar.activation(square_out, x_slot[i], ACT.Square, accum_out=ssq[:, i:i + 1])\
                    .then_inc(x_squared, 1)
                act.wait_ge(x_squared, i + 1)
                nc.scalar.activation(rms[:, i:i + 1], ssq[:, i:i + 1], ACT.Sqrt, bias=eps_col, scale=1.0 / D)\
                    .then_inc(x_rms, 1)

            def transposed(i):
                for g in range(4):
                    act.wait_ge(tr_full, 4 * i + g + 1)
                    nc.scalar.activation(xT[:, 4 * g:4 * g + 4, i * P:(i + 1) * P],
                                         bank[:, 4 + g, :].rearrange("p (k t) -> p k t", k=4), ACT.Copy)\
                        .then_inc(tr_free, 1)

            mean_square(0)
            mean_square(1)
            for b in range(8):
                act.wait_ge(quarter_used, 4 * (b + 1))
                nc.scalar.activation(row_buf_a[:, b % 2, :], bank[:, 2 * (b % 2) + 1, :], ACT.Copy)\
                    .then_inc(row_copied, 1)
                if b < 6:
                    transposed(b)
                if b < 4:
                    mean_square(b + 2)
            for k in range(KT):
                act.wait_ge(modulated1, 2 * (k + 1))
                nc.scalar.activation(hT_hi[:, k, :].bitcast(F32R), xT[:, k, :], ACT.Copy).then_inc(h_hi, 1)
                if k == 0:
                    act.wait_ge(quarter_full[0], 16 * (CONV + 1))
                    for kk in range(QT):
                        at = slice(kk * NB, (kk + 1) * NB)
                        nc.scalar.activation(weight_slot(0)[:, at].bitcast(F32R), ring[:, 0, kk, :], ACT.Copy)\
                            .then_inc(first_hi if kk < QT - 1 else whi_made, 1)
                if k == 3:
                    split_hi(act, 1)

            def copy_row(b, n, buf):
                act.wait_ge(quarter_used, row_seq(b, 3) + 1)
                if b >= 2:
                    act.wait_ge(mrow_stored[b % 2], 16 * (b // 2))
                nc.scalar.activation(buf[:, b % 2, :], bank[:, n, :], ACT.Copy).then_inc(mrow_made, 1)
                act.wait_ge(mrow_made, b + 1)
                act.dma_start(part_dram[:, b * NB:(b + 1) * NB], buf[0:P:32, b % 2, :])\
                   .then_inc(mrow_stored[b % 2], 16)

            def spilled(e):
                if e:
                    act.wait_ge(spill_stored, 16 * e)

            def empty_set(j):
                s = 4 * (j % 2)
                src = bank[:, s:s + 4, :]
                if j < 4:
                    if j == 2:
                        act.wait_ge(glu_done, 2)
                    nc.scalar.activation(glu[:, j % 2, :, :], src, ACT.Sigmoid if j % 2 else ACT.Copy)\
                        .then_inc(set_free, 1)
                    return
                if j == 4:
                    act.wait_ge(glu_done, 4)
                if j == 6:
                    act.wait_ge(conv_step, 8 * TAPS)
                spilled(j - 4)
                buf = spill_q if j < 6 else spill_o
                if j < 6:
                    nc.scalar.activation(buf, src, ACT.Copy, scale=HD ** -0.5).then_inc(set_free, 1)
                else:
                    nc.scalar.activation(buf, src, ACT.Sigmoid).then_inc(set_free, 1)
                act.wait_ge(set_free, 2 + j + 1)
                dst = q_dram if j < 6 else o_dram
                act.dma_start(dst[:, 4 * (j % 2):4 * (j % 2) + 4, :], buf).then_inc(spill_stored, 16)

            for j in range(PAIRED):
                for q in range(4):
                    r = 4 * j + q
                    if q == 3:
                        copy_row(j, 4 - 4 * (j % 2), row_buf_b)
                        split_hi(act, r + 1)
                        act.wait_ge(quarter_used, weight_seq(r) + 1)
                        split_hi(act, r + 2)
                        empty_set(j)
                    elif q < 2:
                        act.wait_ge(quarter_used, weight_seq(r) + 1)
                        split_hi(act, r + 2)

            def empty_kv(n):
                spilled(4 + n)
                for b in BANK_ORDER:
                    if n >= 2:
                        dst, src = spill_v[:, b, :], bank[:, b, :]
                    elif b < 4:
                        dst, src = spill_k[:, b, 0:T], bank[:, b, :]
                    else:
                        m = 2 * (b - 4)
                        dst, src = spill_k[:, m:m + 2, T:L], bank[:, b, :].rearrange("p (m t) -> p m t", m=2)
                    nc.scalar.activation(dst, src, ACT.Copy).then_inc(kv_free, 1)
                act.wait_ge(kv_free, 6 * (n + 1))
                if n < 2:
                    act.dma_start(k_dram[:, 4 * n:4 * n + 4, :], spill_k).then_inc(spill_stored, 16)
                else:
                    act.dma_start(v_dram[:, :, 2 * n - 4:2 * n - 2, :].rearrange("p s h e -> p s (h e)"), spill_v)\
                       .then_inc(spill_stored, 16)

            def gate_steps(step):
                if step == 0:
                    act.wait_ge(pass_full, 3)
                    act.wait_ge(gate_b_loaded, 16)
                    act.wait_ge(ln_scaled, 8)
                    nc.scalar.activation(gates_in[:, C:L], bank[0:GATES, 6, :], ACT.Identity, bias=gate_b)\
                        .then_inc(gate_nat, 1)
                    nc.scalar.activation(gates_in[:, 0:C], bank[0:GATES, 7, 0:C], ACT.Identity, bias=gate_b)\
                        .then_inc(gate_nat, 1)
                    act.wait_ge(gate_nat, 2)
                    act.wait_ge(gate_clear, 2)
                    for g in range(4):
                        kind, d = g % 2, g // 2
                        act.dma_start(grow[2 + kind][32 * d:32 * d + 4, :], gates_in[4 * g:4 * g + 4, :])\
                           .then_inc(gate_spread, 16)
                elif step == 1:
                    act.wait_ge(gate_spread, 64)
                    for kind in range(2):
                        for d in range(2):
                            r = slice(32 * d, 32 * d + 32)
                            for at in (slice(0, C), slice(C, L)):
                                dst = grow[kind][r, at]
                                last = nc.scalar.activation(dst[:, ::-1] if d else dst, grow[2 + kind][r, at], ACT.Copy)
                    last.then_inc(gate_turned, 1)
                    act.wait_ge(gate_turned, 1)
                    nc.scalar.activation(grow[2], grow[1], ACT.Abs).then_inc(gate_act, 1)
                    act.wait_ge(gate_act, 1)
                    nc.scalar.activation(grow[3], grow[2], ACT.Exp, scale=-1.0).then_inc(gate_act, 1)
                    act.wait_ge(gate_act, 2)
                    nc.scalar.activation(grow[4], grow[3], ACT.Ln, bias=one_col[0:64, :]).then_inc(gate_act, 1)
                elif step == 2:
                    act.wait_ge(gate_dve, 5)
                    nc.scalar.activation(grow[1], grow[2], ACT.Exp, scale=-1.0).then_inc(gate_act, 1)

            for n in range(4):
                for q in range(4):
                    r = KV_R + 4 * n + q
                    act.wait_ge(quarter_used, weight_seq(r) + 1)
                    if q == 3:
                        empty_kv(n)
                    if r + 2 < WO_R:
                        split_hi(act, r + 2)
                    if n == 1 and q == 0:
                        act.wait_ge(ln_sub, 8)
                        nc.scalar.activation(ln_sq, convT, ACT.Square).then_inc(ln_squared, 1)
                    if n == 2 and q == 0:
                        act.wait_ge(pass_full, 2)
                        act.wait_ge(mrow_stored[0], 16 * 4)
                        act.wait_ge(mrow_stored[1], 16 * 4)
                        nc.scalar.activation(ln_std, bank[:, 6, :], ACT.Sqrt, bias=eps_col).then_inc(ln_std_made, 1)
                    if n == 2 and q == 2:
                        act.wait_ge(ln_scaled, 8)
                        for f in range(CTILES):
                            nc.scalar.activation(convT[:, f, :], convT[:, f, :], ACT.Silu,
                                                 bias=chan_col[:, 8 + f:9 + f], scale=chan_col[:, f:f + 1])\
                                .then_inc(conv_done, 1)
                    if n == 3 and q < 3:
                        gate_steps(q)
            act.wait_ge(pass_full, 4)
            nc.scalar.activation(g_col, bank[:, 6, 0:384].rearrange("p (s r) -> p s r", r=64), ACT.Copy)\
                .then_inc(set_free, 1)
            nc.scalar.activation(e_col, bank[:, 7, 0:256].rearrange("p (s r) -> p s r", r=64), ACT.Copy)\
                .then_inc(set_free, 1)

            for h in range(HEADS):
                for s in range(6):
                    act.wait_ge(s_full, 6 * h + s + 1)
                    if h and s == 0:
                        act.wait_ge(p_made, 6 * h)
                        act.wait_ge(p_back_made, 6 * h)
                    nc.scalar.activation(scoreT[:, s, :], bank[:, s % 2, :], ACT.Copy).then_inc(s_copied, 1)
                for d in range(2):
                    act.wait_ge(diag_made, 8 * h + 4 * (d + 1))
                    if h:
                        act.wait_ge(num_full, 8 * (h - 1) + 4 * (d + 1))
                    r = 32 * d + h
                    for s in range(6):
                        g = g_col[:, s, r:r + 1]
                        if s >= LT:
                            last = nc.scalar.activation(probT[:, d, s, :], bank[:, 2 + d, :], ACT.Exp, bias=g,
                                                        scale=-1.0)
                        else:
                            lo, hi = ((s + 1) * P, T) if d == 0 else (0, s * P)
                            if hi > lo:
                                nc.scalar.activation(probT[:, d, s, lo:hi], bank[:, 2 + d, lo:hi], ACT.Exp, bias=g,
                                                     scale=-1.0)
                            last = nc.scalar.activation(probT[:, d, s, s * P:(s + 1) * P], diag_arg[:, d, s, :],
                                                        ACT.Exp, scale=-1.0)
                        last.then_inc(w_made, 1)
                for b in (8 + 2 * h, 9 + 2 * h):
                    copy_row(b, 6 + b % 2, row_buf_c)
            act.wait_ge(conv_done, 8)
            for f in range(CTILES):
                nc.scalar.activation(mix_hi[:, 8 + f, :].bitcast(F32R), convT[:, f, :], ACT.Copy)\
                    .then_inc(conv_hi, 1)
            act.wait_ge(num_full, 8 * LT)
            split_hi(act, WO_R)
            split_hi(act, WO_R + 1)
            act.wait_ge(h_summed, 16)
            nc.scalar.activation(hrms, hssq, ACT.Sqrt, bias=eps_col, scale=1.0 / HD).then_inc(h_rms, 1)
            for f in range(8):
                act.wait_ge(ht_mixed, f + 1)
                nc.scalar.activation(mix_hi[:, f, :].bitcast(F32R), oT[:, f, :], ACT.Copy).then_inc(ht_hi, 1)

            def squares(b):
                for j in range(LT):
                    n = 4 * b + j
                    act.wait_ge(wo_step, 8 * b + 5 + j)
                    if n:
                        act.wait_ge(x2_squared, n)
                    nc.scalar.activation(square2_out, x2[:, j, b * NB:(b + 1) * NB], ACT.Square,
                                         accum_out=hssq[:, 4 * j + b:4 * j + b + 1]).then_inc(x2_squared, 1)

            for r in range(WO_R, WO_R + 16):
                act.wait_ge(quarter_used, weight_seq(r) + 1)
                if r + 2 < WO_R + 16:
                    split_hi(act, r + 2)
                if r % 4 == 1 and r > WO_R + 4:
                    squares((r - WO_R) // 4 - 1)
            squares(3)
            act.wait_ge(a2_made, 2)
            nc.scalar.activation(rms2, ssq2, ACT.Sqrt, bias=eps_col, scale=1.0 / D).then_inc(x2_rms, 1)
            def transposed2(i):
                for g in range(4):
                    act.wait_ge(tr2_full, 4 * i + g + 1)
                    nc.scalar.activation(h2_hi[:, 4 * g:4 * g + 4, i * P:(i + 1) * P].bitcast(F32R),
                                         bank[:, 4 + g, :].rearrange("p (k t) -> p k t", k=4), ACT.Copy)\
                        .then_inc(tr2_hi, 1)

            def hi(count, q):
                act.wait_ge(quarter_full[q], count)
                nc.scalar.activation(split[:, q % 2, 0, :].bitcast(F32R),
                                     ring[:, q, :, :].rearrange("p k n -> p (k n)"), ACT.Copy).then_inc(hi_made, 1)

            landed = 16 * WQ
            def copy_query(b):
                s = 4 * (b % 2)
                nc.scalar.activation(query[:, b % 2, :, :], bank[:, s:s + 4, :], ACT.Copy).then_inc(q_copied, 1)

            def copy_scores(b):
                act.wait_ge(score_full, b + 1)
                s = 4 * (b % 2)
                for m in range(4):
                    last = nc.scalar.activation(score[:, :, 4 * b + m, :],
                                                bank[:, s + m, :].rearrange("p (j n) -> p j n", j=LT), ACT.Copy)
                last.then_inc(score_copied, 1)

            for i in range(LT - 1):
                transposed2(i)
            act.wait_ge(h2_made, LT)
            hi(landed + 16, 0)
            transposed2(LT - 1)
            hi(landed + 16, 1)
            for r in range(U0):
                act.wait_ge(split_used, r + 1)
                hi(landed + 16 * ((r + 2) // 4 + 1), (r + 2) % 4)
                if r % 4 == 3:
                    if r == 3:
                        act.wait_ge(x2_stored, 16 * LT)
                        act.wait_ge(tr2_free, 16)
                    copy_query(r // 4)
                if r % 4 == 1 and r > 4:
                    copy_scores(r // 4 - 1)

            def neurons(blk, q, store=True, wait=True):
                act.wait_ge(split_used, blk * 4 + (U0 + q + 1))
                hi(blk * 16 + (landed + 16 * (U0 // 4 + (q + 2) // 4 + 1)), (q + 2) % 4)
                if store:
                    store_neurons(blk * 4 + (q - 1), (q + 1) % 2)
                if wait:
                    act.wait_ge(neuron_stored[q % 2], blk * 32 + (16 * (q // 2)))
                nc.scalar.activation(neuron_out[:, q % 2, :], bank[:, q, :], ACT.Gelu).then_inc(gelu_made, 1)

            def store_neurons(n, s):
                act.wait_ge(gelu_made, n + 1)
                act.dma_start(neuron_dram[bass.ds(n, 1), :, :].rearrange("a p t -> p (a t)"), neuron_out[:, s, :])\
                   .then_inc(neuron_stored[s], 16)

            def stage_group(g, n, at):
                act.wait_ge(onehot_used, n)
                nc.scalar.activation(stage[:, :, at:at + 4].rearrange("p i t -> p t i"),
                                     bank[:, 4 + g, :].rearrange("p (t i) -> p t i", t=4), ACT.Copy)\
                    .then_inc(gbank_free, 1)

            for q in range(4):
                neurons(0, q, q > 0, q > 1)
                if q == 1:
                    copy_scores(3)
            with act.Fori(1, 5) as i:
                for q in range(4):
                    neurons(i, q)
            act.wait_ge(soft_in, 1)
            nc.scalar.activation(gate, gate, ACT.Exp).then_inc(soft_exp, 1)
            for q in range(4):
                neurons(5, q)
            for w in range(3):
                act.wait_ge(slotT_full, w + 1)
                nc.scalar.activation(slotT[:, w, :] if w < 2 else gate_rest, bank[:, 4 + w, :], ACT.Copy)\
                    .then_inc(slotT_made, 1)
            act.sem_inc(gbank_free, 4)
            act.sem_inc(table_stored, 16)
            with act.Fori(0, CHUNKS) as chunk:
                for q in range(4):
                    neurons(chunk * 3 + 6, q)
                act.wait_ge(table_stored, chunk * 16 + 16)
                for n in range(8):
                    neurons(chunk * 3 + (7 + n // 4), n % 4)
                    for g in range(2):
                        stage_group((2 * n + g) % 4, chunk * 16 + (4 + 2 * n + g + 1), 4 * (2 * n + g))
                act.wait_ge(gbank_free, chunk * 16 + (4 + 16))
                act.dma_start(gate_dram[bass.ds(chunk, 1), :, :, :].rearrange("a p i t -> p (a i t)"),
                              stage.rearrange("p i t -> p (i t)")).then_inc(table_stored, 16)
            with act.Fori(30, 32) as i:
                for q in range(4):
                    neurons(i, q)
            store_neurons(NK - 1, 1)

            def a_hi(q, n):
                act.wait_ge(weighed, n)
                nc.scalar.activation(a_split[:, q % 2, 0, :].bitcast(F32R), weigh[:, q, 0, :], ACT.Copy)\
                    .then_inc(a_hi_made, 1)

            def v_hi(blk, q):
                hi(blk * 16 + (landed + 16 * (V0 // 4 + (q + 2) // 4 + 1)), (q + 2) % 4)

            for q in range(2):
                a_hi(q, q + 1)
            for q in range(4):
                act.wait_ge(split_used, V0 + q + 1)
                v_hi(0, q)
                a_hi((q + 2) % 4, q + 3)
                if q == 0:
                    for j in range(LT):
                        act.dma_start(x3[:, j, :], x2_dram[j * P:(j + 1) * P, :]).then_inc(last_rows, 16)
                    act.dma_start(ga2_row, mod_dram[3 * D:4 * D].partition_broadcast(P)).then_inc(last_rows, 16)
                    act.dma_start(g_final_row, g_final[:].partition_broadcast(P)).then_inc(last_rows, 16)
            with act.Fori(1, SWEEPS * PAIRS // 4 - 1) as i:
                for q in range(4):
                    act.wait_ge(split_used, i * 4 + (V0 + q + 1))
                    v_hi(i, q)
                    a_hi((q + 2) % 4, i * 4 + (q + 3))
            for j in range(LT):
                act.wait_ge(merge_step, 16)
                if j:
                    act.wait_ge(y_squared, j)
                nc.scalar.activation(square3_out, x3[:, j, 0:HALF], ACT.Square,
                                     accum_out=hssq[:, 2 * j:2 * j + 1]).then_inc(y_squared, 1)
            for q in range(2):
                n = SWEEPS * PAIRS - 4 + q
                act.wait_ge(split_used, V0 + n + 1)
                v_hi(SWEEPS * PAIRS // 4 - 1, q)
                a_hi(q + 2, n + 3)
            for n, j in enumerate((2, 3, 0, 1)):
                act.wait_ge(merge_step, 16 + 4 * (n + 1))
                act.wait_ge(y_squared, LT + n)
                nc.scalar.activation(square3_out, x3[:, j, HALF:D], ACT.Square,
                                     accum_out=hssq[:, 2 * j + 1:2 * j + 2]).then_inc(y_squared, 1)
            act.wait_ge(y_step, 1)
            nc.scalar.activation(rms3, ssq3, ACT.Sqrt, bias=eps_col, scale=1.0 / D).then_inc(y_rms, 1)

        @block.vector
        def _(dve):
            dve.sem_inc(mod_bank_free, 2)
            dve.wait_ge(setup_cols, 2)
            nc.vector.tensor_copy(chan_col, bank[:, 2, 0:32])
            nc.vector.tensor_copy(mix_col, bank[:, 3, 0:48])
            nc.vector.tensor_copy(conv_col, bank[:, 1, 0:CTILES * TAPS]).then_inc(dve_a, 1)
            dve.wait_ge(csig_made, 1)
            nc.vector.tensor_tensor(c_silu, bank[:, 0, 0:32], c_sig, ALU.mult).then_inc(dve_a, 1)
            dve.wait_ge(dve_a, 2)
            nc.vector.tensor_copy(c_rep.rearrange("p k (v r) -> p k v r", v=2),
                                  c_silu.rearrange("p (v k) -> p k v", v=2).unsqueeze(3)
                                  .to_broadcast([P, KT, 2, 16])).then_inc(crep_made, 1)
            for w in range(2):
                nc.vector.tensor_reduce(pick_col[:, w:w + 1], ident[:, 16 * w::32], AX.X, ALU.add)\
                    .then_inc(crep_made, 1)
            dve.wait_ge(rows_loaded, 16 * 12)
            nc.vector.tensor_copy(gate_split[:, 0, :].bitcast(F32R), gate_w).then_inc(gate_split_made, 1)
            dve.wait_ge(gate_split_made, 1)
            nc.vector.tensor_tensor(gate_split[:, 1, :].bitcast(F32R), gate_w, gate_split[:, 0, :], ALU.subtract)\
                .then_inc(gate_split_made, 1)
            def normalise(i):
                dve.wait_ge(x_rms, i + 1)
                nc.vector.reciprocal(rstd[:, i:i + 1], rms[:, i:i + 1]).then_inc(dve_a, 1)
                dve.wait_ge(dve_a, 3 + i)
                nc.vector.tensor_scalar(x_slot[i], x_slot[i], rstd[:, i:i + 1], None, ALU.mult).then_inc(h_made, 1)

            normalise(0)
            normalise(1)
            for b in range(8):
                dve.wait_ge(mod_summed, b + 1)
                nc.vector.tensor_tensor(mod_col[:, 4 * b:4 * b + 4, :],
                                        bank[:, 2 * (b % 2), 0:8].rearrange("p (k v) -> p k v", v=2),
                                        mix_col[:, 4 * b:4 * b + 4].unsqueeze(2).to_broadcast([P, 4, 2]), ALU.add)\
                    .then_inc(mod_bank_free, 1)
                if b < 4:
                    normalise(b + 2)
            dve.wait_ge(mod_bank_free, 2 + 8)
            nc.vector.scalar_tensor_tensor(mod_col[:, KT:2 * KT, :], mod_col[:, KT:2 * KT, :], 1.0,
                                           mix_col[:, 32:48].unsqueeze(2).to_broadcast([P, KT, 2]), ALU.add,
                                           ALU.mult).then_inc(dve_a, 1)
            dve.wait_ge(dve_a, 9)
            dve.wait_ge(tr_free, 24)

            def rest1(k):
                dve.wait_ge(h_hi, k + 1)
                nc.vector.tensor_tensor(hT_lo[:, k, :].bitcast(F32R), xT[:, k, :], hT_hi[:, k, :], ALU.subtract)\
                    .then_inc(h_split, 1)

            for k in range(KT):
                for v, at in enumerate((slice(0, T), slice(T, L))):
                    nc.vector.tensor_scalar(xT[:, k, at], xT[:, k, at], mod_col[:, KT + k, v:v + 1],
                                            mod_col[:, k, v:v + 1], ALU.mult, ALU.add).then_inc(modulated1, 1)
                if k:
                    rest1(k - 1)
            rest1(KT - 1)

            for half in range(2):
                with dve.Fori(0, 2) as i:
                    dve.wait_ge(glu_done, i + (2 * half + 1))
                    for tap in range(TAPS):
                        for cc in range(2):
                            n = 2 * tap + cc
                            y = top[:, bass.ds(i * (2 * T) + (4120 + (4 * half + cc) * T), T)]\
                                .rearrange("p (r w) -> p r w", w=GRID_W)
                            u = top[:, bass.ds(i * (2 * UPW) + cc * UPW, UPW)]\
                                .rearrange("p (r w) -> p r w", w=PADW)[:, :, tap:tap + GRID_W]
                            w = conv_col[:, bass.ds(i * (2 * TAPS) + (4 * half + cc) * TAPS + tap, 1)]
                            if tap == 0:
                                nc.vector.tensor_scalar(y, u, w, chan_col[:, bass.ds(i * 2 + 16 + 4 * half + cc, 1)],
                                                        ALU.mult, ALU.add).then_inc(conv_step, 1)
                            else:
                                dve.wait_ge(conv_step, i * (2 * TAPS) + (4 * TAPS * half + n - 1))
                                nc.vector.scalar_tensor_tensor(y, u, w, y, ALU.mult, ALU.add)\
                                    .then_inc(conv_step, 1)
            dve.wait_ge(pass_full, 1)
            for f in range(CTILES):
                nc.vector.tensor_tensor(convT[:, f, :], convT[:, f, :], bank[:, 6, :], ALU.subtract)\
                    .then_inc(ln_sub, 1)
            dve.wait_ge(ln_std_made, 1)
            nc.vector.reciprocal(ln_inv, ln_std).then_inc(ln_rstd, 1)
            dve.wait_ge(ln_rstd, 1)
            for f in range(CTILES):
                nc.vector.tensor_tensor(convT[:, f, :], convT[:, f, :], ln_inv, ALU.mult)\
                    .then_inc(ln_scaled, 1)
            for kind in range(2):
                nc.vector.memset(grow[2 + kind], 0.0).then_inc(gate_clear, 1)
            dve.wait_ge(gate_act, 3)
            nc.vector.scalar_tensor_tensor(grow[5], grow[1], 0.0, grow[4], ALU.min, ALU.subtract)\
                .then_inc(gate_dve, 1)
            dve.wait_ge(gate_dve, 1)
            nc.vector.tensor_tensor_scan(grow[3], one_col[0:64, :].to_broadcast([64, L]), grow[5], 0.0, ALU.mult,
                                         ALU.add).then_inc(gate_dve, 1)
            dve.wait_ge(gate_dve, 2)
            nc.vector.tensor_tensor(grow[4], grow[0], grow[3], ALU.subtract).then_inc(gate_dve, 1)
            dve.wait_ge(gate_dve, 3)
            nc.vector.tensor_tensor_scan(grow[5], grow[4], grow[4], 0.0, ALU.max, ALU.max).then_inc(gate_dve, 1)
            dve.wait_ge(gate_dve, 4)
            nc.vector.tensor_tensor(grow[2], grow[3], grow[5], ALU.add).then_inc(gate_dve, 1)
            dve.wait_ge(gate_act, 4)
            for d in range(2):
                r = slice(32 * d, 32 * d + 32)
                g_c, g_x = g_nat[r, 0:C], g_nat[r, C:L]
                m_x, e_x = m_rows[r, :], e_nat[r, :]
                if d:
                    g_c, g_x, m_x, e_x = g_c[:, ::-1], g_x[:, ::-1], m_x[:, ::-1], e_x[:, ::-1]
                nc.vector.tensor_copy(g_c, grow[4][r, 0:C])
                nc.vector.tensor_copy(g_x, grow[4][r, C:L])
                nc.vector.tensor_copy(m_x, grow[5][r, C:L])
                nc.vector.tensor_copy(e_x, grow[1][r, C:L]).then_inc(gate_dve, 1)

            dve.wait_ge(quarter_used, 4 * (KV + 4))
            dve.wait_ge(consts_made, 7)
            nc.vector.memset(v_aug[:, :, :, HD:HD + 1], 1.0).then_inc(v_ones, 1)
            for r in range(8):
                col = 32 * (r // HEADS) + r % HEADS
                last = nc.vector.tensor_copy(pick[:, r, :], ident[0:64, col:col + 1].to_broadcast([64, P]))
            last.then_inc(pick_made, 1)
            steps = 0
            def diagonals(h):
                for d in range(2):
                    r = 32 * d + h
                    dve.wait_ge(m_full, 2 * h + d + 1)
                    if h:
                        dve.wait_ge(w_made, 12 * h)
                    for s in range(LT):
                        nc.vector.scalar_tensor_tensor(diag_arg[:, d, s, :], bank[:, 2 + d, s * P:(s + 1) * P],
                                                       g_col[:, s, r:r + 1], mask[:, d, :], ALU.subtract, ALU.max)\
                            .then_inc(diag_made, 1)

            diagonals(0)
            for h in range(HEADS):
                dve.wait_ge(s_copied, 6 * (h + 1))
                for s in range(6):
                    lo = 0 if s >= LT else s * P
                    dve.wait_ge(w_made, 12 * h + s + 1)
                    nc.vector.tensor_tensor(probT[:, 0, s, lo:T], probT[:, 0, s, lo:T], scoreT[:, s, lo:T],
                                            ALU.mult).then_inc(p_made, 1)
                if h + 1 < HEADS:
                    diagonals(h + 1)
                for d in range(2):
                    for j in range(LT):
                        n = 8 * h + 4 * d + j
                        nb = bank[:, 4 + n % 2, :]
                        bound, inverse = den[:, n % 2:n % 2 + 1], den[:, 2 + n % 2:3 + n % 2]
                        dve.wait_ge(num_full, n + 1)
                        nc.vector.tensor_scalar(bound, nb[:, HD:HD + 1], -1.0,
                                                e_col[:, j, 32 * d + h:32 * d + h + 1], ALU.mult, ALU.max)\
                            .then_inc(num_step, 1)
                        steps += 1
                        dve.wait_ge(num_step, steps)
                        nc.vector.tensor_tensor(bound, nb[:, HD:HD + 1], bound, ALU.max).then_inc(num_step, 1)
                        steps += 1
                        dve.wait_ge(num_step, steps)
                        nc.vector.reciprocal(inverse, bound).then_inc(num_step, 1)
                        steps += 1
                        dve.wait_ge(num_step, steps)
                        hs = h_sum[:, j, h, :]
                        if d == 0:
                            nc.vector.tensor_scalar(hs, nb[:, 0:HD], inverse, None, ALU.mult).then_inc(num_free, 1)
                            continue
                        dve.wait_ge(num_free, 8 * h + j + 1)
                        nc.vector.scalar_tensor_tensor(hs, nb[:, 0:HD], inverse, hs, ALU.mult, ALU.add)\
                            .then_inc(num_free, 1)
                        dve.wait_ge(num_free, n + 1)
                        if j or h:
                            dve.wait_ge(h_summed, 4 * h + j)
                        nc.vector.tensor_tensor_reduce(out=gate_w, in0=hs, in1=hs, scale=1.0, scalar=0.0,
                                                       op0=ALU.mult, op1=ALU.add,
                                                       accum_out=hssq[:, 4 * j + h:4 * j + h + 1])\
                            .then_inc(h_summed, 1)
            dve.wait_ge(h_rms, 1)
            nc.vector.reciprocal(hrstd, hrms).then_inc(num_step, 1)
            steps += 1
            dve.wait_ge(num_step, steps)
            for h in range(HEADS):
                for j in range(LT):
                    hs = h_sum[:, j, h, :]
                    nc.vector.tensor_scalar(hs, hs, hrstd[:, 4 * j + h:4 * j + h + 1], None, ALU.mult)\
                        .then_inc(h_normed, 1)
            def mixed_rest(f):
                dve.wait_ge(ht_hi, f + 1)
                nc.vector.tensor_tensor(mix_lo[:, f, :].bitcast(F32R), oT[:, f, :], mix_hi[:, f, :], ALU.subtract)\
                    .then_inc(ht_lo, 1)

            for f in range(8):
                dve.wait_ge(ht_full, f + 1)
                if f == 0:
                    dve.wait_ge(o_loaded, 16)
                    dve.wait_ge(mrow_stored[0], 16 * 8)
                    dve.wait_ge(mrow_stored[1], 16 * 8)
                nc.vector.scalar_tensor_tensor(oT[:, f, :], bank[:, f % 4, :], chan_col[:, 24 + f:25 + f],
                                               oT[:, f, :], ALU.mult, ALU.mult).then_inc(ht_mixed, 1)
                if f:
                    mixed_rest(f - 1)
            mixed_rest(7)
            dve.wait_ge(parts_loaded, 16)
            for j in range(1, 4):
                nc.vector.tensor_tensor(row_parts[:, 0, :], row_parts[:, 0, :], row_parts[:, j, :], ALU.add)\
                    .then_inc(rows_summed, 1)
                dve.wait_ge(rows_summed, j)
            nc.vector.tensor_tensor(bias_rows, bias_rows, row_parts[:, 0, :], ALU.add).then_inc(rows_summed, 1)

            dve.sem_inc(wo_free, 2)
            dve.wait_ge(ga1_loaded, 16)
            dve.wait_ge(x2_loaded, 64)
            with dve.Fori(0, 2) as i:
                for par in range(2):
                    at = bass.ds(i * (2 * NB) + par * NB, NB)
                    dve.wait_ge(quarter_used, i * 8 + 4 * (WO + par + 1))
                    for j in range(LT):
                        ins = nc.vector.tensor_tensor(out_part[:, j, :], bank[:, 4 - 4 * par + j, :], ga1_row[:, at],
                                                      ALU.mult)
                        ins.then_inc(wo_step, 1)
                    dve.wait_ge(wo_step, i * 16 + 8 * par + 4)
                    for j in range(LT):
                        nc.vector.tensor_tensor(x2[:, j, at], x2[:, j, at], out_part[:, j, :], ALU.add)\
                            .then_inc(wo_step, 1)
                    dve.wait_ge(wo_step, i * 16 + 8 * par + 8)
                    dve.sem_inc(wo_free, 1)
            dve.wait_ge(ffn_rows_loaded, 48)
            nc.vector.scalar_tensor_tensor(sc2_row, sc2_row, 1.0, g_ffn_row, ALU.add, ALU.mult).then_inc(a2_made, 1)
            dve.wait_ge(x2_squared, 16)
            nc.vector.tensor_reduce(ssq2, hssq.rearrange("p (j b) -> p j b", b=4), AX.X, ALU.add)\
                .then_inc(a2_made, 1)
            dve.wait_ge(x2_rms, 1)
            nc.vector.reciprocal(rstd2, rms2).then_inc(a2_made, 1)
            dve.wait_ge(a2_made, 3)
            def modulated(i):
                if i >= 2:
                    dve.wait_ge(tr2_full, 4 * (i - 1))
                nc.vector.scalar_tensor_tensor(h2_tile[i % 2], x2[:, i, :], rstd2[:, i:i + 1], sc2_row, ALU.mult,
                                               ALU.mult).then_inc(h2_step, 1)

            def rest(i):
                for g in range(4):
                    dve.wait_ge(tr2_hi, 4 * i + g + 1)
                    at = (slice(None), slice(4 * g, 4 * g + 4), slice(i * P, (i + 1) * P))
                    nc.vector.tensor_tensor(h2_lo[at].bitcast(F32R), bank[:, 4 + g, :].rearrange(
                        "p (k t) -> p k t", k=4), h2_hi[at], ALU.subtract).then_inc(tr2_free, 1)

            modulated(0)
            for i in range(1, LT):
                modulated(i)
                rest(i - 1)
            rest(LT - 1)

            done = [0]

            def put(ins):
                ins.then_inc(topk, 1)
                done[0] += 1

            def top16(jobs):
                start = done[0]
                n = len(jobs)
                for k, (src, val, idx) in enumerate(jobs):
                    put(nc.vector.max(val[:, 0:8], src))
                for k, (src, val, idx) in enumerate(jobs):
                    dve.wait_ge(topk, start + k + 1)
                    put(nc.vector.max_index(idx[:, 0:8], val[:, 0:8], src))
                for k, (src, val, idx) in enumerate(jobs):
                    put(nc.vector.match_replace(src, val[:, 0:8], src, NEG))
                for k, (src, val, idx) in enumerate(jobs):
                    dve.wait_ge(topk, start + 2 * n + k + 1)
                    put(nc.vector.max(val[:, 8:16], src))
                for k, (src, val, idx) in enumerate(jobs):
                    dve.wait_ge(topk, start + 3 * n + k + 1)
                    put(nc.vector.max_index(idx[:, 8:16], val[:, 8:16], src))
                dve.wait_ge(topk, done[0])

            dve.wait_ge(tr2_full, 16)
            for b in range(4):
                dve.wait_ge(score_copied, b + 1)
                hh = slice(2 * b, 2 * b + 2)
                for j in range(LT):
                    top16([(score[:, j, 4 * b + m, :], top_val[:, j, 4 * b + m, :], top_idx[:, j, 4 * b + m, :])
                           for m in range(4)])
                for j0 in range(0, LT, 2):
                    for jj in range(2):
                        cand = pair_sums(j0 + jj, b)
                        val = top_val[:, j0 + jj, 4 * b:4 * b + 4, :].rearrange("p (h s) k -> p h s k", s=2)
                        put(nc.vector.tensor_tensor(
                            cand, val[:, :, 0, :].unsqueeze(3).to_broadcast([P, 2, TOPK, TOPK]),
                            val[:, :, 1, :].unsqueeze(2).to_broadcast([P, 2, TOPK, TOPK]), ALU.add))
                    dve.wait_ge(topk, done[0])
                    top16([(pair_sums(j0 + jj, b)[:, hl].rearrange("p a c -> p (a c)"), best[:, j0 + jj, 2 * b + hl, :],
                            pos[:, j0 + jj, 2 * b + hl, :]) for jj in range(2) for hl in range(2)])
                put(nc.vector.tensor_single_scalar(pos_a[:, :, hh, :], pos[:, :, hh, :], 4,
                                                   ALU.logical_shift_right))
                put(nc.vector.tensor_single_scalar(pos_b[:, :, hh, :], pos[:, :, hh, :], 15, ALU.bitwise_and))
                dve.wait_ge(topk, done[0])
                for j in range(LT):
                    idx = top_idx[:, j, 4 * b:4 * b + 4, :].rearrange("p (h s) k -> p h s k", s=2)
                    full = [P, 2, TOPK, TOPK]
                    match = [pair_sums(2 * (j % 2) + s, b) for s in range(2)]
                    for s, which in enumerate((pos_a, pos_b)):
                        put(nc.vector.tensor_tensor(
                            match[s], iota[:, 0:TOPK].unsqueeze(1).unsqueeze(1).to_broadcast(full),
                            which[:, j, hh, :].unsqueeze(3).to_broadcast(full), ALU.is_equal))
                    dve.wait_ge(topk, done[0])
                    for s in range(2):
                        put(nc.vector.tensor_tensor(match[s], match[s],
                                                    idx[:, :, s, :].unsqueeze(2).to_broadcast(full), ALU.mult))
                    dve.wait_ge(topk, done[0])
                    for s, dst in enumerate((exp1, exp2)):
                        put(nc.vector.tensor_reduce(dst[:, j, hh, :], match[s], AX.X, ALU.add))
                    dve.wait_ge(topk, done[0])
            dve.wait_ge(topk, done[0])
            best_g = best.rearrange("p j h k -> p (j h) k")
            gate_g = gate.rearrange("p j h k -> p (j h) k")
            nc.vector.tensor_tensor(gate_g, best_g, best_g[:, :, 0:1].to_broadcast([P, LT * PH, TOPK]),
                                    ALU.subtract).then_inc(soft_in, 1)
            dve.wait_ge(soft_exp, 1)
            put(nc.vector.tensor_reduce(soft[:, 0:32], gate_g, AX.X, ALU.add))
            dve.wait_ge(topk, done[0])
            put(nc.vector.reciprocal(soft[:, 32:64], soft[:, 0:32]))
            dve.wait_ge(topk, done[0])
            nc.vector.tensor_tensor(gate_g, gate_g, soft[:, 32:64].unsqueeze(2).to_broadcast([P, LT * PH, TOPK]),
                                    ALU.mult).then_inc(slots_made, 1)
            dve.wait_ge(slotT_made, 3)
            for part in range(3):
                nc.vector.tensor_copy(gate_round, gate_rest).then_inc(gate_parts, 1)
                dve.wait_ge(gate_parts, 3 * part + 1)
                nc.vector.tensor_copy(slotT[:, 2 + part, :], gate_round).then_inc(gate_parts, 1)
                dve.wait_ge(gate_parts, 3 * part + 2)
                nc.vector.tensor_tensor(gate_rest, gate_rest, slotT[:, 2 + part, :], ALU.subtract)\
                    .then_inc(gate_parts, 1)
                dve.wait_ge(gate_parts, 3 * part + 3)
            dve.wait_ge(score_full, 4)
            with dve.Fori(0, 32) as i:
                for g in range(4):
                    dve.wait_ge(onehot_used, i * 4 + (g + 1))
                    for s in range(4):
                        tok = bass.ds(i * 16 + 4 * g + s, 1)
                        nc.vector.tensor_scalar(onehot[:, g, s, 0, :], iota, slotT[:, 0, tok], None, ALU.is_equal)
                        for part in range(3):
                            last = nc.vector.tensor_scalar(onehot[:, g, s, 1 + part, :], iota, slotT[:, 1, tok],
                                                           slotT[:, 2 + part, tok], ALU.is_equal, ALU.mult)
                    last.then_inc(onehot_made, 1)

            def weigh_unit(q, count):
                dve.wait_ge(weigh_full[q], count)
                neurons = weigh[:, q, 0, :].rearrange("p (a c t) -> p a c t", a=2, t=CHUNK)
                gates = weigh[:, q, 1, :].rearrange("p (c a t) -> p a c t", a=2, t=CHUNK)
                nc.vector.tensor_tensor(neurons, neurons, gates, ALU.mult).then_inc(weighed, 1)

            def rest_unit(q, n):
                dve.wait_ge(a_hi_made, n)
                nc.vector.tensor_tensor(a_split[:, q % 2, 1, :].bitcast(F32R), weigh[:, q, 0, :],
                                        a_split[:, q % 2, 0, :], ALU.subtract).then_inc(a_split_made, 1)

            def merge(s):
                for k in range(8):
                    b = (k + 4) % 8
                    if k < 7:
                        dve.wait_ge(sum_full, 7 * s + k + 1)
                    else:
                        dve.wait_ge(split_used, V0 + (s + 1) * PAIRS)
                    if s:
                        dve.wait_ge(merge_step, 16)
                    nc.vector.tensor_tensor(gated[:, b, :], bank[:, b, :],
                                            ga2_row[:, s * HALF + (b % 2) * NB:s * HALF + (b % 2 + 1) * NB],
                                            ALU.mult).then_inc(sum_free, 1)
                for k in range(8):
                    b = (k + 4) % 8
                    part = x3[:, b // 2, s * HALF + (b % 2) * NB:s * HALF + (b % 2 + 1) * NB]
                    dve.wait_ge(sum_free, 8 * s + k + 1)
                    nc.vector.tensor_tensor(part, part, gated[:, b, :], ALU.add).then_inc(merge_step, 2)

            for q in range(3):
                weigh_unit(q, 32)
            with dve.Fori(0, PAIRS // 4) as i:
                for q in range(4):
                    rest_unit(q, i * 4 + (q + 1))
                    weigh_unit((q + 3) % 4, i * 32 + (32 if q == 0 else 64))
            for q in range(2):
                rest_unit(q, PAIRS + q + 1)
                weigh_unit((q + 3) % 4, PAIRS * 8 + (32 if q == 0 else 64))
            dve.wait_ge(last_rows, 16 * (LT + 2))
            merge(0)
            for q in range(2, 4):
                rest_unit(q, PAIRS + q + 1)
                weigh_unit((q + 3) % 4, PAIRS * 8 + 64)
            with dve.Fori(PAIRS // 4 + 1, SWEEPS * PAIRS // 4 - 1) as i:
                for q in range(4):
                    rest_unit(q, i * 4 + (q + 1))
                    weigh_unit((q + 3) % 4, i * 32 + (32 if q == 0 else 64))
            for q in range(4):
                rest_unit(q, SWEEPS * PAIRS - 4 + q + 1)
                if q == 0:
                    weigh_unit(3, SWEEPS * PAIRS * 8)
            merge(1)
            dve.wait_ge(y_squared, 2 * LT)
            nc.vector.tensor_reduce(ssq3, hssq[:, 0:8].rearrange("p (j s) -> p j s", s=2), AX.X, ALU.add)\
                .then_inc(y_step, 1)
            dve.wait_ge(y_rms, 1)
            nc.vector.reciprocal(rstd3, rms3).then_inc(y_step, 1)
            dve.wait_ge(y_step, 2)
            for j in range(LT):
                nc.vector.scalar_tensor_tensor(x3[:, j, :], x3[:, j, :], rstd3[:, j:j + 1], g_final_row, ALU.mult,
                                               ALU.mult).then_inc(y_made, 1)

        @block.tensor
        def _(pe):
            mm = nc.tensor.matmul
            pe.wait_ge(consts_made, 5)
            pe.wait_ge(rows_loaded, 16 * 12)
            nc.tensor.transpose(bank[:, 0, 0:32], vec_rows, ident[0:32, 0:32]).then_inc(setup_cols, 1)
            nc.tensor.transpose(bank[:, 2, 0:32], chan_rows, ident[0:32, 0:32])
            nc.tensor.transpose(bank[:, 3, 0:48], mix_rows, ident[0:48, 0:48])
            for f in range(CTILES):
                last = nc.tensor.transpose(bank[:, 1, TAPS * f:TAPS * (f + 1)], conv_rows[:, f * P:(f + 1) * P],
                                           ident[0:TAPS, 0:TAPS])
            last.then_inc(setup_cols, 1)
            pe.wait_ge(crep_made, 3)

            def mm3(out_, left, right, start, stop):
                for n, (a, b) in enumerate(((0, 0), (0, 1), (1, 0))):
                    last = mm(out_, left[a].bitcast(F32R), right[b].bitcast(F32R), start=start and n == 0,
                              stop=stop and n == 2)
                return last

            def row_quarter(n, at, q):
                for j in range(QT):
                    last = mm(bank[32 * j:32 * j + 32, n, :], c_rep[:, q * QT + j, :], ring[:, at, j, :],
                              start=q == 0, stop=q == 3, tile_position=(0, 32 * j))
                last.then_inc(quarter_used, 1)

            for b in range(8):
                par = b % 2
                for q in range(4):
                    pe.wait_ge(quarter_full[q], 16 * (b + 1))
                    row_quarter(2 * par + 1, q, q)
                pe.wait_ge(row_copied, b + 1)
                pe.wait_ge(mod_bank_free, b + 1)
                for c4 in range(4):
                    last = mm(bank[:, 2 * par, 2 * c4:2 * c4 + 2], row_buf_a[:, par, c4 * P:(c4 + 1) * P],
                              pick_col, start=True, stop=True)
                last.then_inc(mod_summed, 1)
                if b >= 6:
                    continue
                pe.wait_ge(h_made, b + 1)
                for g in range(4):
                    if b:
                        pe.wait_ge(tr_free, 4 * (b - 1) + g + 1)
                    for k in range(4):
                        kk = 4 * g + k
                        last = nc.tensor.transpose(bank[:, 4 + g, k * P:(k + 1) * P],
                                                   x_slot[b][:, kk * P:(kk + 1) * P], ident)
                    last.then_inc(tr_full, 1)
            pe.wait_ge(mod_bank_free, 2 + 8)

            def row_unit(b, q, n):
                seq = row_seq(b, q)
                pe.wait_ge(quarter_full[seq % 4], 16 * (seq // 4 + 1))
                row_quarter(n, seq % 4, q)

            def weight_parts(r, kk, at):
                cols = slice(kk * NB + at.start, kk * NB + at.stop)
                return [weight_slot(r)[:, cols], ring_lo[:, weight_seq(r) % 4, cols]]

            def h_parts(k, at):
                return [hT_hi[:, k, at], hT_lo[:, k, at]]

            for j in range(PAIRED):
                par = j % 2
                pe.wait_ge(set_free, j + 1)
                if j:
                    pe.wait_ge(mrow_made, j)
                for place in range(8):
                    if place in PAIR_M:
                        pe.wait_ge(set_free, j + 2)
                        row_unit(j, PAIR_M.index(place), 4 - 4 * par)
                        continue
                    q = PAIR_W.index(place)
                    r = 4 * j + q
                    if r:
                        pe.wait_ge(wsplit_made, r + 1)
                    for kk in range(QT):
                        k = q * QT + kk
                        if r == 0:
                            if kk < QT - 1:
                                pe.wait_ge(first_split, kk + 1)
                            else:
                                pe.wait_ge(wsplit_made, 1)
                        if j == 0:
                            pe.wait_ge(h_split, k + 1)
                        for m in range(4):
                            last = mm3(bank[:, 4 * par + m, :], weight_parts(r, kk, slice(m * P, (m + 1) * P)),
                                       h_parts(k, slice(0, T)), k == 0, k == KT - 1)
                    last.then_inc(quarter_used, 1)

            def kv_block(n):
                for q in range(4):
                    r = KV_R + 4 * n + q
                    pe.wait_ge(wsplit_made, r + 1)
                    for kk in range(QT):
                        k = q * QT + kk
                        seen = []

                        def first_use(b):
                            if k or b in seen:
                                return
                            seen.append(b)
                            if n:
                                pe.wait_ge(kv_free, 6 * (n - 1) + BANK_ORDER.index(b) + 1)
                            elif b >= 4:
                                pe.wait_ge(set_free, 2 + PAIRED)

                        if n < 2:
                            for m in range(4):
                                w = weight_parts(r, kk, slice(m * P, (m + 1) * P))
                                first_use(m)
                                mm3(bank[:, m, :], w, h_parts(k, slice(0, T)), k == 0, k == KT - 1)
                                b = 4 + m // 2
                                first_use(b)
                                last = mm3(bank[:, b, (m % 2) * C:(m % 2 + 1) * C], w, h_parts(k, slice(T, L)),
                                           k == 0 and m % 2 == 0, k == KT - 1 and m % 2 == 1)
                        else:
                            for b in BANK_ORDER:
                                first_use(b)
                                last = mm3(bank[:, b, :], h_parts(k, slice(b * P, (b + 1) * P)),
                                           weight_parts(r, kk, slice(0, NB)), k == 0, k == KT - 1)
                    last.then_inc(quarter_used, 1)

            pe.wait_ge(mrow_made, PAIRED)
            kv_block(0)
            pe.wait_ge(conv_step, 8 * TAPS)
            for f in range(CTILES):
                last = mm(bank[:, 6, :], mean_w, convT[:, f, :], start=f == 0, stop=f == CTILES - 1)
            last.then_inc(pass_full, 1)
            kv_block(1)
            pe.wait_ge(ln_squared, 1)
            for f in range(CTILES):
                last = mm(bank[:, 6, :], mean_w, ln_sq[:, f, :], start=f == 0, stop=f == CTILES - 1)
            last.then_inc(pass_full, 1)
            kv_block(2)
            pe.wait_ge(gate_split_made, 2)
            pe.wait_ge(ln_std_made, 1)
            for k in range(KT):
                w = [gate_split[:, h, k * GATES:(k + 1) * GATES] for h in range(2)]
                mm3(bank[0:GATES, 6, :], w, h_parts(k, slice(0, T)), k == 0, k == KT - 1)
                last = mm3(bank[0:GATES, 7, 0:C], w, h_parts(k, slice(T, L)), k == 0, k == KT - 1)
            last.then_inc(pass_full, 1)
            kv_block(3)
            pe.wait_ge(gate_dve, 7)
            for s in range(6):
                at = C + s * P if s < LT else (s - LT) * P
                nc.tensor.transpose(bank[:, 6, 64 * s:64 * s + 64], g_nat[:, at:at + P], ident[0:64, 0:64])
            for s in range(LT):
                last = nc.tensor.transpose(bank[:, 7, 64 * s:64 * s + 64], e_nat[:, s * P:(s + 1) * P],
                                           ident[0:64, 0:64])
            last.then_inc(pass_full, 1)
            pe.wait_ge(kv_free, 24)
            pe.wait_ge(set_free, 2 + PAIRED + 2)
            pe.wait_ge(pick_made, 1)

            def row_block(b):
                pe.wait_ge(mrow_made, b - 1)
                for q in range(4):
                    row_unit(b, q, 6 + b % 2)

            def head_scores(h):
                for d in range(2):
                    if h:
                        pe.wait_ge(w_made, 12 * h)
                    mm(bank[:, 2 + d, :], pick[:, HEADS * d + h, :], m_rows, start=True, stop=True)\
                        .then_inc(m_full, 1)
                pe.wait_ge(q_loaded[h], 16)
                pe.wait_ge(k_loaded[h], 16)
                for s in range(6):
                    n = 6 * h + s
                    if n >= 2:
                        pe.wait_ge(s_copied, n - 1)
                    for k in range(2):
                        last = mm(bank[:, s % 2, :], kT[:, 2 * h + k, s * P:(s + 1) * P], qT[:, 2 * h + k, :],
                                  start=k == 0, stop=k == 1)
                    last.then_inc(s_full, 1)

            row_block(8)
            head_scores(0)
            row_block(9)
            for h in range(HEADS):
                if h + 1 < HEADS:
                    head_scores(h + 1)
                    row_block(10 + 2 * h)
                pe.wait_ge(v_loaded[h], 16)
                pe.wait_ge(v_ones, 1)
                for d in range(2):
                    pe.wait_ge((p_made, p_back_made)[d], 6 * (h + 1))
                    for j in range(LT):
                        n = 8 * h + 4 * d + j
                        keys = [4, 5] + [s for s in range(LT) if (s <= j if d == 0 else s >= j)]
                        if n >= 2:
                            pe.wait_ge(num_free, n - 1)
                        for i, s in enumerate(keys):
                            last = mm(bank[:, 4 + n % 2, 0:HD + 1], probT[:, d, s, j * P:(j + 1) * P],
                                      v_aug[:, s, h, :], start=i == 0, stop=i == len(keys) - 1)
                        last.then_inc(num_full, 1)
                if h + 1 < HEADS:
                    row_block(11 + 2 * h)
            for f in range(8):
                h, e = f // 2, f % 2
                pe.wait_ge(h_normed, 4 * (h + 1))
                if f >= 4:
                    pe.wait_ge(ht_mixed, f - 3)
                for j in range(LT):
                    last = nc.tensor.transpose(bank[:, f % 4, j * P:(j + 1) * P], h_sum[:, j, h, e * P:(e + 1) * P],
                                               ident)
                last.then_inc(ht_full, 1)

            pe.wait_ge(conv_lo, 8)
            pe.wait_ge(num_free, 32)
            pe.wait_ge(mrow_made, 16)
            for b in range(4):
                pe.wait_ge(wo_free, b + 1)
                for q in range(4):
                    r = WO_R + 4 * b + q
                    pe.wait_ge(wsplit_made, r + 1)
                    if b == 0 and q >= 2:
                        pe.wait_ge(ht_lo, 4 * (q - 1))
                    if b == 1 and q == 0:
                        pe.wait_ge(ht_mixed, 8)
                    for kk in range(QT):
                        k = (q + 2) % 4 * QT + kk
                        for j in range(LT):
                            at = slice(j * P, (j + 1) * P)
                            last = mm3(bank[:, 4 - 4 * (b % 2) + j, :], [mix_hi[:, k, at], mix_lo[:, k, at]],
                                       weight_parts(r, kk, slice(0, NB)), q == 0 and kk == 0, q == 3 and kk == 3)
                    last.then_inc(quarter_used, 1)
            pe.wait_ge(wo_free, 6)
            for i in range(LT):
                pe.wait_ge(h2_made, i + 1)
                for g in range(4):
                    if i:
                        pe.wait_ge(tr2_free, 4 * (i - 1) + g + 1)
                    for k in range(4):
                        kk = 4 * g + k
                        last = nc.tensor.transpose(bank[:, 4 + g, k * P:(k + 1) * P],
                                                   h2_tile[i % 2][:, kk * P:(kk + 1) * P], ident)
                    last.then_inc(tr2_full, 1)
            pe.wait_ge(tr2_free, 16)

            def query_unit(r):
                b, q = r // 4, r % 4
                pe.wait_ge(split_made, r + 1)
                for kk in range(QT):
                    k = q * QT + kk
                    for m in range(4):
                        at = slice(kk * NB + m * P, kk * NB + (m + 1) * P)
                        last = mm3(bank[:, 4 * (b % 2) + m, :], [split[:, r % 2, h, at] for h in range(2)],
                                   [h2_hi[:, k, :], h2_lo[:, k, :]], k == 0, k == KT - 1)
                last.then_inc(split_used, 1)

            def scores(b):
                pe.wait_ge(q_copied, b + 1)
                for m in range(4):
                    for j in range(LT):
                        last = mm(bank[:, 4 * (b % 2) + m, j * P:(j + 1) * P],
                                  query[:, b % 2, m, j * P:(j + 1) * P], keysT[:, m % 2, :], start=True, stop=True)
                last.then_inc(score_full, 1)

            for r in range(U0):
                if r % 4 == 0 and r >= 8:
                    pe.wait_ge(score_copied, r // 4 - 1)
                query_unit(r)
                if r % 4 == 1 and r >= 4:
                    scores(r // 4 - 1)

            def neurons(blk, q, wait=True):
                pe.wait_ge(split_made, blk * 4 + (U0 + q + 1))
                if wait:
                    pe.wait_ge(gelu_made, blk * 4 + (q - 3))
                for k in range(KT):
                    last = mm3(bank[:, q, :], [split[:, q % 2, h, k * P:(k + 1) * P] for h in range(2)],
                               [h2_hi[:, k, :], h2_lo[:, k, :]], k == 0, k == KT - 1)
                last.then_inc(split_used, 1)

            pe.wait_ge(score_copied, 3)
            for q in range(4):
                neurons(0, q, False)
                if q == 0:
                    scores(3)
            with pe.Fori(1, 6) as i:
                for q in range(4):
                    neurons(i, q)
            pe.wait_ge(slots_made, 1)
            pe.wait_ge(score_copied, 4)
            for w, src in enumerate((exp1, exp2, gate)):
                for j in range(LT):
                    last = nc.tensor.transpose(bank[:, 4 + w, j * P:(j + 1) * P],
                                               src[:, j, :, :].rearrange("p h k -> p (h k)"), ident)
                last.then_inc(slotT_full, 1)
            pe.sem_inc(onehot_used, 4)
            with pe.Fori(0, CHUNKS) as chunk:
                for q in range(4):
                    neurons(chunk * 3 + 6, q)
                for n in range(8):
                    neurons(chunk * 3 + (7 + n // 4), n % 4)
                    for g in range(2 * n, 2 * n + 2):
                        pe.wait_ge(onehot_made, chunk * 16 + (g + 1))
                        pe.wait_ge(gbank_free, chunk * 16 + (g + 1))
                        for s in range(4):
                            for part in range(3):
                                last = mm(bank[:, 4 + g % 4, s * NK:(s + 1) * NK], onehot[:, g % 4, s, 1 + part, :],
                                          onehot[:, g % 4, s, 0, :], start=part == 0, stop=part == 2)
                        last.then_inc(onehot_used, 1)
            with pe.Fori(30, 32) as i:
                for q in range(4):
                    neurons(i, q)

            def sums(count, q, first=None, stop=False):
                pe.wait_ge(split_made, count + (V0 + q + 1))
                pe.wait_ge(a_split_made, count + (q + 1))
                edge = first is not None or stop
                order = [(a, k) for k in range(8) for a in range(2)] if edge else \
                    [(a, k) for a in range(2) for k in range(8)]
                for a, k in order:
                    b = (k + 4) % 8
                    if first == 0 and a == 0:
                        if b == 4:
                            pe.wait_ge(gbank_free, 4 + 128)
                        if b < 4:
                            pe.wait_ge(gelu_made, NK - 3 + b)
                    if first == 1 and a == 0:
                        pe.wait_ge(sum_free, k + 1)
                    j, n = b // 2, b % 2
                    last = mm3(bank[:, b, :],
                               [a_split[:, q % 2, h, a * T + j * P:a * T + (j + 1) * P] for h in range(2)],
                               [split[:, q % 2, h, a * HALF + n * NB:a * HALF + (n + 1) * NB] for h in range(2)],
                               first is not None and a == 0, stop and a == 1)
                    if stop and a == 1 and k < 7:
                        last.then_inc(sum_full, 1)
                last.then_inc(split_used, 1)

            for s in range(SWEEPS):
                for q in range(4):
                    sums(s * PAIRS, q, s if q == 0 else None)
                with pe.Fori(1, PAIRS // 4 - 1) as i:
                    for q in range(4):
                        sums(i * 4 + s * PAIRS, q)
                for q in range(4):
                    sums((s + 1) * PAIRS - 4, q, None, q == 3)


_INS = ['x', 'c', 'ctx', 'c_ctx', 'w_mod', 'b_mod', 'g_mix', 'g_ffn', 'w_in', 'b_gate', 'g_mhn', 'conv_w', 'conv_b',
        'cn_g', 'cn_b', 'w_out', 'w_query', 'sub_keys', 'u_emb', 'v_emb', 'g_final']


def kernel(**inputs):
    import numpy as _np
    import concourse.bacc as _bacc
    from concourse import mybir as _mybir
    from concourse.bass_utils import run_bass_kernel_spmd as _run

    laid = {name: _np.asarray(inputs[name]) for name in _INS}
    laid['sub_keys'] = laid['sub_keys'][0].transpose(2, 0, 1)
    laid['u_emb'] = laid['u_emb'][0].reshape(NK, NK, KT, P).transpose(0, 3, 2, 1).reshape(NK, P, KT * NK)

    nc = _bacc.Bacc("TRN2", target_bir_lowering=False, num_devices=1)
    arrays, args = {}, []
    for name in _INS:
        a = _np.ascontiguousarray(laid[name])
        arrays[f"in_{name}"] = a
        args.append(nc.dram_tensor(f"in_{name}", a.shape, _mybir.dt.from_np(a.dtype), kind="ExternalInput").ap())
    args.append(nc.dram_tensor("out", (1, T, D), _mybir.dt.float32, kind="ExternalOutput").ap())
    hybrid_layer(nc, *args)
    r = _run(nc, [arrays], core_ids=[0])
    return r.results[0]["out"]
```
